# Optimizing a Trainium2 kernel written in Bass

```python
import jax, jax.numpy as jnp
from jax import lax
import numpy as np

D_MODEL = 1024
BATCH = 1
SEQ = 256
DEPTH = 2

N_MIXERS = 2
N_ATTN_LAYERS = (DEPTH + 1) // 2
N_HGRN_LAYERS = DEPTH // 2
DILATED_GROUPS = ((128, 1), (512, 4), (2048, 16))
N_GROUPS = len(DILATED_GROUPS)
ATTN_HEADS = 8
ATTN_HEAD_DIM = D_MODEL // ATTN_HEADS
ATTN_WIDTH = ATTN_HEADS * ATTN_HEAD_DIM
NUM_BUCKETS = 32
MAX_DISTANCE = 2048
HGRN_HEADS = 8
HGRN_KDIM = 128
HGRN_VDIM = D_MODEL // HGRN_HEADS
HGRN_FWD = HGRN_HEADS * HGRN_KDIM
HGRN_CHUNK = 64
FFN_HIDDEN = ((8 * D_MODEL // 3 + 255) // 256) * 256
RMS_EPS = 1e-6

kernel_name = "hybrid_dilated_attn_hgrn2_swiglu_adaln"

def rms_norm(x, gain, eps=RMS_EPS):
    xf = x.astype(jnp.float32)
    y = xf * lax.rsqrt(jnp.mean(xf * xf, axis=-1, keepdims=True) + eps)
    return (y * gain.astype(jnp.float32)).astype(x.dtype)

def t5_bucket(dist):
    n = np.asarray(dist, dtype=np.int64)
    max_exact = NUM_BUCKETS // 2
    large = max_exact + (np.log(np.maximum(n, 1) / max_exact)
                         / np.log(MAX_DISTANCE / max_exact)
                         * (NUM_BUCKETS - max_exact)).astype(np.int64)
    large = np.minimum(large, NUM_BUCKETS - 1)
    return np.where(n < max_exact, n, large).astype(np.int32)

def dilated_window_group(q, k, v, bias_j, window, dilation):
    B, S, H, Dh = q.shape
    d = dilation
    blk = window // dilation
    span = d * blk
    s_pad = -(-S // span) * span
    pad = s_pad - S
    if pad:
        padw = ((0, 0), (0, pad), (0, 0), (0, 0))
        q, k, v = jnp.pad(q, padw), jnp.pad(k, padw), jnp.pad(v, padw)
    L = s_pad // d
    nb = L // blk

    def to_sub(t):
        X = t.shape[-1]
        return t.reshape(B, L, d, H, X).transpose(0, 2, 1, 3, 4).reshape(B, d, nb, blk, H, X)

    def from_sub(t):
        X = t.shape[-1]
        return t.reshape(B, d, L, H, X).transpose(0, 2, 1, 3, 4).reshape(B, s_pad, H, X)[:, :S]

    qb, kb, vb = to_sub(q), to_sub(k), to_sub(v)
    def with_prev(t):
        prev = jnp.concatenate([jnp.zeros_like(t[:, :, :1]), t[:, :, :-1]], axis=2)
        return jnp.concatenate([prev, t], axis=3)
    kk, vv = with_prev(kb), with_prev(vb)

    qi = np.arange(blk)[:, None]
    ki = np.arange(2 * blk)[None, :]
    j = blk + qi - ki
    band = (j >= 0) & (j <= blk)
    mask = np.broadcast_to(band, (nb, blk, 2 * blk)).copy()
    mask[0, :, :blk] = False
    mask = jnp.asarray(mask.reshape(1, 1, nb, blk, 1, 2 * blk))
    bias = bias_j[np.clip(j, 0, blk)].transpose(0, 2, 1)

    s = jnp.einsum('brnqhd,brnkhd->brnqhk', qb, kk) * (Dh ** -0.5) + bias
    s = jnp.where(mask, s, -jnp.inf)
    m = jnp.max(s, axis=-1, keepdims=True)
    p = jnp.exp(s - m)
    l = jnp.sum(p, axis=-1, keepdims=True)
    o = jnp.einsum('brnqhk,brnkhd->brnqhd', p, vv) / l
    return from_sub(o), from_sub(m), from_sub(l)

def dilated_attention(h, w_qkv, w_out, q_gain, k_gain, rel_bias):
    B, S, _ = h.shape
    qkv = (h @ w_qkv).astype(jnp.float32).reshape(B, S, N_GROUPS, 3, ATTN_HEADS, ATTN_HEAD_DIM)
    outs, maxes, dens = [], [], []
    for g, (window, dil) in enumerate(DILATED_GROUPS):
        q = rms_norm(qkv[:, :, g, 0], q_gain[g])
        k = rms_norm(qkv[:, :, g, 1], k_gain[g])
        v = qkv[:, :, g, 2]
        steps = window // dil
        bucket = t5_bucket(np.arange(steps + 1) * dil)
        bias_j = rel_bias[bucket, g * ATTN_HEADS:(g + 1) * ATTN_HEADS].astype(jnp.float32)
        o, m, l = dilated_window_group(q, k, v, bias_j, window, dil)
        outs.append(o); maxes.append(m); dens.append(l)
    o = jnp.stack(outs)
    m = jnp.stack(maxes)
    l = jnp.stack(dens)
    wts = l * jnp.exp(m - jnp.max(m, axis=0, keepdims=True))
    out = jnp.sum(wts * o, axis=0) / jnp.sum(wts, axis=0)
    return out.reshape(B, S, ATTN_WIDTH).astype(h.dtype) @ w_out

def hgrn2_mixer(h, w_in, w_out, gnorm_gain, lower_bound):
    B, S, _ = h.shape
    proj = h @ w_in
    q, f, i, g = jnp.split(proj, [HGRN_FWD, 2 * HGRN_FWD, 2 * HGRN_FWD + D_MODEL], axis=-1)
    q = jax.nn.silu(q.astype(jnp.float32))
    lb = lower_bound.astype(jnp.float32)
    fg = lb + (1.0 - lb) * jax.nn.sigmoid(f.astype(jnp.float32))
    logf = jnp.log(fg)
    kin = 1.0 - fg
    nc = S // HGRN_CHUNK

    def chunk(t, dim):
        t = t.reshape(B, S, HGRN_HEADS, dim).transpose(0, 2, 1, 3)
        return jnp.moveaxis(t.reshape(B, HGRN_HEADS, nc, HGRN_CHUNK, dim), 2, 0)

    qc, kc, gc = chunk(q, HGRN_KDIM), chunk(kin, HGRN_KDIM), chunk(logf, HGRN_KDIM)
    vc = chunk(i.astype(jnp.float32), HGRN_VDIM)
    tri = jnp.asarray(np.tril(np.ones((HGRN_CHUNK, HGRN_CHUNK), dtype=bool))[None, None, :, :, None])

    def step(state, xs):
        qq, kq, vq, gq = xs
        G = jnp.cumsum(gq, axis=2)
        diff = G[:, :, :, None, :] - G[:, :, None, :, :]
        decay = jnp.exp(jnp.where(tri, diff, -jnp.inf))
        A = jnp.einsum('bhtk,bhsk,bhtsk->bhts', qq, kq, decay)
        o = jnp.einsum('bhts,bhsv->bhtv', A, vq) + jnp.einsum('bhtk,bhkv->bhtv', qq * jnp.exp(G), state)
        G_last = G[:, :, -1:, :]
        new_state = (jnp.exp(G_last[:, :, 0, :])[..., None] * state
                     + jnp.einsum('bhsk,bhsv->bhkv', kq * jnp.exp(G_last - G), vq))
        return new_state, o

    state0 = jnp.zeros((B, HGRN_HEADS, HGRN_KDIM, HGRN_VDIM), jnp.float32)
    _, o = lax.scan(step, state0, (qc, kc, vc, gc))
    o = jnp.moveaxis(o, 0, 2).reshape(B, HGRN_HEADS, S, HGRN_VDIM).transpose(0, 2, 1, 3)
    o = rms_norm(o, gnorm_gain).reshape(B, S, D_MODEL)
    o = o * jax.nn.silu(g.astype(jnp.float32))
    return o.astype(h.dtype) @ w_out

def swiglu(h, w1, w3, w2):
    return (jax.nn.silu(h @ w1) * (h @ w3)) @ w2

def setup_inputs(seed: int = 0) -> dict:
    key = jax.random.key(seed)
    ks = jax.random.split(key, 20)
    f32 = jnp.float32
    def nrm(k, shape, fan_in, mult=1.0):
        return jax.random.normal(k, shape, f32) * (mult * fan_in ** -0.5)
    def gain(k, shape):
        return 1.0 + 0.05 * jax.random.normal(k, shape, f32)
    return {
        "x": jax.random.normal(ks[0], (BATCH, SEQ, D_MODEL), f32),
        "c": jax.random.normal(ks[1], (BATCH, D_MODEL), f32),
        "rel_bias": 0.5 * jax.random.normal(ks[2], (NUM_BUCKETS, N_GROUPS * ATTN_HEADS), f32),
        "ada_w": nrm(ks[3], (DEPTH, D_MODEL, 6 * D_MODEL), D_MODEL, 0.5),
        "ada_b": 0.02 * jax.random.normal(ks[4], (DEPTH, 6 * D_MODEL), f32),
        "norm_mix": gain(ks[5], (DEPTH, D_MODEL)),
        "norm_ffn": gain(ks[6], (DEPTH, D_MODEL)),
        "attn_w_qkv": nrm(ks[7], (N_ATTN_LAYERS, D_MODEL, N_GROUPS * 3 * ATTN_WIDTH), D_MODEL),
        "attn_w_out": nrm(ks[8], (N_ATTN_LAYERS, ATTN_WIDTH, D_MODEL), ATTN_WIDTH),
        "attn_q_gain": gain(ks[9], (N_ATTN_LAYERS, N_GROUPS, ATTN_HEAD_DIM)),
        "attn_k_gain": gain(ks[10], (N_ATTN_LAYERS, N_GROUPS, ATTN_HEAD_DIM)),
        "hgrn_w_in": nrm(ks[11], (N_HGRN_LAYERS, D_MODEL, 2 * HGRN_FWD + 2 * D_MODEL), D_MODEL),
        "hgrn_w_out": nrm(ks[12], (N_HGRN_LAYERS, D_MODEL, D_MODEL), D_MODEL),
        "hgrn_gnorm": gain(ks[13], (N_HGRN_LAYERS, HGRN_VDIM)),
        "hgrn_lower_bounds": jax.random.normal(ks[14], (DEPTH, HGRN_FWD), f32),
        "ffn_w1": nrm(ks[15], (DEPTH, D_MODEL, FFN_HIDDEN), D_MODEL),
        "ffn_w3": nrm(ks[16], (DEPTH, D_MODEL, FFN_HIDDEN), D_MODEL),
        "ffn_w2": nrm(ks[17], (DEPTH, FFN_HIDDEN, D_MODEL), FFN_HIDDEN),
    }

def reference(x, c, rel_bias, ada_w, ada_b, norm_mix, norm_ffn, attn_w_qkv, attn_w_out,
              attn_q_gain, attn_k_gain, hgrn_w_in, hgrn_w_out, hgrn_gnorm, hgrn_lower_bounds,
              ffn_w1, ffn_w3, ffn_w2):
    p = jax.nn.softmax(hgrn_lower_bounds.astype(jnp.float32), axis=0)
    lbs = jnp.cumsum(p, axis=0) - p[0]
    c_act = jax.nn.silu(c)
    for i in range(DEPTH):
        mod = c_act @ ada_w[i] + ada_b[i]
        sh1, sc1, g1, sh2, sc2, g2 = jnp.split(mod[:, None, :], 6, axis=-1)
        h = rms_norm(x, norm_mix[i]) * (1.0 + sc1) + sh1
        a = i // N_MIXERS
        if i % N_MIXERS == 0:
            y = dilated_attention(h, attn_w_qkv[a], attn_w_out[a], attn_q_gain[a],
                                  attn_k_gain[a], rel_bias)
        else:
            y = hgrn2_mixer(h, hgrn_w_in[a], hgrn_w_out[a], hgrn_gnorm[a], lbs[i])
        x = x + g1 * y
        h = rms_norm(x, norm_ffn[i]) * (1.0 + sc2) + sh2
        x = x + g2 * swiglu(h, ffn_w1[i], ffn_w3[i], ffn_w2[i])
    return x


_drawn_inputs = setup_inputs


def setup_inputs(seed=0):
    import zlib

    import numpy as np

    out = dict(_drawn_inputs(seed))
    spreads = {}
    factors = {'norm_mix': 4.039,
     'attn_q_gain': 8.0,
     'attn_k_gain': 8.0,
     'hgrn_gnorm': 5.375,
     'hgrn_lower_bounds': 3.429,
     'norm_ffn': 3.932}
    for name, (base, spread) in spreads.items():
        noise = np.random.default_rng([zlib.crc32(name.encode()), seed]).standard_normal(out[name].shape)
        drawn = base * np.exp(spread * noise) if base else spread * noise
        out[name] = __import__('jax').numpy.asarray(drawn.astype(out[name].dtype))
    for name, factor in factors.items():
        out[name] = (out[name] * factor).astype(out[name].dtype)
    return out
```

```python
from contextlib import ExitStack

import numpy as np
import concourse.bass as bass
from concourse import mybir

ALU = mybir.AluOpType
ACT = mybir.ActivationFunctionType
AX_X = mybir.AxisListType.X
F32 = mybir.dt.float32
F32R = mybir.dt.float32r
I32 = mybir.dt.int32

P = 128
SEQ = 256
D = 1024
KC = D // P
T = SEQ // P
HEADS = 8
GROUPS = ((128, 1), (512, 4), (2048, 16))
NG = len(GROUPS)
BUCKETS = 32
MAX_DISTANCE = 2048
F = ((8 * D // 3 + 255) // 256) * 256
FC = 256
NF = F // FC
EPS = 1e-6
MASKED = -1e30
UNIT = 2048
RAW = 3
SPL = 3
AHEAD = 2
PAIRS = HEADS // 2
QU = 9
ADA_COLS = D
FIRST = 8
ADA_RING = 2
ADA_BLOCKS = 6 * D // ADA_COLS
LEVELS = 8

M_OUT0 = PAIRS * QU
M_FFN0 = M_OUT0 + 4
M_IN = M_FFN0 + 3 * NF
M_OUT1 = M_IN + 16
M_FFN1 = M_OUT1 + 4
UNITS = M_FFN1 + 3 * NF


def distance_table():
    table = np.zeros((NG * BUCKETS + NG, 2 * P + P - 1), np.float32)
    exact = BUCKETS // 2
    for g, (window, dil) in enumerate(GROUPS):
        for i in range(table.shape[1]):
            dist = 2 * P - 1 - i
            if dist < 0 or dist > window or dist % dil:
                table[NG * BUCKETS + g, i] = 1.0
                continue
            large = exact + int(np.log(max(dist, 1) / exact) / np.log(MAX_DISTANCE / exact) * (BUCKETS - exact))
            table[g * BUCKETS + (dist if dist < exact else min(large, BUCKETS - 1)), i] = 1.0
    return table


def mask_rows():
    rows = np.zeros((NG, NG * HEADS), np.float32)
    for g in range(NG):
        rows[g, g * HEADS:(g + 1) * HEADS] = MASKED
    return rows


def tree_masks():
    s, t = np.meshgrid(np.arange(P), np.arange(P), indexing="ij")
    masks = np.zeros((P, LEVELS, P), np.int32)
    masks[:, 0] = s == t
    for level in range(1, LEVELS):
        h = 1 << (level - 1)
        masks[:, level] = (s // (2 * h) == t // (2 * h)) & (s % (2 * h) < h) & (t % (2 * h) >= h)
    return masks


def hybrid_trunk(nc, a, out):
    TABLE = 2 * P + P - 1
    GH = NG * HEADS
    with ExitStack() as ctx:
        def sb(name, shape, dt=F32):
            return ctx.enter_context(nc.sbuf_tensor(name, shape, dt))

        def sem(name):
            return ctx.enter_context(nc.semaphore(name))

        bank = [ctx.enter_context(nc.psum_tensor(f"bank{i}", [P, 512], F32)) for i in range(8)]

        raw = sb("raw", [P, RAW, UNIT])
        whi = sb("whi", [P, SPL, UNIT], F32R)
        wlo = sb("wlo", [P, SPL, UNIT], F32R)
        ada_w = sb("ada_w", [P, ADA_RING, ADA_COLS])
        acc = sb("acc", [P, 2, ADA_COLS])
        x = sb("x", [P, T, D])
        hT_hi = sb("hT_hi", [P, KC, SEQ], F32R)
        hT_lo = sb("hT_lo", [P, KC, SEQ], F32R)
        oT_hi = sb("oT_hi", [P, KC, SEQ], F32R)
        oT_lo = sb("oT_lo", [P, KC, SEQ], F32R)
        gate = sb("gate", [P, 2, D])
        ident = sb("ident", [P, P])
        ones = sb("ones", [P, P])
        rows = sb("rows", [64, P])
        cols = sb("cols", [P, 64])
        cact = sb("cact", [P, KC])
        mod_a = sb("mod_a", [P, 2, 2, KC])
        mod_b = sb("mod_b", [P, 2, 2, KC])
        lb = sb("lb", [P, 2, KC])
        lbd = sb("lbd", [P, KC])
        small = sb("small", [P, 64])
        eps = sb("eps", [P, 1])
        late_gate = sb("late_gate", [P, D])
        arena = sb("arena", [P, 14336])

        def part(at, shape):
            v = arena[:, at:at + int(np.prod(shape))]
            if len(shape) > 1:
                names = "abcd"[:len(shape)]
                v = v.rearrange(f"p ({' '.join(names)}) -> p {' '.join(names)}",
                                **{k: n for k, n in zip(names, shape)})
            return v

        hT = part(0, [KC, SEQ])
        xn = part(3072, [T, D])
        first_w = [part(at, [ADA_COLS]) for at in (0, 1024, 2048, 5120, 6144, 7168, 8192, 11264)]
        qT = part(0, [2, NG, 2 * SEQ])
        kT = part(3072, [2, NG, 2 * SEQ])
        vN = part(6144, [2, T, NG * 2 * P])
        qkn = part(9216, [2, T * 512])
        prob = part(11264, [768])
        probT = part(12032, [768])
        bias = part(12800, [2, NG, SEQ])
        rel3 = qkn[0:NG * BUCKETS + NG, 0, 0:GH]
        tabw = qkn[0:NG * BUCKETS + NG, 0, 64:64 + TABLE]
        tabT = qkn[0:GH, 0, 512:512 + TABLE]
        sil = part(6144, [T, FC])
        hid = part(6656, [T, FC])
        rq = part(0, [1024])
        rk = part(1024, [1024])
        rG = part(2048, [1024])
        gates = xn
        nat = part(5120, [T, 512])
        rE = part(6144, [2, 1024])
        rZ = part(8192, [2, 1024])
        rV = part(10240, [T, 1024])
        Am = part(12288, [3, 512])
        sq = sb("sq", [P, T, 512])
        masks = sb("masks", [P, LEVELS, P], I32)

        def hidT(v, n):
            return v[:, 2 * (n % 2):2 * (n % 2) + 2, :]

        scratch = nc.dram_tensor("bias_rows", (GH, TABLE), F32, kind="Internal").ap()

        raw_in = [sem(f"raw_in{i}") for i in range(RAW)]
        ada_in = [sem(f"ada_in{i}") for i in range(ADA_RING)]
        first_in = [sem(f"first_in{i}") for i in range(FIRST)]
        bias_in = [sem(f"bias_in{i}") for i in range(2)]
        names = """x_in rows_in masks_in rel_in tab_out out_done
            rounded split pe_unit
            pool_setup pool_chain
            cols_t cols_s cact_s lbd_s lb_s
            ada_used ada_red ada_ev adab_in0 adab_in1 ada_zero
            tab_mm tab_cp
            xn_ssq xn_ln xn_rstd xn_s xn_tr xn_aff xn_hi xn_lo res
            qk_sq qk_red qk_ln qk_rstd qk_norm qk_tr qk_tev v_ev
            att_s att_m att_nm att_p att_rs att_pn att_tr pt_ev att_pv ot_hi ot_ev
            f_sil f_hid f_tr f_hi f_lo
            yres_t
            r_nat r_tr r_tev r_fg r_k r_ln r_G r_D r_E r_q r_mm r_A r_zero r_o r_oev r_osq r_ored r_oln r_orstd
            r_sg r_on r_otr r_ohi r_olo r_gn""".split()
        s = {n: sem(n) for n in names}

        block = ctx.enter_context(nc.Block())

        def cols_of(w, c0, n, k0, nk):
            return w.rearrange("(k p) n -> p k n", p=P)[:, k0:k0 + nk, c0:c0 + n]

        def pieces(m):
            if m < M_OUT0:
                pr, j = divmod(m, QU)
                w = a["attn_w_qkv"][0]
                col = lambda g, which: (3 * g + which) * D + pr * 256
                if j == 8:
                    return [(cols_of(w, col(2, 2), 256, 0, 8), 8, 0, 256)]
                k0 = 4 * (j % 2)
                left, right = ((j // 2, 0), (j // 2, 1)) if j < 6 else ((0, 2), (1, 2))
                return [(cols_of(w, col(*left), 256, k0, 4), 4, 0, 256), (cols_of(w, col(*right), 256, k0, 4), 4, 256, 256)]
            if M_IN <= m < M_OUT1:
                c, j = divmod(m - M_IN, 2)
                first = [0, 1024, 2048, 512, 1536, 2560, 3072, 3584][c]
                return [(cols_of(a["hgrn_w_in"][0], first, 512, 4 * j, 4), 4, 0, 512)]
            for base, w in ((M_OUT0, a["attn_w_out"][0]), (M_OUT1, a["hgrn_w_out"][0])):
                if base <= m < base + 4:
                    return [(cols_of(w, 0, 1024, 2 * (m - base), 2), 2, 0, 1024)]
            layer, r = (0, m - M_FFN0) if m < M_IN else (1, m - M_FFN1)
            kind, j = ffn_step(r)
            if kind == 2:
                return [(cols_of(a["ffn_w2"][layer], 0, 1024, 2 * j, 2), 2, 0, 1024)]
            return [(cols_of(a["ffn_w1"][layer], j * FC, FC, 4 * kind, 4), 4, 0, FC),
                    (cols_of(a["ffn_w3"][layer], j * FC, FC, 4 * kind, 4), 4, FC, FC)]

        def ffn_step(r):
            if r < 2:
                return r, 0
            if r == 3 * NF - 1:
                return 2, NF - 1
            j, k = divmod(r + 1, 3)
            return (k, j) if k < 2 else (2, j - 1)

        need, came = [], [0] * RAW
        for m in range(UNITS):
            came[m % RAW] += 16 * len(pieces(m))
            need.append(came[m % RAW])

        def load_bias(sp, h):
            if h >= 2:
                sp.wait_ge(s["att_nm"], 2 * (h - 1))
            skewed = bass.AP(scratch.tensor, h * TABLE, [[1, P], [HEADS * TABLE, NG], [1, SEQ]])
            sp.dma_start(bias[:, h % 2], skewed).then_inc(bias_in[h % 2], 16)

        @block.sync
        def _(sp):
            sp.dma_start(x[:], a["x"][0].rearrange("(t p) d -> p t d", p=P)).then_inc(s["x_in"], 16)
            for n, (name, r0, nr) in enumerate(ROWS):
                src = a[name].rearrange(ROW_AP[name], d=P)
                sp.dma_start(rows[r0:r0 + nr, :], src).then_inc(s["rows_in"], 16)
            for g in range(NG):
                sp.wait_ge(s["pool_setup"], 4)
                sp.dma_start(rel3[g * BUCKETS:(g + 1) * BUCKETS, g * HEADS:(g + 1) * HEADS],
                             a["rel_bias"][:, g * HEADS:(g + 1) * HEADS]).then_inc(s["rel_in"], 16)
            sp.dma_start(rel3[NG * BUCKETS:, :], a["mask_rows"]).then_inc(s["rel_in"], 16)
            sp.dma_start(tabw, a["distance_table"]).then_inc(s["rel_in"], 16)
            for m in range(UNITS):
                if m == 0:
                    sp.wait_ge(s["ada_used"], KC)
                if m >= RAW:
                    sp.wait_ge(s["split"], m - RAW + 1)
                for src, nk, c0, n in pieces(m):
                    slot = raw[:, m % RAW, :].rearrange("p (k n) -> p k n", k=nk)
                    sp.dma_start(slot[:, :, c0:c0 + n], src).then_inc(raw_in[m % RAW], 16)
                if m == 2:
                    sp.dma_start(masks[:], a["tree_masks"]).then_inc(s["masks_in"], 16)
                    sp.wait_ge(s["tab_cp"], 1)
                    sp.dma_start(scratch, tabT).then_inc(s["tab_out"], 16)
                    sp.wait_ge(s["tab_out"], 16)
                    load_bias(sp, 0)
                    load_bias(sp, 1)
                for h in range(2, HEADS):
                    if m == QU * (h // 2 + 1) + 4 * (h % 2):
                        load_bias(sp, h)
            sp.wait_ge(s["res"], 16)
            sp.dma_start(out[0].rearrange("(t p) d -> p t d", p=P), x[:]).then_inc(s["out_done"], 16)
            sp.wait_ge(s["out_done"], 16)

        @block.gpsimd
        def _(pool):
            pool.memset(ident[:], 0.0).then_inc(s["pool_setup"], 1)
            pool.memset(ones[:], 1.0).then_inc(s["pool_setup"], 1)
            pool.memset(eps[:], EPS).then_inc(s["pool_setup"], 1)
            pool.memset(rel3, 0.0).then_inc(s["pool_setup"], 1)
            pool.memset(acc[:], 0.0).then_inc(s["ada_zero"], 1)
            pool.wait_ge(s["pool_setup"], 1)
            pool.affine_select(out=ident[:], in_=ident[:], compare_op=ALU.not_equal, fill=1.0, base=0,
                               pattern=[[-1, P]], channel_multiplier=1).then_inc(s["pool_setup"], 1)
            for n in range(2 * ADA_BLOCKS * KC):
                layer, b, k = n // (ADA_BLOCKS * KC), n // KC % ADA_BLOCKS, n % KC
                if k == 0:
                    blk = ADA_BLOCKS * layer + b
                    if blk >= 2:
                        pool.wait_ge(s["ada_red"], tasks_until(blk - 2))
                        pool.memset(acc[:, blk % 2], 0.0).then_inc(s["ada_zero"], 1)
                    pool.wait_ge(s["ada_zero"], max(1, blk))
                    pool.dma_start(acc[0:1, blk % 2, :], a["ada_b"][layer:layer + 1, b * ADA_COLS:(b + 1) * ADA_COLS]
                                   ).then_inc(s[f"adab_in{blk % 2}"], 16)
                if n < 2 * KC:
                    if n >= FIRST:
                        pool.wait_ge(s["ada_used"], n - FIRST + 1)
                    pool.dma_start(first_w[n % FIRST], a["ada_w"][layer, k * P:(k + 1) * P, b * ADA_COLS:(b + 1) * ADA_COLS]
                                   ).then_inc(first_in[n % FIRST], 16)
                    continue
                if n >= 2 * KC + ADA_RING:
                    pool.wait_ge(s["ada_used"], n - ADA_RING + 1)
                pool.dma_start(ada_w[:, n % ADA_RING], a["ada_w"][layer, k * P:(k + 1) * P, b * ADA_COLS:(b + 1) * ADA_COLS]
                               ).then_inc(ada_in[n % ADA_RING], 16)

        PURE = PAIRS * QU

        def chunk_end(n):
            pr, c = divmod(n, 5)
            return pr * QU + (2 * c + 2 if c < 4 else 9)

        def blocks_of(qt):
            return [(g, kt) for g in range(NG) for kt in range(qt + 1)]

        VSTEPS = 45 - M_OUT0

        def gh(level):
            return 1 << (level - 1)

        def hT4(n):
            return hT[:, 2 * n:2 * n + 2, :].rearrange("p a (b t) -> p (a b) t", b=2)

        @block.tensor
        def _(pe):
            def unit(m, lhs_hi, lhs_lo, nk, k0, n, dst, first, last):
                sl = m % SPL
                w = [v[:, sl, :].rearrange("p (k n) -> p k n", k=nk) for v in (whi, wlo)]
                pe.wait_ge(s["split"], m + 1)
                for t in range(T):
                    for k in range(nk):
                        hi = lhs_hi[:, k0 + k, t * P:(t + 1) * P]
                        lo = lhs_lo[:, k0 + k, t * P:(t + 1) * P]
                        for c, d in enumerate(dst[t]):
                            cut = slice(c * 512, c * 512 + n)
                            for q, (l, r) in enumerate(((hi, w[0]), (hi, w[1]), (lo, w[0]))):
                                mm = nc.tensor.matmul(d[:, 0:n], l, r[:, k, cut],
                                                      start=first and k == 0 and q == 0,
                                                      stop=last and k == nk - 1 and q == 2)
                mm.then_inc(s["pe_unit"], 1)

            def norm_t(q):
                pe.wait_ge(s["xn_s"], 2 * (q + 1))
                for grp in range(4):
                    for k in range(2):
                        for t in range(T):
                            c = (2 * grp + k) * P
                            mm = nc.tensor.transpose(bank[4 + grp][:, k * SEQ + t * P:k * SEQ + (t + 1) * P],
                                                     xn[:, t, c:c + P], ident[:])
                    mm.then_inc(s["xn_tr"], 1)

            pv = [0, 0]

            def reduce_task(r, b=7):
                blk, kind, half = TASKS[r]
                pe.wait_ge(s["ada_used"], KC * (blk + 1))
                if r:
                    pe.wait_ge(s["ada_ev"], r)
                if pv[0]:
                    pe.wait_ge(s["ot_ev"], pv[0])
                pv[1] = r + 1
                src = acc[:, blk % 2, :]
                if kind == "row":
                    mm = nc.tensor.matmul(bank[b][:], ones[:], src[:, half:half + 512], start=True, stop=True)
                else:
                    for j in range(kind):
                        mm = nc.tensor.matmul(bank[b][:, j:j + 1], src[:, half + j * P:half + (j + 1) * P],
                                              ones[:, 0:1], start=True, stop=True)
                mm.then_inc(s["ada_red"], 1)

            pe.wait_ge(s["rows_in"], 16 * len(ROWS))
            pe.wait_ge(s["pool_setup"], 5)
            nc.tensor.transpose(bank[0][:, 0:NROWS], rows[0:NROWS, :], ident[0:NROWS, 0:NROWS]).then_inc(s["cols_t"], 1)
            pe.wait_ge(s["rel_in"], 16 * 5)
            nc.tensor.matmul(bank[1][0:GH, 0:TABLE], rel3, tabw, start=True, stop=True).then_inc(s["tab_mm"], 1)
            norm_t(0)
            pe.wait_ge(s["ada_used"], KC)
            for r in range(2):
                reduce_task(r, 3)
            pe.wait_ge(s["tab_cp"], 1)

            def qkv_unit(m):
                pr, j = divmod(m, QU)
                n = 5 * pr + min(j // 2, 4)
                if m == 0:
                    pe.wait_ge(s["xn_lo"], 4)
                if j % 2 == 0 and n >= 2:
                    c = (n - 2) % 5
                    if c < 3:
                        pe.wait_ge(s["qk_norm"], 3 * ((n - 2) // 5) + c + 1)
                    else:
                        pe.wait_ge(s["v_ev"], 2 * ((n - 2) // 5) + c - 2)
                b = 2 * (n % 2)
                nk, w = (8, 256) if j == 8 else (4, 512)
                unit(m, hT_hi, hT_lo, nk, 0 if j == 8 else 4 * (j % 2), w, [[bank[b]], [bank[b + 1]]],
                     j % 2 == 0, j % 2 == 1 or j == 8)

            def qk_transposes(n, which):
                pe.wait_ge(s["qk_norm"], n + 1)
                pe.wait_ge(s["qk_tev"], 2 * n + which)
                for h in range(2):
                    for t in range(T):
                        c = t * 512 + (2 * which + h) * P
                        mm = nc.tensor.transpose(bank[6][:, h * SEQ + t * P:h * SEQ + (t + 1) * P],
                                                 qkn[:, n % 2, c:c + P], ident[:])
                mm.then_inc(s["qk_tr"], 1)

            def att_scores(J):
                pr, hh, qt = J // 4, J // 2 % 2, 1 - J % 2
                pe.wait_ge(s["qk_tev"], 6 * (pr + 1))
                if J:
                    pe.wait_ge(s["pt_ev"], J)
                w = (qt + 1) * P
                for g in range(NG):
                    dst = bank[4][:, g * w:(g + 1) * w] if (g + 1) * w <= 512 else bank[5][:, 0:w]
                    base = hh * SEQ
                    mm = nc.tensor.matmul(dst, qT[:, pr % 2, g, base + qt * P:base + (qt + 1) * P],
                                          kT[:, pr % 2, g, base:base + w], start=True, stop=True)
                mm.then_inc(s["att_s"], 1)

            def att_transposes(J):
                qt = 1 - J % 2
                pe.wait_ge(s["att_pn"], J + 1)
                for i in range(len(blocks_of(qt))):
                    mm = nc.tensor.transpose(bank[4 + i // 4][:, i % 4 * P:(i % 4 + 1) * P],
                                             prob[:, i * P:(i + 1) * P], ident[:])
                mm.then_inc(s["att_tr"], 1)

            def att_values(J):
                pr, hh, qt = J // 4, J // 2 % 2, 1 - J % 2
                pe.wait_ge(s["pt_ev"], J + 1)
                pe.wait_ge(s["v_ev"], 2 * (pr + 1))
                if J:
                    pe.wait_ge(s["ot_ev"], J)
                pe.wait_ge(s["ada_ev"], pv[1])
                pv[0] = J + 1
                todo = blocks_of(qt)
                for i, (g, kt) in enumerate(todo):
                    c = g * 256 + hh * P
                    mm = nc.tensor.matmul(bank[7][:, 0:P], vN[:, pr % 2, kt, c:c + P], probT[:, i * P:(i + 1) * P],
                                          start=i == 0, stop=i == len(todo) - 1)
                mm.then_inc(s["att_pv"], 1)

            def qkv_extra(m):
                pr, j = divmod(m, QU)
                if pr >= 1:
                    J = 4 * (pr - 1) + j // 2
                    if j % 2 == 0 and j < 8:
                        att_scores(J)
                    if j % 2 == 0 and j > 0:
                        att_values(J - 1)
                    if j % 2 == 1:
                        att_transposes(J)
                if pr < PAIRS and 3 <= j <= 8:
                    qk_transposes(3 * pr + (j - 3) // 2, (j - 3) % 2)

            for m in range(PURE):
                qkv_unit(m)
                qkv_extra(m)
                for r in tasks_at(m):
                    reduce_task(r)
            Y = [[bank[0], bank[1]], [bank[2], bank[3]]]
            for v in range(QU):
                if v < 3:
                    if v == 0:
                        pe.wait_ge(s["v_ev"], 2 * PAIRS)
                        pe.wait_ge(s["qk_norm"], 3 * PAIRS)
                    pe.wait_ge(s["ot_ev"], 4 * (v + 1))
                    unit(M_OUT0 + v, oT_hi, oT_lo, 2, 2 * v, 512, Y, v == 0, False)
                qkv_extra(PURE + v)
            pe.wait_ge(s["ot_ev"], 16)
            unit(M_OUT0 + 3, oT_hi, oT_lo, 2, 6, 512, Y, False, True)

            def ffn(f, base):
                q = 2 * f + 1
                pe.wait_ge(s["ada_ev"], 8)
                norm_t(q)
                pe.wait_ge(s["xn_lo"], 4 * (q + 1))
                for r in range(3 * NF):
                    kind, j = ffn_step(r)
                    n = NF * f + j
                    if kind < 2:
                        if kind == 0 and j:
                            pe.wait_ge(s["f_hid"], n)
                        unit(base + r, hT_hi, hT_lo, 4, 4 * kind, 512, [[bank[4]], [bank[5]]], kind == 0, kind == 1)
                    else:
                        pe.wait_ge(s["f_lo"], n + 1)
                        unit(base + r, hidT(oT_hi, n), hidT(oT_lo, n), 2, 0, 512, Y, j == 0, j == NF - 1)
                    jt = 0 if r == 1 else j + 1 if kind == 2 and j < NF - 1 else None
                    if jt is not None:
                        n = NF * f + jt
                        pe.wait_ge(s["f_hid"], n + 1)
                        if n:
                            pe.wait_ge(s["f_lo"], n)
                        for k in range(2):
                            for t in range(T):
                                mm = nc.tensor.transpose(bank[6][:, k * SEQ + t * P:k * SEQ + (t + 1) * P],
                                                         hid[:, t, k * P:(k + 1) * P], ident[:])
                        mm.then_inc(s["f_tr"], 1)
                    if f == 0:
                        for task in tasks_at(M_FFN0 + r):
                            reduce_task(task)

            ffn(0, M_FFN0)

            norm_t(2)
            pe.wait_ge(s["xn_lo"], 12)

            def rec_transposes(c):
                n = {0: 0, 1: 1, 3: 2, 4: 3}[c]
                pe.wait_ge(s["r_nat"], c + 1)
                if n:
                    pe.wait_ge(s["r_tev"], n)
                for h in range(4):
                    for t in range(T):
                        mm = nc.tensor.transpose(bank[6 + h // 2][:, h % 2 * SEQ + t * P:h % 2 * SEQ + (t + 1) * P],
                                                 nat[:, t, h * P:(h + 1) * P], ident[:])
                mm.then_inc(s["r_tr"], 1)

            def rec_level(half, level):
                n = (LEVELS + 1) * half + level
                if level:
                    pe.wait_ge(s["r_q"], LEVELS * half + level)
                else:
                    pe.wait_ge(s["r_k"], half + 1)
                if n:
                    pe.wait_ge(s["r_A"], n)
                if half and level == 0:
                    pe.wait_ge(s["r_oev"], 2)
                if level == 0:
                    q_, k_ = rq, rk
                else:
                    q_ = k_ = rZ[:, level % 2]
                for h in range(4):
                    c = slice(h * P, (h + 1) * P)
                    if level < LEVELS:
                        for t in range(T):
                            tok = slice(h * SEQ + t * P, h * SEQ + (t + 1) * P)
                            mm = nc.tensor.matmul(bank[4 + t][:, c], k_[:, tok], q_[:, tok], start=True, stop=True)
                    else:
                        mm = nc.tensor.matmul(bank[4][:, c], k_[:, h * SEQ:h * SEQ + P],
                                              q_[:, h * SEQ + P:(h + 1) * SEQ], start=True, stop=True)
                mm.then_inc(s["r_mm"], 1)

            def rec_out(half, t):
                pe.wait_ge(s["r_A"], (LEVELS + 1) * (half + 1))
                pe.wait_ge(s["r_nat"], 6 if half else 3)
                for h in range(4):
                    c = slice(h * P, (h + 1) * P)
                    v = slice(half * 512 + h * P, half * 512 + (h + 1) * P)
                    mm = nc.tensor.matmul(bank[4 + t][:, c], Am[:, t, c], rV[:, t, v], start=True, stop=t == 0)
                    if t:
                        mm = nc.tensor.matmul(bank[4 + t][:, c], Am[:, 2, c], rV[:, 0, v], start=False, stop=True)
                mm.then_inc(s["r_o"], 1)

            for c in range(8):
                for j in range(2):
                    if j == 0 and c >= 2:
                        pe.wait_ge(s["r_nat"], c - 1)
                    b = 2 * (c % 2)
                    unit(M_IN + 2 * c + j, hT_hi, hT_lo, 4, 4 * j, 512, [[bank[b]], [bank[b + 1]]], j == 0, j == 1)
                    step = 2 * c + j
                    if step in (2, 4, 8, 10):
                        rec_transposes(step // 2 - 1)
                    for half, level in levels_at(step):
                        rec_level(half, level)
                    if step == 9:
                        for t in range(T):
                            rec_out(0, t)
            for half, level in levels_at(16):
                rec_level(half, level)
            for t in range(T):
                rec_out(1, t)
            for t in range(T):
                pe.wait_ge(s["r_on"], t + 1)
                for g in range(2):
                    n = 2 * t + g
                    if n >= 2:
                        pe.wait_ge(s["r_olo"], n - 1)
                    for h in range(4):
                        mm = nc.tensor.transpose(bank[4 + g][:, h * P:(h + 1) * P],
                                                 rV[:, t, (4 * g + h) * P:(4 * g + h + 1) * P], ident[:])
                    mm.then_inc(s["r_otr"], 1)
            pe.wait_ge(s["r_olo"], 4)
            pe.wait_ge(s["r_nat"], 8)
            for v in range(4):
                unit(M_OUT1 + v, oT_hi, oT_lo, 2, 2 * v, 512, Y, v == 0, v == 3)
            ffn(1, M_FFN1)

        @block.scalar
        def _(act):
            count = {}

            def copy(dst, src):
                return nc.scalar.activation(dst, src, ACT.Copy)

            def round_unit(m):
                if m >= UNITS:
                    return
                act.wait_ge(raw_in[m % RAW], need[m])
                if m >= SPL:
                    act.wait_ge(s["pe_unit"], m - SPL + 1)
                copy(whi[:, m % SPL, :], raw[:, m % RAW, :]).then_inc(s["rounded"], 1)

            def rsqrt(dst, src, ln_sem, out_sem, n, scale):
                nc.scalar.activation(dst, src, ACT.Ln, bias=eps[:, 0:1], scale=scale).then_inc(s[ln_sem], 1)
                act.wait_ge(s[ln_sem], n + 1)
                nc.scalar.activation(dst, dst, ACT.Exp, scale=-0.5).then_inc(s[out_sem], 1)

            def norm_stats(q):
                if q:
                    act.wait_ge(s["res"], 4 * q)
                else:
                    act.wait_ge(s["x_in"], 16)
                    act.wait_ge(s["pool_setup"], 3)
                for t in range(T):
                    if q or t:
                        act.wait_ge(s["xn_ssq"], 2 * q + t)
                    nc.scalar.activation(prob_junk, x[:, t], ACT.Square, accum_out=small[:, t:t + 1]
                                         ).then_inc(s["xn_ssq"], 1)
                act.wait_ge(s["xn_ssq"], 2 * (q + 1))
                rsqrt(small[:, 2:4], small[:, 0:2], "xn_ln", "xn_rstd", q, 1.0 / D)

            def norm_round(q):
                for grp in range(4):
                    act.wait_ge(s["xn_aff"], 4 * q + grp + 1)
                    copy(hT_hi[:, 2 * grp:2 * grp + 2, :], hT[:, 2 * grp:2 * grp + 2, :]).then_inc(s["xn_hi"], 1)

            prob_junk = sq[:, :, :].rearrange("p a b -> p (a b)")

            act.wait_ge(s["cols_s"], 1)
            nc.scalar.activation(cact[:], cols[:, 0:KC], ACT.Silu).then_inc(s["cact_s"], 1)
            act.wait_ge(s["lbd_s"], 1)
            nc.scalar.activation(lb[:, 0, :], lbd[:], ACT.Sigmoid).then_inc(s["lb_s"], 1)
            nc.scalar.preload_act_table_set("natural_log_exp_and_others")
            norm_stats(0)
            for m in range(AHEAD):
                round_unit(m)
            norm_round(0)

            def qk_square(n):
                act.wait_ge(s["pe_unit"], chunk_end(5 * (n // 3) + n % 3))
                if n:
                    act.wait_ge(s["qk_red"], n)
                b = 2 * ((5 * (n // 3) + n % 3) % 2)
                for t in range(T):
                    i = nc.scalar.activation(sq[:, t], bank[b + t][:], ACT.Square)
                i.then_inc(s["qk_sq"], 1)

            def qk_rsqrt(n):
                act.wait_ge(s["qk_red"], n + 1)
                if n:
                    act.wait_ge(s["qk_norm"], n)
                rsqrt(small[:, 16:24], small[:, 8:16], "qk_ln", "qk_rstd", n, 1.0 / P)

            def qk_evac(n, which):
                pr, g = divmod(n, 3)
                act.wait_ge(s["qk_tr"], 2 * n + which + 1)
                if pr >= 2:
                    act.wait_ge(s["att_s"], 4 * (pr - 1))
                view = lambda y: y.rearrange("p (b t) -> p b t", t=P)
                dst, src = view((qT, kT)[which][:, pr % 2, g, :]), view(bank[6][:])
                if which == 0:
                    src = src[:, :, ::-1]
                nc.scalar.activation(dst, src, ACT.Copy, scale=gains[:, which * NG + g:which * NG + g + 1]
                                     ).then_inc(s["qk_tev"], 1)

            def v_evac(pr, c):
                n = 5 * pr + 3 + c
                act.wait_ge(s["pe_unit"], chunk_end(n))
                if pr >= 2:
                    act.wait_ge(s["att_pv"], 4 * (pr - 1))
                b = 2 * (n % 2)
                for t in range(T):
                    i = copy(vN[:, pr % 2, t, 512:768], bank[b + t][:, 0:256]) if c else \
                        copy(vN[:, pr % 2, t, 0:512], bank[b + t][:])
                i.then_inc(s["v_ev"], 1)

            def att_exp(J):
                w = 768 if J % 2 == 0 else 384
                act.wait_ge(s["att_nm"], J + 1)
                nc.scalar.activation(prob[:, 0:w], prob[:, 0:w], ACT.Exp, bias=small[:, 26:27],
                                     accum_out=small[:, 27:28]).then_inc(s["att_p"], 1)

            def att_evac(J):
                act.wait_ge(s["att_tr"], J + 1)
                if J:
                    act.wait_ge(s["att_pv"], J)
                if J % 2 == 0:
                    copy(probT[:, 0:512], bank[4][:])
                    i = copy(probT[:, 512:768], bank[5][:, 0:256])
                else:
                    i = copy(probT[:, 0:384], bank[4][:, 0:384])
                i.then_inc(s["pt_ev"], 1)

            def att_out(J):
                h, qt = J // 2, 1 - J % 2
                act.wait_ge(s["att_pv"], J + 1)
                copy(oT_hi[:, h, qt * P:(qt + 1) * P], bank[7][:, P - 1::-1]).then_inc(s["ot_hi"], 1)

            def qkv_extra(m):
                pr, j = divmod(m, QU)
                if pr < PAIRS and j in (1, 3, 5):
                    qk_square(3 * pr + j // 2)
                if pr < PAIRS and j in (2, 4, 6):
                    qk_rsqrt(3 * pr + j // 2 - 1)
                if pr >= 1:
                    J = 4 * (pr - 1) + j // 2
                    if j % 2 == 0 and j > 0:
                        att_out(J - 1)
                    if j % 2 == 0 and j < 8:
                        att_exp(J)
                    if j % 2 == 1:
                        att_evac(J)
                if pr < PAIRS:
                    if 3 <= j <= 8:
                        qk_evac(3 * pr + (j - 3) // 2, (j - 3) % 2)
                    if j >= 7:
                        v_evac(pr, j - 7)

            gains = cols[:, GAIN0:GAIN0 + 2 * NG]
            act.wait_ge(s["cols_s"], 2)
            for m in range(PURE):
                round_unit(m + AHEAD)
                qkv_extra(m)
            for v in range(QU):
                if v < 4:
                    round_unit(M_OUT0 + v + AHEAD) if v < 3 else None
                qkv_extra(PURE + v)
            round_unit(M_OUT0 + 3 + AHEAD)

            def ffn(f, base):
                norm_stats(2 * f + 1)
                nc.scalar.preload_act_table(ACT.Silu)
                norm_round(2 * f + 1)
                for r in range(3 * NF):
                    kind, j = ffn_step(r)
                    round_unit(base + r + AHEAD)
                    if kind == 1:
                        n = NF * f + j
                        act.wait_ge(s["pe_unit"], base + r + 1)
                        if n:
                            act.wait_ge(s["f_hid"], n)
                        for t in range(T):
                            i = nc.scalar.activation(sil[:, t], bank[4 + t][:, 0:FC], ACT.Silu)
                        i.then_inc(s["f_sil"], 1)
                    jt = 0 if r == 1 else j + 1 if kind == 2 and j < NF - 1 else None
                    if jt is not None:
                        n = NF * f + jt
                        act.wait_ge(s["f_tr"], n + 1)
                        if n >= 2:
                            act.wait_ge(s["pe_unit"], base_of(n - 2) + 1)
                        copy(hidT(oT_hi, n), bank[6][:].rearrange("p (k t) -> p k t", k=2)).then_inc(s["f_hi"], 1)

            ffn(0, M_FFN0)
            nc.scalar.preload_act_table_set("natural_log_exp_and_others")
            norm_stats(2)
            norm_round(2)

            def rec_exp(half, level):
                n = LEVELS * half + level - 1
                act.wait_ge(s["r_D"], n + 1)
                nc.scalar.activation(rE[:, level % 2], rE[:, level % 2], ACT.Exp).then_inc(s["r_E"], 1)

            def rec_cross(half):
                n = (LEVELS + 1) * half + LEVELS
                act.wait_ge(s["r_mm"], n + 1)
                copy(Am[:, 2], bank[4][:]).then_inc(s["r_A"], 1)

            def rec_out(half):
                act.wait_ge(s["r_o"], 2 * half + 2)
                act.wait_ge(s["r_ored"], 2 * half) if half else None
                for t in range(T):
                    nc.scalar.activation(sq[:, t], bank[4 + t][:], ACT.Square).then_inc(s["r_osq"], 1)
                    copy(rV[:, t, half * 512:(half + 1) * 512], bank[4 + t][:]).then_inc(s["r_oev"], 1)

            for step in range(16):
                c, j = divmod(step, 2)
                round_unit(M_IN + step + AHEAD)
                if j == 1:
                    act.wait_ge(s["pe_unit"], M_IN + step + 1)
                    b = 2 * (c % 2)
                    for t in range(T):
                        src = bank[b + t][:]
                        if c in (2, 5):
                            h = c // 3
                            i = copy(rV[:, t, h * 512:(h + 1) * 512], src)
                        elif c < 6:
                            if c:
                                act.wait_ge(s["r_tr"], {1: 1, 3: 2, 4: 3}[c])
                            i = copy(nat[:, t], src)
                        else:
                            i = nc.scalar.activation(gates[:, t, (c - 6) * 512:(c - 5) * 512], src, ACT.Silu)
                    i.then_inc(s["r_nat"], 1)
                if step == 9:
                    rec_out(0)
                if step in (2, 4, 9, 10):
                    n = {2: 0, 4: 1, 9: 2, 10: 3}[step]
                    act.wait_ge(s["r_tr"], n + 1)
                    if n == 2:
                        act.wait_ge(s["r_q"], LEVELS)
                    if n == 3:
                        act.wait_ge(s["r_mm"], LEVELS + 1)
                    dst = rq if n % 2 == 0 else rk
                    for g in range(2):
                        i = nc.scalar.activation(dst[:, g * 512:(g + 1) * 512], bank[6 + g][:],
                                                 ACT.Silu if n % 2 == 0 else ACT.Sigmoid)
                    i.then_inc(s["r_tev"], 1)
                    if n % 2:
                        act.wait_ge(s["r_fg"], n // 2 + 1)
                        nc.scalar.activation(rG, rE[:, 0], ACT.Ln).then_inc(s["r_ln"], 1)
                for half, level in levels_at(step):
                    if level:
                        rec_exp(half, level)
                    if level == LEVELS:
                        rec_cross(half)
            for half, level in levels_at(16):
                if level:
                    rec_exp(half, level)
                if level == LEVELS:
                    rec_cross(half)
            rec_out(1)
            act.wait_ge(s["r_ored"], 4)
            rsqrt(small[:, 48:64], small[:, 32:48], "r_oln", "r_orstd", 0, 1.0 / P)
            for n in range(4):
                t, g = divmod(n, 2)
                act.wait_ge(s["r_otr"], n + 1)
                act.wait_ge(s["r_gn"], n + 1)
                copy(oT_hi[:, 4 * g:4 * g + 4, t * P:(t + 1) * P], hT4(n)).then_inc(s["r_ohi"], 1)
            for v in range(4):
                round_unit(M_OUT1 + v + AHEAD)
            ffn(1, M_FFN1)

        @block.vector
        def _(dve):
            def fp(v):
                return v.bitcast(F32)

            def split_unit(m):
                if m >= UNITS:
                    return
                dve.wait_ge(s["rounded"], m + 1)
                nc.vector.tensor_tensor(wlo[:, m % SPL, :], raw[:, m % RAW, :], fp(whi[:, m % SPL, :]), ALU.subtract
                                        ).then_inc(s["split"], 1)

            def ada_op(n):
                blk, k = divmod(n, KC)
                if n < 2 * KC:
                    w = first_w[n % FIRST]
                    dve.wait_ge(first_in[n % FIRST], 16 * (n // FIRST + 1))
                else:
                    w = ada_w[:, n % ADA_RING]
                    dve.wait_ge(ada_in[n % ADA_RING], 16 * ((n - 2 * KC) // ADA_RING + 1))
                if k == 0:
                    dve.wait_ge(s[f"adab_in{blk % 2}"], 16 * (blk // 2 + 1))
                if n:
                    dve.wait_ge(s["ada_used"], n)
                nc.vector.scalar_tensor_tensor(out=acc[:, blk % 2], in0=w, scalar=cact[:, k:k + 1],
                                               in1=acc[:, blk % 2], op0=ALU.mult, op1=ALU.add
                                               ).then_inc(s["ada_used"], 1)

            def ada_evac(r, b=7):
                blk, kind, half = TASKS[r]
                layer = blk // ADA_BLOCKS
                dve.wait_ge(s["ada_red"], r + 1)
                src = bank[b][:, 0:KC]
                what = blk % ADA_BLOCKS
                if what in (2, 5):
                    dst = late_gate if (layer, what) == (1, 5) else gate[:, what // 5, :]
                    i = nc.vector.tensor_copy(dst[:, half:half + 512], bank[b][:])
                elif what in (0, 3):
                    i = nc.vector.tensor_copy(mod_b[:, layer, what // 3], src)
                else:
                    i = scale_gain(layer, what // 4, src)
                i.then_inc(s["ada_ev"], 1)

            def scale_gain(layer, sub, src):
                g = cols[:, NORM0 + (2 * sub + layer) * KC:NORM0 + (2 * sub + layer + 1) * KC]
                return nc.vector.scalar_tensor_tensor(out=mod_a[:, layer, sub], in0=src, scalar=1.0, in1=g,
                                                      op0=ALU.add, op1=ALU.mult)

            def norm_scale(q):
                dve.wait_ge(s["xn_rstd"], q + 1)
                for t in range(T):
                    nc.vector.tensor_scalar(xn[:, t], x[:, t], small[:, 2 + t:3 + t], None, ALU.mult
                                            ).then_inc(s["xn_s"], 1)

            def norm_affine(q):
                layer, sub = q // 2, q % 2
                for grp in range(4):
                    dve.wait_ge(s["xn_tr"], 4 * q + grp + 1)
                    for k in range(2):
                        kc = 2 * grp + k
                        i = nc.vector.tensor_scalar(hT[:, kc], bank[4 + grp][:, k * SEQ:(k + 1) * SEQ],
                                                    mod_a[:, layer, sub, kc:kc + 1], mod_b[:, layer, sub, kc:kc + 1],
                                                    ALU.mult, ALU.add)
                    i.then_inc(s["xn_aff"], 1)
                for grp in range(4):
                    dve.wait_ge(s["xn_hi"], 4 * q + grp + 1)
                    cut = slice(2 * grp, 2 * grp + 2)
                    nc.vector.tensor_tensor(hT_lo[:, cut, :], hT[:, cut, :], fp(hT_hi[:, cut, :]), ALU.subtract
                                            ).then_inc(s["xn_lo"], 1)

            def residual(q, last_unit):
                g = gate[:, 0, :] if q % 2 == 0 else (gate[:, 1, :] if q == 1 else late_gate)
                dve.wait_ge(s["pe_unit"], last_unit + 1)
                for b in range(4):
                    t, c = divmod(b, 2)
                    cut = slice(c * 512, (c + 1) * 512)
                    n = 4 * q + b
                    if n >= 2:
                        dve.wait_ge(s["res"], n - 1)
                    nc.vector.tensor_tensor(sq[:, b % 2], bank[b][:], g[:, cut], ALU.mult).then_inc(s["yres_t"], 1)
                    dve.wait_ge(s["yres_t"], n + 1)
                    nc.vector.tensor_tensor(x[:, t, cut], x[:, t, cut], sq[:, b % 2], ALU.add).then_inc(s["res"], 1)

            dve.wait_ge(s["cols_t"], 1)
            nc.vector.tensor_copy(cols[:, 0:NROWS], bank[0][:, 0:NROWS]).then_inc(s["cols_s"], 1)
            dve.wait_ge(s["cols_s"], 1)
            nc.vector.tensor_scalar(cols[:, GAIN0:GAIN0 + NG], cols[:, GAIN0:GAIN0 + NG], float(P) ** -0.5, None,
                                    ALU.mult).then_inc(s["cols_s"], 1)
            nc.vector.tensor_tensor(lbd[:], cols[:, LB0 + KC:LB0 + 2 * KC], cols[:, LB0:LB0 + KC], ALU.subtract
                                    ).then_inc(s["lbd_s"], 1)
            dve.wait_ge(s["tab_mm"], 1)
            nc.vector.tensor_copy(tabT, bank[1][0:GH, 0:TABLE]).then_inc(s["tab_cp"], 1)
            dve.wait_ge(s["lb_s"], 1)
            nc.vector.tensor_scalar(lb[:, 1, :], lb[:, 0, :], -1.0, 1.0, ALU.mult, ALU.add).then_inc(s["lbd_s"], 1)
            dve.wait_ge(s["cact_s"], 1)
            dve.wait_ge(s["ada_zero"], 1)
            norm_scale(0)
            for n in range(2 * KC):
                ada_op(n)
            for m in range(AHEAD):
                split_unit(m)
            for r in range(2):
                ada_evac(r, 3)
            dve.wait_ge(s["ada_ev"], 2)
            norm_affine(0)

            def qk_reduce(n):
                dve.wait_ge(s["qk_sq"], n + 1)
                if n:
                    dve.wait_ge(s["qk_rstd"], n)
                nc.vector.tensor_reduce(small[:, 8:16], sq[:, :, :].rearrange("p t (h d) -> p (t h) d", d=P), AX_X,
                                        ALU.add).then_inc(s["qk_red"], 1)

            def qk_normalise(n):
                dve.wait_ge(s["qk_rstd"], n + 1)
                if n >= 2:
                    dve.wait_ge(s["qk_tr"], 2 * (n - 1))
                if n == 0:
                    dve.wait_ge(s["tab_out"], 16)
                b = 2 * ((5 * (n // 3) + n % 3) % 2)
                for t in range(T):
                    r = small[:, 16 + 4 * t:20 + 4 * t].rearrange("p (h o) -> p h o", o=1).to_broadcast([P, 4, P])
                    i = nc.vector.tensor_tensor(qkn[:, n % 2, t * 512:(t + 1) * 512].rearrange("p (h d) -> p h d", d=P),
                                                bank[b + t][:].rearrange("p (h d) -> p h d", d=P), r, ALU.mult)
                i.then_inc(s["qk_norm"], 1)

            def att_max(J):
                h, qt = J // 2, 1 - J % 2
                dve.wait_ge(s["att_s"], J + 1)
                if J:
                    dve.wait_ge(s["att_tr"], J)
                dve.wait_ge(bias_in[h % 2], 16 * (h // 2 + 1))
                mx = small[:, 24:26]
                if qt:
                    nc.vector.tensor_tensor_reduce(prob[:, 0:512].rearrange("p (g k) -> p g k", g=2),
                                                   bank[4][:].rearrange("p (g k) -> p g k", g=2),
                                                   bias[:, h % 2, 0:2, :], 1.0, -3e38, ALU.add, ALU.max,
                                                   mx[:, 0:1])
                    nc.vector.tensor_tensor_reduce(prob[:, 512:768], bank[5][:, 0:256], bias[:, h % 2, 2, :], 1.0,
                                                   -3e38, ALU.add, ALU.max, mx[:, 1:2]).then_inc(s["att_m"], 1)
                    dve.wait_ge(s["att_m"], J + 1)
                    nc.vector.tensor_scalar(small[:, 26:27], mx[:, 0:1], mx[:, 1:2], -1.0, ALU.max, ALU.mult
                                            ).then_inc(s["att_nm"], 1)
                else:
                    nc.vector.tensor_tensor_reduce(prob[:, 0:384].rearrange("p (g k) -> p g k", g=3),
                                                   bank[4][:, 0:384].rearrange("p (g k) -> p g k", g=3),
                                                   bias[:, h % 2, :, P:2 * P], 1.0, -3e38, ALU.add, ALU.max,
                                                   mx[:, 0:1]).then_inc(s["att_m"], 1)
                    dve.wait_ge(s["att_m"], J + 1)
                    nc.vector.tensor_scalar(small[:, 26:27], mx[:, 0:1], -1.0, None, ALU.mult
                                            ).then_inc(s["att_nm"], 1)

            def att_normalise(J):
                w = 768 if J % 2 == 0 else 384
                dve.wait_ge(s["att_p"], J + 1)
                nc.vector.reciprocal(small[:, 28:29], small[:, 27:28]).then_inc(s["att_rs"], 1)
                dve.wait_ge(s["att_rs"], J + 1)
                nc.vector.tensor_scalar(prob[:, 0:w], prob[:, 0:w], small[:, 28:29], None, ALU.mult
                                        ).then_inc(s["att_pn"], 1)

            def att_out(J):
                h, qt = J // 2, 1 - J % 2
                dve.wait_ge(s["ot_hi"], J + 1)
                cut = slice(qt * P, (qt + 1) * P)
                nc.vector.tensor_tensor(oT_lo[:, h, cut], bank[7][:, P - 1::-1], fp(oT_hi[:, h, cut]), ALU.subtract
                                        ).then_inc(s["ot_ev"], 1)

            def qkv_extra(m):
                pr, j = divmod(m, QU)
                J = 4 * (pr - 1) + j // 2
                if pr >= 1 and j % 2 == 0 and j > 0:
                    att_out(J - 1)
                if pr >= 1 and j % 2 == 0 and j < 8:
                    att_max(J)
                if m < 4 * KC:
                    ada_op(2 * KC + m)
                if pr >= 1 and j % 2 == 0 and j < 8:
                    att_normalise(J)
                if pr < PAIRS:
                    if j in (1, 3, 5):
                        qk_reduce(3 * pr + j // 2)
                    if j in (2, 4, 6):
                        qk_normalise(3 * pr + j // 2 - 1)

            for m in range(PURE):
                split_unit(m + AHEAD)
                qkv_extra(m)
                for r in tasks_at(m):
                    ada_evac(r)
            for v in range(QU):
                if v < 3:
                    split_unit(M_OUT0 + v + AHEAD)
                qkv_extra(PURE + v)
            split_unit(M_OUT0 + 3 + AHEAD)
            residual(0, M_OUT0 + 3)

            def ffn(f, base):
                q = 2 * f + 1
                norm_scale(q)
                norm_affine(q)
                for r in range(3 * NF):
                    kind, j = ffn_step(r)
                    split_unit(base + r + AHEAD)
                    if kind == 1:
                        n = NF * f + j
                        dve.wait_ge(s["f_sil"], n + 1)
                        if n:
                            dve.wait_ge(s["f_tr"], n)
                        for t in range(T):
                            i = nc.vector.tensor_tensor(hid[:, t], bank[4 + t][:, FC:2 * FC], sil[:, t], ALU.mult)
                        i.then_inc(s["f_hid"], 1)
                    jt = 0 if r == 1 else j + 1 if kind == 2 and j < NF - 1 else None
                    if jt is not None:
                        n = NF * f + jt
                        dve.wait_ge(s["f_hi"], n + 1)
                        nc.vector.tensor_tensor(hidT(oT_lo, n), bank[6][:].rearrange("p (k t) -> p k t", k=2),
                                                fp(hidT(oT_hi, n)), ALU.subtract).then_inc(s["f_lo"], 1)
                    if f == 0:
                        for n in range(3 * r // 2, min(3 * (r + 1) // 2, ADA_BLOCKS * KC)):
                            ada_op(ADA_BLOCKS * KC + n)
                        for task in tasks_at(M_FFN0 + r):
                            ada_evac(task)
                residual(q, base + 3 * NF - 1)

            ffn(0, M_FFN0)
            norm_scale(2)
            norm_affine(2)
            nc.vector.memset(Am, 0.0).then_inc(s["r_zero"], 1)
            dve.wait_ge(s["r_zero"], 1)

            def rec_gates(half):
                dve.wait_ge(s["r_tev"], 2 * half + 2)
                dve.wait_ge(s["lbd_s"], 2)
                for h in range(4):
                    c = 4 * half + h
                    cut = slice(h * SEQ, (h + 1) * SEQ)
                    i = nc.vector.tensor_scalar(rE[:, 0, cut], rk[:, cut], lb[:, 1, c:c + 1], lb[:, 0, c:c + 1],
                                                ALU.mult, ALU.add)
                i.then_inc(s["r_fg"], 1)
                dve.wait_ge(s["r_fg"], half + 1)
                nc.vector.tensor_scalar(rk, rE[:, 0], -1.0, 1.0, ALU.mult, ALU.add).then_inc(s["r_k"], 1)
                dve.wait_ge(s["r_ln"], half + 1)
                for h in range(4):
                    for t in range(T):
                        cut = slice(h * SEQ + t * P, h * SEQ + (t + 1) * P)
                        i = nc.vector.tensor_tensor_scan(rE[:, 1, cut], rG[:, cut], rG[:, cut], 0.0, ALU.add,
                                                         ALU.bypass)
                i.then_inc(s["r_G"], 1)
                dve.wait_ge(s["r_G"], 2 * half + 1)
                nc.vector.tensor_copy(rG, rE[:, 1]).then_inc(s["r_G"], 1)
                dve.wait_ge(s["r_G"], 2 * half + 2)

            def rec_diff(half, level):
                E = rE[:, level % 2]
                if level < LEVELS:
                    h = gh(level)
                    v = lambda y: y.rearrange("p (b two h) -> p b two h", two=2, h=h)
                    G = v(rG)
                    mid = G[:, :, 0, h - 1:h].to_broadcast([P, 1024 // (2 * h), h])
                    nc.vector.tensor_tensor(v(E)[:, :, 0, :], mid, G[:, :, 0, :], ALU.subtract)
                    i = nc.vector.tensor_tensor(v(E)[:, :, 1, :], G[:, :, 1, :], mid, ALU.subtract)
                else:
                    v = lambda y: y.rearrange("p (h t n) -> p h t n", t=2, n=P)
                    G = v(rG)
                    end = G[:, :, 0, P - 1:P].to_broadcast([P, 4, P])
                    nc.vector.tensor_tensor(v(E)[:, :, 0, :], end, G[:, :, 0, :], ALU.subtract)
                    i = nc.vector.tensor_copy(v(E)[:, :, 1, :], G[:, :, 1, :])
                i.then_inc(s["r_D"], 1)

            def rec_scale(half, level):
                n = (LEVELS + 1) * half + level
                if level == 0:
                    dve.wait_ge(s["r_k"], half + 1)
                    return
                dve.wait_ge(s["r_E"], LEVELS * half + level)
                if n >= 2:
                    dve.wait_ge(s["r_mm"], n - 1)
                h = gh(level)
                v = lambda y: y.rearrange("p (b two h) -> p b two h", two=2, h=h)
                E = v(rE[:, level % 2])
                Z = v(rZ[:, level % 2])
                nc.vector.tensor_tensor(Z[:, :, 0, :], v(rk)[:, :, 0, :], E[:, :, 0, :], ALU.mult)
                nc.vector.tensor_tensor(Z[:, :, 1, :], v(rq)[:, :, 1, :], E[:, :, 1, :], ALU.mult
                                        ).then_inc(s["r_q"], 1)

            def rec_take(half, level):
                n = (LEVELS + 1) * half + level
                dve.wait_ge(s["r_mm"], n + 1)
                if level == LEVELS:
                    return
                if half and level == 0:
                    dve.wait_ge(s["r_o"], 2)
                for t in range(T):
                    m = masks[:, level, :].rearrange("p (o t) -> p o t", o=1).to_broadcast([P, 4, P])
                    i = nc.vector.copy_predicated(Am[:, t].rearrange("p (h t) -> p h t", h=4), m,
                                                  bank[4 + t][:].rearrange("p (h t) -> p h t", h=4))
                i.then_inc(s["r_A"], 1)

            def rec_norm(half, t):
                n = 2 * half + t
                dve.wait_ge(s["r_osq"], n + 1)
                nc.vector.tensor_reduce(small[:, 32 + 8 * t + 4 * half:36 + 8 * t + 4 * half],
                                        sq[:, t].rearrange("p (h d) -> p h d", d=P), AX_X, ALU.add
                                        ).then_inc(s["r_ored"], 1)

            dve.wait_ge(s["masks_in"], 16)
            for step in range(17):
                if step < 16:
                    split_unit(M_IN + step + AHEAD)
                    if step == 9:
                        for t in range(T):
                            rec_norm(0, t)
                    if step in (4, 10):
                        rec_gates(step // 10)
                        rec_diff(step // 10, 1)
                for half, level in levels_at(step):
                    rec_scale(half, level)
                    if 1 <= level < LEVELS:
                        rec_diff(half, level + 1)
                    rec_take(half, level)
            for t in range(T):
                rec_norm(1, t)
            dve.wait_ge(s["r_orstd"], 1)
            dve.wait_ge(s["r_nat"], 8)
            dve.wait_ge(s["r_oev"], 4)
            for t in range(T):
                v = lambda y: y.rearrange("p (h d) -> p h d", d=P)
                r = small[:, 48 + 8 * t:56 + 8 * t].rearrange("p (h o) -> p h o", o=1).to_broadcast([P, HEADS, P])
                nc.vector.tensor_tensor(v(rV[:, t]), v(rV[:, t]), r, ALU.mult).then_inc(s["r_sg"], 1)
                dve.wait_ge(s["r_sg"], t + 1)
                nc.vector.tensor_tensor(rV[:, t], rV[:, t], gates[:, t], ALU.mult).then_inc(s["r_on"], 1)
            for n in range(4):
                t, g = divmod(n, 2)
                dve.wait_ge(s["r_otr"], n + 1)
                nc.vector.tensor_scalar(hT4(n), bank[4 + g][:].rearrange("p (h t) -> p h t", h=4),
                                        cols[:, GNORM0:GNORM0 + 1], None, ALU.mult).then_inc(s["r_gn"], 1)
                dve.wait_ge(s["r_ohi"], n + 1)
                nc.vector.tensor_tensor(oT_lo[:, 4 * g:4 * g + 4, t * P:(t + 1) * P], hT4(n),
                                        fp(oT_hi[:, 4 * g:4 * g + 4, t * P:(t + 1) * P]), ALU.subtract
                                        ).then_inc(s["r_olo"], 1)
            for v in range(4):
                split_unit(M_OUT1 + v + AHEAD)
            residual(2, M_OUT1 + 3)
            ffn(1, M_FFN1)


ROWS = [("c", 0, 8), ("norm_mix", 8, 16), ("norm_ffn", 24, 16), ("attn_q_gain", 40, 3), ("attn_k_gain", 43, 3),
        ("hgrn_lower_bounds", 46, 16), ("hgrn_gnorm", 62, 1)]
ROW_AP = {"c": "a (k d) -> (a k) d", "norm_mix": "a (k d) -> (a k) d", "norm_ffn": "a (k d) -> (a k) d",
          "attn_q_gain": "a g d -> (a g) d", "attn_k_gain": "a g d -> (a g) d",
          "hgrn_lower_bounds": "a (k d) -> (a k) d", "hgrn_gnorm": "a d -> a d"}
ROW_AP = {k: v for k, v in ROW_AP.items()}
NROWS = 63
NORM0, GAIN0, LB0, GNORM0 = 8, 40, 46, 62

TASKS = [(blk, kind, c0) for blk in range(2 * ADA_BLOCKS)
         for kind, c0 in ([("row", 0), ("row", 512)] if blk % ADA_BLOCKS in (2, 5) else [(KC, 0)])]


def tasks_until(block):
    return sum(1 for t in TASKS if t[0] <= block)


def tasks_at(m):
    late = {6: [8], 11: [9], 16: [10], 17: [11], 22: [12], 27: [13], 32: [14, 15]}
    return {9: [2], 10: [3], 18: [4], 26: [5], 33: [6], 34: [7]}.get(m, []) + late.get(m - M_FFN0, [])


def levels_at(step):
    if 5 <= step <= 8:
        return [(0, level) for level in ((0, 1), (2, 3), (4, 5, 6), (7, 8))[step - 5]]
    if 11 <= step <= 15:
        return [(1, level) for level in ((0, 1), (2,), (3, 4), (5,), (6, 7))[step - 11]]
    if step == 16:
        return [(1, 8)]
    return []


def base_of(n):
    f, j = divmod(n, NF)
    return (M_FFN0, M_FFN1)[f] + (3 * (j + 1) + 1 if j < NF - 1 else 3 * NF - 1)


_INS = ["x", "c", "rel_bias", "ada_w", "ada_b", "norm_mix", "norm_ffn", "attn_w_qkv", "attn_w_out", "attn_q_gain",
        "attn_k_gain", "hgrn_w_in", "hgrn_w_out", "hgrn_gnorm", "hgrn_lower_bounds", "ffn_w1", "ffn_w3", "ffn_w2"]


def kernel(**inputs):
    import numpy as _np
    import concourse.bacc as _bacc
    from concourse import mybir as _mybir
    from concourse.bass_utils import run_bass_kernel_spmd as _run

    nc = _bacc.Bacc("TRN2", target_bir_lowering=False, num_devices=1)
    data = {name: _np.ascontiguousarray(inputs[name]) for name in _INS}
    data |= {"distance_table": distance_table(), "mask_rows": mask_rows(), "tree_masks": tree_masks()}
    arrays, args = {}, {}
    for name, v in data.items():
        arrays[f"in_{name}_dram"] = v
        args[name] = nc.dram_tensor(f"in_{name}_dram", v.shape, _mybir.dt.from_np(v.dtype), kind="ExternalInput").ap()
    out = nc.dram_tensor("out_0_dram", (1, SEQ, D), F32, kind="ExternalOutput").ap()
    hybrid_trunk(nc, args, out)
    r = _run(nc, [arrays], core_ids=[0])
    return r.results[0]["out_0_dram"]
```

```python
from contextlib import ExitStack

import numpy as np
import concourse.bass as bass
from concourse import mybir

ALU = mybir.AluOpType
ACT = mybir.ActivationFunctionType
AX_X = mybir.AxisListType.X
F32 = mybir.dt.float32
F32R = mybir.dt.float32r
I32 = mybir.dt.int32

P = 128
SEQ = 256
D = 1024
KC = D // P
T = SEQ // P
HEADS = 8
GROUPS = ((128, 1), (512, 4), (2048, 16))
NG = len(GROUPS)
BUCKETS = 32
MAX_DISTANCE = 2048
F = ((8 * D // 3 + 255) // 256) * 256
FC = 256
NF = F // FC
EPS = 1e-6
MASKED = -1e30
UNIT = 2048
RAW = 3
SPL = 3
AHEAD = 2
PAIRS = HEADS // 2
QU = 9
ADA_COLS = D
FIRST = 8
ADA_RING = 2
ADA_BLOCKS = 6 * D // ADA_COLS
LEVELS = 8
PRODUCTS = LEVELS + 2

M_OUT0 = PAIRS * QU
M_FFN0 = M_OUT0 + 4
M_IN = M_FFN0 + 3 * NF
M_OUT1 = M_IN + 16
M_FFN1 = M_OUT1 + 4
UNITS = M_FFN1 + 3 * NF


def distance_table():
    table = np.zeros((NG * BUCKETS + NG, 2 * P + P - 1), np.float32)
    exact = BUCKETS // 2
    for g, (window, dil) in enumerate(GROUPS):
        for i in range(table.shape[1]):
            dist = 2 * P - 1 - i
            if dist < 0 or dist > window or dist % dil:
                table[NG * BUCKETS + g, i] = 1.0
                continue
            large = exact + int(np.log(max(dist, 1) / exact) / np.log(MAX_DISTANCE / exact) * (BUCKETS - exact))
            table[g * BUCKETS + (dist if dist < exact else min(large, BUCKETS - 1)), i] = 1.0
    return table


def mask_rows():
    rows = np.zeros((NG, NG * HEADS), np.float32)
    for g in range(NG):
        rows[g, g * HEADS:(g + 1) * HEADS] = MASKED
    return rows


def pair_masks():
    masks = np.zeros((P, PRODUCTS - 1, P // 2), np.int32)
    s = np.arange(P)[:, None]
    for product in range(PRODUCTS - 1):
        if product < 2:
            masks[:, product] = s == product + 2 * np.arange(P // 2)[None, :]
            continue
        h = 1 << (product - 2)
        t = np.arange(P).reshape(-1, 2, h)[:, 1].reshape(1, -1)
        masks[:, product] = (s // (2 * h) == t // (2 * h)) & (s % (2 * h) < h)
    return masks


def gh(level):
    return 1 << (level - 1)


def hybrid_trunk(nc, a, out):
    TABLE = 2 * P + P - 1
    GH = NG * HEADS
    with ExitStack() as ctx:
        def sb(name, shape, dt=F32):
            return ctx.enter_context(nc.sbuf_tensor(name, shape, dt))

        def sem(name):
            return ctx.enter_context(nc.semaphore(name))

        bank = [ctx.enter_context(nc.psum_tensor(f"bank{i}", [P, 512], F32)) for i in range(8)]

        raw = sb("raw", [P, RAW, UNIT])
        whi = sb("whi", [P, SPL, UNIT], F32R)
        wlo = sb("wlo", [P, SPL, UNIT], F32R)
        ada_w = sb("ada_w", [P, ADA_RING, ADA_COLS])
        acc = sb("acc", [P, 2, ADA_COLS])
        x = sb("x", [P, T, D])
        hT_hi = sb("hT_hi", [P, KC, SEQ], F32R)
        hT_lo = sb("hT_lo", [P, KC, SEQ], F32R)
        oT_hi = sb("oT_hi", [P, KC, SEQ], F32R)
        oT_lo = sb("oT_lo", [P, KC, SEQ], F32R)
        gate = sb("gate", [P, 2, D])
        ident = sb("ident", [P, P])
        ones = sb("ones", [P, P])
        rows = sb("rows", [64, P])
        cols = sb("cols", [P, 64])
        cact = sb("cact", [P, KC])
        mod_a = sb("mod_a", [P, 2, 2, KC])
        mod_b = sb("mod_b", [P, 2, 2, KC])
        lb = sb("lb", [P, 2, KC])
        lbd = sb("lbd", [P, KC])
        small = sb("small", [P, 64])
        eps = sb("eps", [P, 1])
        late_gate = sb("late_gate", [P, D])
        arena = sb("arena", [P, 14336])

        def part(at, shape):
            v = arena[:, at:at + int(np.prod(shape))]
            if len(shape) > 1:
                names = "abcd"[:len(shape)]
                v = v.rearrange(f"p ({' '.join(names)}) -> p {' '.join(names)}",
                                **{k: n for k, n in zip(names, shape)})
            return v

        hT = part(0, [KC, SEQ])
        xn = part(3072, [T, D])
        first_w = [part(at, [ADA_COLS]) for at in (0, 1024, 2048, 5120, 6144, 7168, 8192, 11264)]
        qT = part(0, [2, NG, 2 * SEQ])
        kT = part(3072, [2, NG, 2 * SEQ])
        vN = part(6144, [2, T, NG * 2 * P])
        qkn = part(9216, [2, T * 512])
        prob = part(11264, [768])
        probT = part(12032, [768])
        bias = part(12800, [2, NG, SEQ])
        rel3 = qkn[0:NG * BUCKETS + NG, 0, 0:GH]
        tabw = qkn[0:NG * BUCKETS + NG, 0, 64:64 + TABLE]
        tabT = qkn[0:GH, 0, 512:512 + TABLE]
        sil = part(6144, [T, FC])
        hid = part(6656, [T, FC])
        rq = [part(0, [1024]), ada_w[:, 0]]
        rk = [part(1024, [1024]), acc[:, 0]]
        rG = [part(2048, [1024]), acc[:, 1]]
        forget, logf = part(3072, [1024]), part(4096, [1024])
        gates = xn
        nat = part(5120, [T, 512])
        rE = part(6144, [2, 1024])
        rZ = part(8192, [2, 1024])
        rV = part(10240, [T, 1024])
        Am = part(12288, [3, 512])
        sq = sb("sq", [P, T, 512])
        masks = sb("masks", [P, PRODUCTS - 1, P // 2], I32)

        def hidT(v, n):
            return v[:, 2 * (n % 2):2 * (n % 2) + 2, :]

        scratch = nc.dram_tensor("bias_rows", (GH, TABLE), F32, kind="Internal").ap()

        raw_in = [sem(f"raw_in{i}") for i in range(RAW)]
        ada_in = [sem(f"ada_in{i}") for i in range(ADA_RING)]
        first_in = [sem(f"first_in{i}") for i in range(FIRST)]
        bias_in = [sem(f"bias_in{i}") for i in range(2)]
        names = """x_in rows_in masks_in rel_in tab_out out_done
            rounded split pe_unit
            pool_setup pool_chain
            cols_t cols_s cact_s lbd_s lb_s
            ada_used ada_red ada_ev adab_in0 adab_in1 ada_zero
            tab_mm tab_cp
            xn_ssq xn_ln xn_rstd xn_s xn_tr xn_aff xn_hi xn_lo res
            qk_sq qk_red qk_ln qk_rstd qk_norm qk_tr qk_tev v_ev
            att_s att_m att_nm att_p att_rs att_pn att_tr pt_ev att_pv ot_hi ot_ev
            f_sil f_hid f_tr f_hi f_lo
            yres_t y_first newton
            r_nat r_tr r_tev r_fg r_k r_ln r_G r_D r_E r_q r_mm r_A r_zero r_X r_o r_oev r_osq r_ored r_oln r_orstd
            r_on r_otr r_ohi r_olo""".split()
        s = {n: sem(n) for n in names}

        block = ctx.enter_context(nc.Block())

        def cols_of(w, c0, n, k0, nk):
            return w.rearrange("(k p) n -> p k n", p=P)[:, k0:k0 + nk, c0:c0 + n]

        def pieces(m):
            if m < M_OUT0:
                pr, j = divmod(m, QU)
                w = a["attn_w_qkv"][0]
                col = lambda g, which: (3 * g + which) * D + pr * 256
                if j == 8:
                    return [(cols_of(w, col(2, 2), 256, 0, 8), 8, 0, 256)]
                k0 = 4 * (j % 2)
                left, right = ((j // 2, 0), (j // 2, 1)) if j < 6 else ((0, 2), (1, 2))
                return [(cols_of(w, col(*left), 256, k0, 4), 4, 0, 256), (cols_of(w, col(*right), 256, k0, 4), 4, 256, 256)]
            if M_IN <= m < M_OUT1:
                c, j = divmod(m - M_IN, 2)
                first = [1024, 0, 2048, 1536, 512, 2560, 3072, 3584][c]
                return [(cols_of(a["hgrn_w_in"][0], first, 512, 4 * j, 4), 4, 0, 512)]
            for base, w in ((M_OUT0, a["attn_w_out"][0]), (M_OUT1, a["hgrn_w_out"][0])):
                if base <= m < base + 4:
                    return [(cols_of(w, 0, 1024, 2 * (m - base), 2), 2, 0, 1024)]
            layer, r = (0, m - M_FFN0) if m < M_IN else (1, m - M_FFN1)
            kind, j = ffn_step(r)
            if kind == 2:
                return [(cols_of(a["ffn_w2"][layer], 0, 1024, 2 * j, 2), 2, 0, 1024)]
            return [(cols_of(a["ffn_w1"][layer], j * FC, FC, 4 * kind, 4), 4, 0, FC),
                    (cols_of(a["ffn_w3"][layer], j * FC, FC, 4 * kind, 4), 4, FC, FC)]

        def ffn_step(r):
            if r < 2:
                return r, 0
            if r == 3 * NF - 1:
                return 2, NF - 1
            j, k = divmod(r + 1, 3)
            return (k, j) if k < 2 else (2, j - 1)

        need, came = [], [0] * RAW
        for m in range(UNITS):
            came[m % RAW] += 16 * len(pieces(m))
            need.append(came[m % RAW])

        def load_bias(sp, h):
            if h >= 2:
                sp.wait_ge(s["att_nm"], 2 * (h - 1))
            skewed = bass.AP(scratch.tensor, h * TABLE, [[1, P], [HEADS * TABLE, NG], [1, SEQ]])
            sp.dma_start(bias[:, h % 2], skewed).then_inc(bias_in[h % 2], 16)

        @block.sync
        def _(sp):
            sp.dma_start(x[:], a["x"][0].rearrange("(t p) d -> p t d", p=P)).then_inc(s["x_in"], 16)
            for n, (name, r0, nr) in enumerate(ROWS):
                src = a[name].rearrange(ROW_AP[name], d=P)
                sp.dma_start(rows[r0:r0 + nr, :], src).then_inc(s["rows_in"], 16)
            for g in range(NG):
                sp.wait_ge(s["pool_setup"], 4)
                sp.dma_start(rel3[g * BUCKETS:(g + 1) * BUCKETS, g * HEADS:(g + 1) * HEADS],
                             a["rel_bias"][:, g * HEADS:(g + 1) * HEADS]).then_inc(s["rel_in"], 16)
            sp.dma_start(rel3[NG * BUCKETS:, :], a["mask_rows"]).then_inc(s["rel_in"], 16)
            sp.dma_start(tabw, a["distance_table"]).then_inc(s["rel_in"], 16)
            for m in range(UNITS):
                if m == 0:
                    sp.wait_ge(s["ada_used"], KC)
                if m >= RAW:
                    sp.wait_ge(s["split"], m - RAW + 1)
                for src, nk, c0, n in pieces(m):
                    slot = raw[:, m % RAW, :].rearrange("p (k n) -> p k n", k=nk)
                    sp.dma_start(slot[:, :, c0:c0 + n], src).then_inc(raw_in[m % RAW], 16)
                if m == 2:
                    sp.dma_start(masks[:], a["pair_masks"]).then_inc(s["masks_in"], 16)
                    sp.wait_ge(s["tab_cp"], 1)
                    sp.dma_start(scratch, tabT).then_inc(s["tab_out"], 16)
                    sp.wait_ge(s["tab_out"], 16)
                    load_bias(sp, 0)
                    load_bias(sp, 1)
                for h in range(2, HEADS):
                    if m == QU * (h // 2 + 1) + 4 * (h % 2):
                        load_bias(sp, h)
            for t in range(T):
                sp.wait_ge(s["res"], 4 * 3 + 2 * (t + 1))
                sp.dma_start(out[0, t * P:(t + 1) * P, :], x[:, t]).then_inc(s["out_done"], 16)
            sp.wait_ge(s["out_done"], 16 * T)

        @block.gpsimd
        def _(pool):
            pool.memset(ident[:], 0.0).then_inc(s["pool_setup"], 1)
            pool.memset(ones[:], 1.0).then_inc(s["pool_setup"], 1)
            pool.memset(eps[:], EPS).then_inc(s["pool_setup"], 1)
            pool.memset(rel3, 0.0).then_inc(s["pool_setup"], 1)
            pool.memset(acc[:], 0.0).then_inc(s["ada_zero"], 1)
            pool.wait_ge(s["pool_setup"], 1)
            pool.affine_select(out=ident[:], in_=ident[:], compare_op=ALU.not_equal, fill=1.0, base=0,
                               pattern=[[-1, P]], channel_multiplier=1).then_inc(s["pool_setup"], 1)
            for n in range(2 * ADA_BLOCKS * KC):
                layer, b, k = n // (ADA_BLOCKS * KC), n // KC % ADA_BLOCKS, n % KC
                if k == 0:
                    blk = ADA_BLOCKS * layer + b
                    if blk >= 2:
                        pool.wait_ge(s["ada_red"], tasks_until(blk - 2))
                        pool.memset(acc[:, blk % 2], 0.0).then_inc(s["ada_zero"], 1)
                    pool.wait_ge(s["ada_zero"], max(1, blk))
                    pool.dma_start(acc[0:1, blk % 2, :], a["ada_b"][layer:layer + 1, b * ADA_COLS:(b + 1) * ADA_COLS]
                                   ).then_inc(s[f"adab_in{blk % 2}"], 16)
                if n < 2 * KC:
                    if n >= FIRST:
                        pool.wait_ge(s["ada_used"], n - FIRST + 1)
                    pool.dma_start(first_w[n % FIRST], a["ada_w"][layer, k * P:(k + 1) * P, b * ADA_COLS:(b + 1) * ADA_COLS]
                                   ).then_inc(first_in[n % FIRST], 16)
                    continue
                if n >= 2 * KC + ADA_RING:
                    pool.wait_ge(s["ada_used"], n - ADA_RING + 1)
                pool.dma_start(ada_w[:, n % ADA_RING], a["ada_w"][layer, k * P:(k + 1) * P, b * ADA_COLS:(b + 1) * ADA_COLS]
                               ).then_inc(ada_in[n % ADA_RING], 16)

            def rec_diff(half, level):
                E, G = rE[:, level % 2], rG[half]
                pool.wait_ge(s["r_G"], half + 1)
                if LEVELS * half + level > 2:
                    pool.wait_ge(s["r_q"], LEVELS * half + level - 2)
                if level < LEVELS:
                    h = gh(level)
                    v = lambda y: y.rearrange("p (b two h) -> p b two h", two=2, h=h)
                    mid = v(G)[:, :, 0, h - 1:h].to_broadcast([P, 1024 // (2 * h), h])
                    pool.tensor_tensor(v(E)[:, :, 0, :], mid, v(G)[:, :, 0, :], ALU.subtract)
                    i = pool.tensor_tensor(v(E)[:, :, 1, :], v(G)[:, :, 1, :], mid, ALU.subtract)
                else:
                    v = lambda y: y.rearrange("p (h t n) -> p h t n", t=2, n=P)
                    end = v(G)[:, :, 0, P - 1:P].to_broadcast([P, 4, P])
                    pool.tensor_tensor(v(E)[:, :, 0, :], end, v(G)[:, :, 0, :], ALU.subtract)
                    i = pool.tensor_copy(v(E)[:, :, 1, :], v(G)[:, :, 1, :])
                i.then_inc(s["r_D"], 1)

            for half in range(2):
                for level in range(1, LEVELS + 1):
                    rec_diff(half, level)

        PURE = PAIRS * QU

        def chunk_end(n):
            pr, c = divmod(n, 5)
            return pr * QU + (2 * c + 2 if c < 4 else 9)

        def blocks_of(qt):
            return [(g, kt) for g in range(NG) for kt in range(qt + 1)]

        VSTEPS = 45 - M_OUT0

        @block.tensor
        def _(pe):
            def unit(m, lhs_hi, lhs_lo, nk, k0, n, dst, first, last, tiles=range(T), tile_done=None):
                sl = m % SPL
                w = [v[:, sl, :].rearrange("p (k n) -> p k n", k=nk) for v in (whi, wlo)]
                pe.wait_ge(s["split"], m + 1)
                for t in tiles:
                    for k in range(nk):
                        hi = lhs_hi[:, k0 + k, t * P:(t + 1) * P]
                        lo = lhs_lo[:, k0 + k, t * P:(t + 1) * P]
                        for c, d in enumerate(dst[t]):
                            cut = slice(c * 512, c * 512 + n)
                            for q, (l, r) in enumerate(((hi, w[0]), (hi, w[1]), (lo, w[0]))):
                                mm = nc.tensor.matmul(d[:, 0:n], l, r[:, k, cut],
                                                      start=first and k == 0 and q == 0,
                                                      stop=last and k == nk - 1 and q == 2)
                    if t == 0 and tile_done is not None:
                        mm.then_inc(s[tile_done], 1)
                if t == T - 1:
                    mm.then_inc(s["pe_unit"], 1)

            def norm_t(q, t):
                pe.wait_ge(s["xn_s"], 2 * q + t + 1)
                for g in range(2):
                    for k in range(4):
                        c = (4 * g + k) * P
                        mm = nc.tensor.transpose(bank[4 + 2 * t + g][:, k * P:(k + 1) * P], xn[:, t, c:c + P], ident[:])
                    mm.then_inc(s["xn_tr"], 1)

            def first_units(q, m, dst):
                for t in range(T):
                    pe.wait_ge(s["xn_lo"], 4 * q + 2 * t + 2)
                    for j in range(2):
                        unit(m + j, hT_hi, hT_lo, 4, 4 * j, 512, dst, j == 0, j == 1, tiles=(t,))

            pv = [0, 0]

            def reduce_task(r, b=7):
                blk, kind, half = TASKS[r]
                pe.wait_ge(s["ada_used"], KC * (blk + 1))
                if r:
                    pe.wait_ge(s["ada_ev"], r)
                if pv[0]:
                    pe.wait_ge(s["ot_ev"], pv[0])
                pv[1] = r + 1
                src = acc[:, blk % 2, :]
                if kind == "row":
                    mm = nc.tensor.matmul(bank[b][:], ones[:], src[:, half:half + 512], start=True, stop=True)
                else:
                    for j in range(kind):
                        mm = nc.tensor.matmul(bank[b][:, j:j + 1], src[:, half + j * P:half + (j + 1) * P],
                                              ones[:, 0:1], start=True, stop=True)
                mm.then_inc(s["ada_red"], 1)

            pe.wait_ge(s["rows_in"], 16 * len(ROWS))
            pe.wait_ge(s["pool_setup"], 5)
            nc.tensor.transpose(bank[0][:, 0:NROWS], rows[0:NROWS, :], ident[0:NROWS, 0:NROWS]).then_inc(s["cols_t"], 1)
            pe.wait_ge(s["rel_in"], 16 * 5)
            nc.tensor.matmul(bank[1][0:GH, 0:TABLE], rel3, tabw, start=True, stop=True).then_inc(s["tab_mm"], 1)
            for t in range(T):
                norm_t(0, t)
            pe.wait_ge(s["ada_used"], KC)
            for r in range(2):
                reduce_task(r, 3)
            pe.wait_ge(s["tab_cp"], 1)

            def qkv_unit(m):
                pr, j = divmod(m, QU)
                n = 5 * pr + min(j // 2, 4)
                if j % 2 == 0 and n >= 2:
                    c = (n - 2) % 5
                    if c < 3:
                        pe.wait_ge(s["qk_norm"], 3 * ((n - 2) // 5) + c + 1)
                    else:
                        pe.wait_ge(s["v_ev"], 2 * ((n - 2) // 5) + c - 2)
                b = 2 * (n % 2)
                nk, w = (8, 256) if j == 8 else (4, 512)
                unit(m, hT_hi, hT_lo, nk, 0 if j == 8 else 4 * (j % 2), w, [[bank[b]], [bank[b + 1]]],
                     j % 2 == 0, j % 2 == 1 or j == 8)

            def qk_transposes(n, which):
                pe.wait_ge(s["qk_norm"], n + 1)
                pe.wait_ge(s["qk_tev"], 2 * n + which)
                for h in range(2):
                    for t in range(T):
                        c = t * 512 + (2 * which + h) * P
                        mm = nc.tensor.transpose(bank[6][:, h * SEQ + t * P:h * SEQ + (t + 1) * P],
                                                 qkn[:, n % 2, c:c + P], ident[:])
                mm.then_inc(s["qk_tr"], 1)

            def att_scores(J):
                pr, hh, qt = J // 4, J // 2 % 2, 1 - J % 2
                pe.wait_ge(s["qk_tev"], 6 * (pr + 1))
                if J:
                    pe.wait_ge(s["pt_ev"], J)
                w = (qt + 1) * P
                for g in range(NG):
                    dst = bank[4][:, g * w:(g + 1) * w] if (g + 1) * w <= 512 else bank[5][:, 0:w]
                    base = hh * SEQ
                    mm = nc.tensor.matmul(dst, qT[:, pr % 2, g, base + qt * P:base + (qt + 1) * P],
                                          kT[:, pr % 2, g, base:base + w], start=True, stop=True)
                mm.then_inc(s["att_s"], 1)

            def att_transposes(J):
                qt = 1 - J % 2
                pe.wait_ge(s["att_pn"], J + 1)
                for i in range(len(blocks_of(qt))):
                    mm = nc.tensor.transpose(bank[4 + i // 4][:, i % 4 * P:(i % 4 + 1) * P],
                                             prob[:, i * P:(i + 1) * P], ident[:])
                mm.then_inc(s["att_tr"], 1)

            def att_values(J):
                pr, hh, qt = J // 4, J // 2 % 2, 1 - J % 2
                pe.wait_ge(s["pt_ev"], J + 1)
                pe.wait_ge(s["v_ev"], 2 * (pr + 1))
                if J:
                    pe.wait_ge(s["ot_ev"], J)
                pe.wait_ge(s["ada_ev"], pv[1])
                pv[0] = J + 1
                todo = blocks_of(qt)
                for i, (g, kt) in enumerate(todo):
                    c = g * 256 + hh * P
                    mm = nc.tensor.matmul(bank[7][:, 0:P], vN[:, pr % 2, kt, c:c + P], probT[:, i * P:(i + 1) * P],
                                          start=i == 0, stop=i == len(todo) - 1)
                mm.then_inc(s["att_pv"], 1)

            def qkv_extra(m):
                pr, j = divmod(m, QU)
                if pr >= 1:
                    J = 4 * (pr - 1) + j // 2
                    if j % 2 == 0 and j < 8:
                        att_scores(J)
                    if j % 2 == 0 and j > 0:
                        att_values(J - 1)
                    if j % 2 == 1:
                        att_transposes(J)
                if pr < PAIRS and 3 <= j <= 8:
                    qk_transposes(3 * pr + (j - 3) // 2, (j - 3) % 2)

            first_units(0, 0, [[bank[0]], [bank[1]]])
            for m in range(PURE):
                if m >= 2:
                    qkv_unit(m)
                qkv_extra(m)
                for r in tasks_at(m):
                    reduce_task(r)
            Y = [[bank[0], bank[1]], [bank[2], bank[3]]]
            for v in range(QU):
                if v < 3:
                    if v == 0:
                        pe.wait_ge(s["v_ev"], 2 * PAIRS)
                        pe.wait_ge(s["qk_norm"], 3 * PAIRS)
                    pe.wait_ge(s["ot_ev"], 4 * (v + 1))
                    unit(M_OUT0 + v, oT_hi, oT_lo, 2, 2 * v, 512, Y, v == 0, False)
                qkv_extra(PURE + v)
            pe.wait_ge(s["ot_ev"], 16)
            unit(M_OUT0 + 3, oT_hi, oT_lo, 2, 6, 512, Y, False, True, tile_done="y_first")

            def ffn(f, base):
                q = 2 * f + 1
                pe.wait_ge(s["ada_ev"], 8)
                for t in range(T):
                    norm_t(q, t)
                first_units(q, base, [[bank[4]], [bank[5]]])
                for r in range(3 * NF):
                    kind, j = ffn_step(r)
                    n = NF * f + j
                    if kind < 2 and j == 0:
                        pass
                    elif kind < 2:
                        if kind == 0:
                            pe.wait_ge(s["f_hid"], n)
                        unit(base + r, hT_hi, hT_lo, 4, 4 * kind, 512, [[bank[4]], [bank[5]]], kind == 0, kind == 1)
                    else:
                        pe.wait_ge(s["f_lo"], n + 1)
                        unit(base + r, hidT(oT_hi, n), hidT(oT_lo, n), 2, 0, 512, Y, j == 0, j == NF - 1,
                             tile_done="y_first" if j == NF - 1 else None)
                    jt = 0 if r == 1 else j + 1 if kind == 2 and j < NF - 1 else None
                    if jt is not None:
                        n = NF * f + jt
                        pe.wait_ge(s["f_hid"], n + 1)
                        if n:
                            pe.wait_ge(s["f_lo"], n)
                        for k in range(2):
                            for t in range(T):
                                mm = nc.tensor.transpose(bank[6][:, k * SEQ + t * P:k * SEQ + (t + 1) * P],
                                                         hid[:, t, k * P:(k + 1) * P], ident[:])
                        mm.then_inc(s["f_tr"], 1)
                    if f == 0:
                        for task in tasks_at(M_FFN0 + r):
                            reduce_task(task)

            ffn(0, M_FFN0)

            for t in range(T):
                norm_t(2, t)

            def rec_transposes(n):
                pe.wait_ge(s["r_nat"], (1, 2, 4, 5)[n])
                if n:
                    pe.wait_ge(s["r_tev"], n)
                for h in range(4):
                    for t in range(T):
                        mm = nc.tensor.transpose(bank[6 + h // 2][:, h % 2 * SEQ + t * P:h % 2 * SEQ + (t + 1) * P],
                                                 nat[:, t, h * P:(h + 1) * P], ident[:])
                mm.then_inc(s["r_tr"], 1)

            def rec_product(half, o):
                level = o - 1
                dst = bank[4 + o % 2]
                if o < 2:
                    pe.wait_ge(s["r_tev"], 2 * half + 2)
                    pe.wait_ge(s["r_k"], half + 1)
                    q_, k_ = rq[half], rk[half]
                else:
                    pe.wait_ge(s["r_q"], LEVELS * half + level)
                    q_ = k_ = rZ[:, level % 2]
                if o == 1:
                    pe.wait_ge(s["r_X"], half) if half else None
                elif half or o:
                    pe.wait_ge(s["r_A"], (LEVELS + 1) * half + max(o - 1, 0))
                for h in range(4):
                    if level == LEVELS:
                        mm = nc.tensor.matmul(dst[:, h * P:(h + 1) * P], k_[:, h * SEQ:h * SEQ + P],
                                              q_[:, h * SEQ + P:(h + 1) * SEQ], start=True, stop=True)
                        continue
                    for t in range(T):
                        tok = slice(h * SEQ + t * P, h * SEQ + (t + 1) * P)
                        y = dst[:, (4 * t + h) * 64:(4 * t + h + 1) * 64]
                        if o < 2:
                            cols_t = q_[:, tok].rearrange("p (b two) -> p b two", two=2)[:, :, o]
                        else:
                            n = gh(level)
                            cols_t = q_[:, tok].rearrange("p (b two h) -> p b two h", two=2, h=n)[:, :, 1, :]
                            y = y.rearrange("p (b h) -> p b h", h=n)
                        mm = nc.tensor.matmul(y, k_[:, tok], cols_t, start=True, stop=True)
                mm.then_inc(s["r_mm"], 1)

            def rec_values(half, t):
                pe.wait_ge(s["r_A"], (LEVELS + 1) * (half + 1))
                pe.wait_ge(s["r_X"], half + 1)
                pe.wait_ge(s["r_nat"], 6 if half else 3)
                if half:
                    pe.wait_ge(s["r_olo"], 2)
                else:
                    pe.wait_ge(s["r_tev"], 4)
                for h in range(4):
                    c = slice(h * P, (h + 1) * P)
                    v = slice(half * 512 + h * P, half * 512 + (h + 1) * P)
                    mm = nc.tensor.matmul(bank[6 + t][:, c], Am[:, t, c], rV[:, t, v], start=True, stop=t == 0)
                    if t:
                        mm = nc.tensor.matmul(bank[6 + t][:, c], Am[:, 2, c], rV[:, 0, v], start=False, stop=True)
                mm.then_inc(s["r_o"], 1)

            def rec_out_transposes(half, t):
                pe.wait_ge(s["r_on"], 2 * half + t + 1)
                for h in range(4):
                    mm = nc.tensor.transpose(bank[6 + t][:, h * P:(h + 1) * P],
                                             rV[:, t, (4 * half + h) * P:(4 * half + h + 1) * P], ident[:])
                mm.then_inc(s["r_otr"], 1)

            for step in range(16):
                c, j = divmod(step, 2)
                if j == 0 and c >= 2:
                    pe.wait_ge(s["r_nat"], c - 1)
                b = 2 * (c % 2)
                if c:
                    unit(M_IN + step, hT_hi, hT_lo, 4, 4 * j, 512, [[bank[b]], [bank[b + 1]]], j == 0, j == 1)
                elif j == 0:
                    first_units(2, M_IN, [[bank[0]], [bank[1]]])
                if step in TRANSPOSED:
                    rec_transposes(TRANSPOSED.index(step))
                if step == 11:
                    for t in range(T):
                        rec_values(0, t)
                for half, o in products_at(step):
                    rec_product(half, o)
                if step == 14:
                    for t in range(T):
                        rec_out_transposes(0, t)
            pe.wait_ge(s["r_nat"], 8)
            pe.wait_ge(s["r_olo"], 2)
            unit(M_OUT1, oT_hi, oT_lo, 2, 0, 512, Y, True, False)
            for t in range(T):
                rec_values(1, t)
            unit(M_OUT1 + 1, oT_hi, oT_lo, 2, 2, 512, Y, False, False)
            for t in range(T):
                rec_out_transposes(1, t)
            pe.wait_ge(s["r_olo"], 4)
            unit(M_OUT1 + 2, oT_hi, oT_lo, 2, 4, 512, Y, False, False)
            unit(M_OUT1 + 3, oT_hi, oT_lo, 2, 6, 512, Y, False, True, tile_done="y_first")
            ffn(1, M_FFN1)

        @block.scalar
        def _(act):
            count = {}

            def copy(dst, src):
                return nc.scalar.activation(dst, src, ACT.Copy)

            def round_unit(m):
                if m >= UNITS:
                    return
                act.wait_ge(raw_in[m % RAW], need[m])
                if m >= SPL:
                    act.wait_ge(s["pe_unit"], m - SPL + 1)
                copy(whi[:, m % SPL, :], raw[:, m % RAW, :]).then_inc(s["rounded"], 1)

            def rsqrt(dst, src, ln_sem, out_sem, n, scale):
                nc.scalar.activation(dst, src, ACT.Ln, bias=eps[:, 0:1], scale=scale).then_inc(s[ln_sem], 1)
                act.wait_ge(s[ln_sem], n + 1)
                nc.scalar.activation(dst, dst, ACT.Exp, scale=-0.5).then_inc(s[out_sem], 1)

            def norm_stats(q):
                if q == 0:
                    act.wait_ge(s["x_in"], 16)
                    act.wait_ge(s["pool_setup"], 3)
                for t in range(T):
                    if q:
                        act.wait_ge(s["res"], 4 * (q - 1) + 2 * (t + 1))
                    if q or t:
                        act.wait_ge(s["xn_ssq"], 2 * q + t)
                    junk = part(2048, [D]) if q else sq[:, :, :].rearrange("p a b -> p (a b)")
                    nc.scalar.activation(junk, x[:, t], ACT.Square, accum_out=small[:, t:t + 1]
                                         ).then_inc(s["xn_ssq"], 1)
                    act.wait_ge(s["xn_ssq"], 2 * q + t + 1)
                    rsqrt(small[:, 2 + t:3 + t], small[:, t:t + 1], "xn_ln", "xn_rstd", 2 * q + t, 1.0 / D)

            def norm_round(q):
                for n in range(4):
                    t, g = divmod(n, 2)
                    cut = slice(t * P, (t + 1) * P)
                    act.wait_ge(s["xn_aff"], 4 * q + n + 1)
                    copy(hT_hi[:, 4 * g:4 * g + 4, cut], hT[:, 4 * g:4 * g + 4, cut]).then_inc(s["xn_hi"], 1)

            act.wait_ge(s["cols_s"], 1)
            nc.scalar.activation(cact[:], cols[:, 0:KC], ACT.Silu).then_inc(s["cact_s"], 1)
            act.wait_ge(s["lbd_s"], 1)
            nc.scalar.activation(lb[:, 0, :], lbd[:], ACT.Sigmoid).then_inc(s["lb_s"], 1)
            nc.scalar.preload_act_table_set("natural_log_exp_and_others")
            norm_stats(0)
            for m in range(AHEAD):
                round_unit(m)
            norm_round(0)

            def qk_square(n):
                act.wait_ge(s["pe_unit"], chunk_end(5 * (n // 3) + n % 3))
                if n:
                    act.wait_ge(s["qk_red"], n)
                b = 2 * ((5 * (n // 3) + n % 3) % 2)
                for t in range(T):
                    i = nc.scalar.activation(sq[:, t], bank[b + t][:], ACT.Square)
                i.then_inc(s["qk_sq"], 1)

            def qk_rsqrt(n):
                act.wait_ge(s["qk_red"], n + 1)
                if n:
                    act.wait_ge(s["qk_norm"], n)
                rsqrt(small[:, 16:24], small[:, 8:16], "qk_ln", "qk_rstd", n, 1.0 / P)

            def qk_evac(n, which):
                pr, g = divmod(n, 3)
                act.wait_ge(s["qk_tr"], 2 * n + which + 1)
                if pr >= 2:
                    act.wait_ge(s["att_s"], 4 * (pr - 1))
                view = lambda y: y.rearrange("p (b t) -> p b t", t=P)
                dst, src = view((qT, kT)[which][:, pr % 2, g, :]), view(bank[6][:])
                if which == 0:
                    src = src[:, :, ::-1]
                nc.scalar.activation(dst, src, ACT.Copy, scale=gains[:, which * NG + g:which * NG + g + 1]
                                     ).then_inc(s["qk_tev"], 1)

            def v_evac(pr, c):
                n = 5 * pr + 3 + c
                act.wait_ge(s["pe_unit"], chunk_end(n))
                if pr >= 2:
                    act.wait_ge(s["att_pv"], 4 * (pr - 1))
                b = 2 * (n % 2)
                for t in range(T):
                    i = copy(vN[:, pr % 2, t, 512:768], bank[b + t][:, 0:256]) if c else \
                        copy(vN[:, pr % 2, t, 0:512], bank[b + t][:])
                i.then_inc(s["v_ev"], 1)

            def att_exp(J):
                w = 768 if J % 2 == 0 else 384
                act.wait_ge(s["att_nm"], J + 1)
                nc.scalar.activation(prob[:, 0:w], prob[:, 0:w], ACT.Exp, bias=small[:, 26:27],
                                     accum_out=small[:, 27:28]).then_inc(s["att_p"], 1)

            def att_evac(J):
                act.wait_ge(s["att_tr"], J + 1)
                if J:
                    act.wait_ge(s["att_pv"], J)
                if J % 2 == 0:
                    copy(probT[:, 0:512], bank[4][:])
                    i = copy(probT[:, 512:768], bank[5][:, 0:256])
                else:
                    i = copy(probT[:, 0:384], bank[4][:, 0:384])
                i.then_inc(s["pt_ev"], 1)

            def att_out(J):
                h, qt = J // 2, 1 - J % 2
                act.wait_ge(s["att_pv"], J + 1)
                copy(oT_hi[:, h, qt * P:(qt + 1) * P], bank[7][:, P - 1::-1]).then_inc(s["ot_hi"], 1)

            def qkv_extra(m):
                pr, j = divmod(m, QU)
                if pr < PAIRS and j in (1, 3, 5):
                    qk_square(3 * pr + j // 2)
                if pr < PAIRS and j in (2, 4, 6):
                    qk_rsqrt(3 * pr + j // 2 - 1)
                if pr >= 1:
                    J = 4 * (pr - 1) + j // 2
                    if j % 2 == 0 and j > 0:
                        att_out(J - 1)
                    if j % 2 == 0 and j < 8:
                        att_exp(J)
                    if j % 2 == 1:
                        att_evac(J)
                if pr < PAIRS:
                    if 3 <= j <= 8:
                        qk_evac(3 * pr + (j - 3) // 2, (j - 3) % 2)
                    if j >= 7:
                        v_evac(pr, j - 7)

            gains = cols[:, GAIN0:GAIN0 + 2 * NG]
            act.wait_ge(s["cols_s"], 2)
            for m in range(PURE):
                round_unit(m + AHEAD)
                qkv_extra(m)
            for v in range(QU):
                if v < 4:
                    round_unit(M_OUT0 + v + AHEAD) if v < 3 else None
                qkv_extra(PURE + v)
            round_unit(M_OUT0 + 3 + AHEAD)

            def ffn(f, base):
                norm_stats(2 * f + 1)
                nc.scalar.preload_act_table(ACT.Silu)
                norm_round(2 * f + 1)
                for r in range(3 * NF):
                    kind, j = ffn_step(r)
                    round_unit(base + r + AHEAD)
                    if kind == 1:
                        n = NF * f + j
                        act.wait_ge(s["pe_unit"], base + r + 1)
                        if n:
                            act.wait_ge(s["f_hid"], n)
                        for t in range(T):
                            i = nc.scalar.activation(sil[:, t], bank[4 + t][:, 0:FC], ACT.Silu)
                        i.then_inc(s["f_sil"], 1)
                    jt = 0 if r == 1 else j + 1 if kind == 2 and j < NF - 1 else None
                    if jt is not None:
                        n = NF * f + jt
                        act.wait_ge(s["f_tr"], n + 1)
                        if n >= 2:
                            act.wait_ge(s["pe_unit"], base_of(n - 2) + 1)
                        copy(hidT(oT_hi, n), bank[6][:].rearrange("p (k t) -> p k t", k=2)).then_inc(s["f_hi"], 1)

            ffn(0, M_FFN0)
            nc.scalar.preload_act_table_set("natural_log_exp_and_others")
            norm_stats(2)
            norm_round(2)

            def rec_exp(half, level):
                n = LEVELS * half + level - 1
                act.wait_ge(s["r_D"], n + 1)
                nc.scalar.activation(rE[:, level % 2], rE[:, level % 2], ACT.Exp).then_inc(s["r_E"], 1)

            def rec_cross(half):
                act.wait_ge(s["r_mm"], PRODUCTS * (half + 1))
                if half:
                    act.wait_ge(s["r_o"], 2)
                copy(Am[:, 2], bank[5][:]).then_inc(s["r_X"], 1)

            def rec_out(half):
                for t in range(T):
                    act.wait_ge(s["r_o"], 2 * half + t + 1)
                    if half:
                        act.wait_ge(s["r_ored"], 2)
                    nc.scalar.activation(sq[:, t], bank[6 + t][:], ACT.Square).then_inc(s["r_osq"], 1)
                for t in range(T):
                    copy(rV[:, t, half * 512:(half + 1) * 512], bank[6 + t][:]).then_inc(s["r_oev"], 1)

            def rec_rsqrt(half):
                act.wait_ge(s["r_ored"], 2 * half + 2)
                c = 8 * half
                rsqrt(small[:, 48 + c:56 + c], small[:, 32 + c:40 + c], "r_oln", "r_orstd", half, 1.0 / P)

            def rec_out_round(half, t):
                act.wait_ge(s["r_otr"], 2 * half + t + 1)
                nc.scalar.activation(oT_hi[:, 4 * half:4 * half + 4, t * P:(t + 1) * P],
                                     bank[6 + t][:].rearrange("p (h t) -> p h t", t=P), ACT.Copy,
                                     scale=cols[:, GNORM0:GNORM0 + 1]).then_inc(s["r_ohi"], 1)

            def rec_transposed(n):
                half = n // 2
                act.wait_ge(s["r_tr"], n + 1)
                dst = rq[half] if n % 2 else rk[half]
                for g in range(2):
                    i = nc.scalar.activation(dst[:, g * 512:(g + 1) * 512], bank[6 + g][:],
                                             ACT.Silu if n % 2 else ACT.Sigmoid)
                i.then_inc(s["r_tev"], 1)
                nc.scalar.preload_act_table_set("natural_log_exp_and_others")

            def rec_log(half):
                act.wait_ge(s["r_fg"], half + 1)
                if half:
                    act.wait_ge(s["r_G"], half)
                nc.scalar.activation(logf, forget, ACT.Ln).then_inc(s["r_ln"], 1)

            def rec_chunk(c):
                act.wait_ge(s["pe_unit"], M_IN + 2 * c + 2)
                b = 2 * (c % 2)
                if c in (1, 3, 4):
                    act.wait_ge(s["r_tr"], {1: 1, 3: 2, 4: 3}[c])
                if c == 6:
                    act.wait_ge(s["r_G"], 2)
                for t in range(T):
                    src = bank[b + t][:]
                    if c in (2, 5):
                        h = c // 3
                        i = copy(rV[:, t, h * 512:(h + 1) * 512], src)
                    elif c < 6:
                        i = copy(nat[:, t], src)
                    else:
                        i = nc.scalar.activation(gates[:, t, (c - 6) * 512:(c - 5) * 512], src, ACT.Silu)
                i.then_inc(s["r_nat"], 1)
                if c >= 6:
                    nc.scalar.preload_act_table_set("natural_log_exp_and_others")

            for step in range(16):
                if step == 10:
                    rec_cross(0)
                if step - 1 in TRANSPOSED and step != 9:
                    rec_transposed(TRANSPOSED.index(step - 1))
                for half, o in products_at(step):
                    if o >= 2:
                        rec_exp(half, o - 1)
                round_unit(M_IN + step + AHEAD)
                if step == 9:
                    rec_transposed(2)
                if step in (3, 9):
                    rec_log(step // 9)
                if step == 12:
                    rec_out(0)
                if step == 13:
                    rec_rsqrt(0)
                if step == 15:
                    for t in range(T):
                        rec_out_round(0, t)
                if step % 2:
                    rec_chunk(step // 2)
            rec_cross(1)
            round_unit(M_OUT1 + AHEAD)
            round_unit(M_OUT1 + 1 + AHEAD)
            rec_out(1)
            rec_rsqrt(1)
            for t in range(T):
                rec_out_round(1, t)
            round_unit(M_OUT1 + 2 + AHEAD)
            round_unit(M_OUT1 + 3 + AHEAD)
            ffn(1, M_FFN1)

        @block.vector
        def _(dve):
            def fp(v):
                return v.bitcast(F32)

            def split_unit(m):
                if m >= UNITS:
                    return
                dve.wait_ge(s["rounded"], m + 1)
                nc.vector.tensor_tensor(wlo[:, m % SPL, :], raw[:, m % RAW, :], fp(whi[:, m % SPL, :]), ALU.subtract
                                        ).then_inc(s["split"], 1)

            def ada_op(n):
                blk, k = divmod(n, KC)
                if n < 2 * KC:
                    w = first_w[n % FIRST]
                    dve.wait_ge(first_in[n % FIRST], 16 * (n // FIRST + 1))
                else:
                    w = ada_w[:, n % ADA_RING]
                    dve.wait_ge(ada_in[n % ADA_RING], 16 * ((n - 2 * KC) // ADA_RING + 1))
                if k == 0:
                    dve.wait_ge(s[f"adab_in{blk % 2}"], 16 * (blk // 2 + 1))
                if n:
                    dve.wait_ge(s["ada_used"], n)
                nc.vector.scalar_tensor_tensor(out=acc[:, blk % 2], in0=w, scalar=cact[:, k:k + 1],
                                               in1=acc[:, blk % 2], op0=ALU.mult, op1=ALU.add
                                               ).then_inc(s["ada_used"], 1)

            def ada_evac(r, b=7):
                blk, kind, half = TASKS[r]
                layer = blk // ADA_BLOCKS
                dve.wait_ge(s["ada_red"], r + 1)
                src = bank[b][:, 0:KC]
                what = blk % ADA_BLOCKS
                if what in (2, 5):
                    dst = late_gate if (layer, what) == (1, 5) else gate[:, what // 5, :]
                    i = nc.vector.tensor_copy(dst[:, half:half + 512], bank[b][:])
                elif what in (0, 3):
                    i = nc.vector.tensor_copy(mod_b[:, layer, what // 3], src)
                else:
                    i = scale_gain(layer, what // 4, src)
                i.then_inc(s["ada_ev"], 1)

            def scale_gain(layer, sub, src):
                g = cols[:, NORM0 + (2 * sub + layer) * KC:NORM0 + (2 * sub + layer + 1) * KC]
                return nc.vector.scalar_tensor_tensor(out=mod_a[:, layer, sub], in0=src, scalar=1.0, in1=g,
                                                      op0=ALU.add, op1=ALU.mult)

            done = [0]

            def refine(y, ss, n, c, inv):
                v, w = small[:, c:c + n], small[:, c + n:c + 2 * n]
                nc.vector.tensor_scalar(v, ss, -0.5 * inv, -0.5 * EPS, ALU.mult, ALU.add)
                nc.vector.tensor_tensor(w, y, y, ALU.mult).then_inc(s["newton"], 1)
                dve.wait_ge(s["newton"], done[0] + 1)
                nc.vector.tensor_tensor(w, w, v, ALU.mult).then_inc(s["newton"], 1)
                dve.wait_ge(s["newton"], done[0] + 2)
                nc.vector.scalar_tensor_tensor(out=y, in0=w, scalar=1.5, in1=y, op0=ALU.add, op1=ALU.mult
                                               ).then_inc(s["newton"], 1)
                dve.wait_ge(s["newton"], done[0] + 3)
                done[0] += 3

            def norm_scale(q, t):
                dve.wait_ge(s["xn_rstd"], 2 * q + t + 1)
                refine(small[:, 2 + t:3 + t], small[:, t:t + 1], 1, 4 + 2 * t, 1.0 / D)
                nc.vector.tensor_scalar(xn[:, t], x[:, t], small[:, 2 + t:3 + t], None, ALU.mult
                                        ).then_inc(s["xn_s"], 1)

            def norm_affine(q, t, g):
                layer, sub = q // 2, q % 2
                dve.wait_ge(s["xn_tr"], 4 * q + 2 * t + g + 1)
                for k in range(4):
                    kc = 4 * g + k
                    i = nc.vector.tensor_scalar(hT[:, kc, t * P:(t + 1) * P], bank[4 + 2 * t + g][:, k * P:(k + 1) * P],
                                                mod_a[:, layer, sub, kc:kc + 1], mod_b[:, layer, sub, kc:kc + 1],
                                                ALU.mult, ALU.add)
                i.then_inc(s["xn_aff"], 1)

            def norm_rest(q, t):
                for g in range(2):
                    dve.wait_ge(s["xn_hi"], 4 * q + 2 * t + g + 1)
                    v = lambda y: y[:, 4 * g:4 * g + 4, t * P:(t + 1) * P]
                    nc.vector.tensor_tensor(v(hT_lo), v(hT), fp(v(hT_hi)), ALU.subtract).then_inc(s["xn_lo"], 1)

            def norm(q):
                norm_scale(q, 0)
                norm_affine(q, 0, 0)
                norm_affine(q, 0, 1)
                norm_scale(q, 1)
                norm_rest(q, 0)
                norm_affine(q, 1, 0)
                norm_affine(q, 1, 1)
                norm_rest(q, 1)

            def residual(q, last_unit):
                g = gate[:, 0, :] if q % 2 == 0 else (gate[:, 1, :] if q == 1 else late_gate)
                for b in range(4):
                    t, c = divmod(b, 2)
                    if b == 0:
                        dve.wait_ge(s["y_first"], q + 1)
                    if b == 2:
                        dve.wait_ge(s["pe_unit"], last_unit + 1)
                    cut = slice(c * 512, (c + 1) * 512)
                    n = 4 * q + b
                    if n >= 2:
                        dve.wait_ge(s["res"], n - 1)
                    nc.vector.tensor_tensor(sq[:, b % 2], bank[b][:], g[:, cut], ALU.mult).then_inc(s["yres_t"], 1)
                    dve.wait_ge(s["yres_t"], n + 1)
                    nc.vector.tensor_tensor(x[:, t, cut], x[:, t, cut], sq[:, b % 2], ALU.add).then_inc(s["res"], 1)

            dve.wait_ge(s["cols_t"], 1)
            nc.vector.tensor_copy(cols[:, 0:NROWS], bank[0][:, 0:NROWS]).then_inc(s["cols_s"], 1)
            dve.wait_ge(s["cols_s"], 1)
            nc.vector.tensor_scalar(cols[:, GAIN0:GAIN0 + NG], cols[:, GAIN0:GAIN0 + NG], float(P) ** -0.5, None,
                                    ALU.mult).then_inc(s["cols_s"], 1)
            nc.vector.tensor_tensor(lbd[:], cols[:, LB0 + KC:LB0 + 2 * KC], cols[:, LB0:LB0 + KC], ALU.subtract
                                    ).then_inc(s["lbd_s"], 1)
            dve.wait_ge(s["tab_mm"], 1)
            nc.vector.tensor_copy(tabT, bank[1][0:GH, 0:TABLE]).then_inc(s["tab_cp"], 1)
            dve.wait_ge(s["lb_s"], 1)
            nc.vector.tensor_scalar(lb[:, 1, :], lb[:, 0, :], -1.0, 1.0, ALU.mult, ALU.add).then_inc(s["lbd_s"], 1)
            dve.wait_ge(s["cact_s"], 1)
            dve.wait_ge(s["ada_zero"], 1)
            for t in range(T):
                norm_scale(0, t)
            for n in range(2 * KC):
                ada_op(n)
            for m in range(AHEAD):
                split_unit(m)
            for r in range(2):
                ada_evac(r, 3)
            dve.wait_ge(s["ada_ev"], 2)
            for t in range(T):
                norm_affine(0, t, 0)
                norm_affine(0, t, 1)
                norm_rest(0, t)

            def qk_reduce(n):
                dve.wait_ge(s["qk_sq"], n + 1)
                if n:
                    dve.wait_ge(s["qk_rstd"], n)
                nc.vector.tensor_reduce(small[:, 8:16], sq[:, :, :].rearrange("p t (h d) -> p (t h) d", d=P), AX_X,
                                        ALU.add).then_inc(s["qk_red"], 1)

            def qk_normalise(n):
                dve.wait_ge(s["qk_rstd"], n + 1)
                if n >= 2:
                    dve.wait_ge(s["qk_tr"], 2 * (n - 1))
                if n == 0:
                    dve.wait_ge(s["tab_out"], 16)
                refine(small[:, 16:24], small[:, 8:16], 8, 32, 1.0 / P)
                b = 2 * ((5 * (n // 3) + n % 3) % 2)
                for t in range(T):
                    r = small[:, 16 + 4 * t:20 + 4 * t].rearrange("p (h o) -> p h o", o=1).to_broadcast([P, 4, P])
                    i = nc.vector.tensor_tensor(qkn[:, n % 2, t * 512:(t + 1) * 512].rearrange("p (h d) -> p h d", d=P),
                                                bank[b + t][:].rearrange("p (h d) -> p h d", d=P), r, ALU.mult)
                i.then_inc(s["qk_norm"], 1)

            def att_max(J):
                h, qt = J // 2, 1 - J % 2
                dve.wait_ge(s["att_s"], J + 1)
                if J:
                    dve.wait_ge(s["att_tr"], J)
                dve.wait_ge(bias_in[h % 2], 16 * (h // 2 + 1))
                mx = small[:, 24:26]
                if qt:
                    nc.vector.tensor_tensor_reduce(prob[:, 0:512].rearrange("p (g k) -> p g k", g=2),
                                                   bank[4][:].rearrange("p (g k) -> p g k", g=2),
                                                   bias[:, h % 2, 0:2, :], 1.0, -3e38, ALU.add, ALU.max,
                                                   mx[:, 0:1])
                    nc.vector.tensor_tensor_reduce(prob[:, 512:768], bank[5][:, 0:256], bias[:, h % 2, 2, :], 1.0,
                                                   -3e38, ALU.add, ALU.max, mx[:, 1:2]).then_inc(s["att_m"], 1)
                    dve.wait_ge(s["att_m"], J + 1)
                    nc.vector.tensor_scalar(small[:, 26:27], mx[:, 0:1], mx[:, 1:2], -1.0, ALU.max, ALU.mult
                                            ).then_inc(s["att_nm"], 1)
                else:
                    nc.vector.tensor_tensor_reduce(prob[:, 0:384].rearrange("p (g k) -> p g k", g=3),
                                                   bank[4][:, 0:384].rearrange("p (g k) -> p g k", g=3),
                                                   bias[:, h % 2, :, P:2 * P], 1.0, -3e38, ALU.add, ALU.max,
                                                   mx[:, 0:1]).then_inc(s["att_m"], 1)
                    dve.wait_ge(s["att_m"], J + 1)
                    nc.vector.tensor_scalar(small[:, 26:27], mx[:, 0:1], -1.0, None, ALU.mult
                                            ).then_inc(s["att_nm"], 1)

            def att_normalise(J):
                w = 768 if J % 2 == 0 else 384
                dve.wait_ge(s["att_p"], J + 1)
                nc.vector.reciprocal(small[:, 28:29], small[:, 27:28]).then_inc(s["att_rs"], 1)
                dve.wait_ge(s["att_rs"], J + 1)
                nc.vector.tensor_scalar(prob[:, 0:w], prob[:, 0:w], small[:, 28:29], None, ALU.mult
                                        ).then_inc(s["att_pn"], 1)

            def att_out(J):
                h, qt = J // 2, 1 - J % 2
                dve.wait_ge(s["ot_hi"], J + 1)
                cut = slice(qt * P, (qt + 1) * P)
                nc.vector.tensor_tensor(oT_lo[:, h, cut], bank[7][:, P - 1::-1], fp(oT_hi[:, h, cut]), ALU.subtract
                                        ).then_inc(s["ot_ev"], 1)

            def qkv_extra(m):
                pr, j = divmod(m, QU)
                J = 4 * (pr - 1) + j // 2
                if pr >= 1 and j % 2 == 0 and j > 0:
                    att_out(J - 1)
                if pr >= 1 and j % 2 == 0 and j < 8:
                    att_max(J)
                if m < 4 * KC:
                    ada_op(2 * KC + m)
                if pr >= 1 and j % 2 == 0 and j < 8:
                    att_normalise(J)
                if pr < PAIRS:
                    if j in (1, 3, 5):
                        qk_reduce(3 * pr + j // 2)
                    if j in (2, 4, 6):
                        qk_normalise(3 * pr + j // 2 - 1)

            for m in range(PURE):
                split_unit(m + AHEAD)
                qkv_extra(m)
                for r in tasks_at(m):
                    ada_evac(r)
            for v in range(QU):
                if v < 3:
                    split_unit(M_OUT0 + v + AHEAD)
                qkv_extra(PURE + v)
            split_unit(M_OUT0 + 3 + AHEAD)
            residual(0, M_OUT0 + 3)

            def ffn(f, base):
                q = 2 * f + 1
                norm(q)
                for r in range(3 * NF):
                    kind, j = ffn_step(r)
                    split_unit(base + r + AHEAD)
                    if kind == 1:
                        n = NF * f + j
                        dve.wait_ge(s["f_sil"], n + 1)
                        if n:
                            dve.wait_ge(s["f_tr"], n)
                        for t in range(T):
                            i = nc.vector.tensor_tensor(hid[:, t], bank[4 + t][:, FC:2 * FC], sil[:, t], ALU.mult)
                        i.then_inc(s["f_hid"], 1)
                    jt = 0 if r == 1 else j + 1 if kind == 2 and j < NF - 1 else None
                    if jt is not None:
                        n = NF * f + jt
                        dve.wait_ge(s["f_hi"], n + 1)
                        nc.vector.tensor_tensor(hidT(oT_lo, n), bank[6][:].rearrange("p (k t) -> p k t", k=2),
                                                fp(hidT(oT_hi, n)), ALU.subtract).then_inc(s["f_lo"], 1)
                    if f == 0:
                        for n in range(3 * r // 2, min(3 * (r + 1) // 2, ADA_BLOCKS * KC)):
                            ada_op(ADA_BLOCKS * KC + n)
                        for task in tasks_at(M_FFN0 + r):
                            ada_evac(task)
                residual(q, base + 3 * NF - 1)

            ffn(0, M_FFN0)
            norm(2)
            nc.vector.memset(Am, 0.0).then_inc(s["r_zero"], 1)
            dve.wait_ge(s["r_zero"], 1)

            def rec_gates(half):
                dve.wait_ge(s["r_tev"], 2 * half + 1)
                dve.wait_ge(s["lbd_s"], 2)
                for h in range(4):
                    c = 4 * half + h
                    cut = slice(h * SEQ, (h + 1) * SEQ)
                    i = nc.vector.tensor_scalar(forget[:, cut], rk[half][:, cut], lb[:, 1, c:c + 1],
                                                lb[:, 0, c:c + 1], ALU.mult, ALU.add)
                i.then_inc(s["r_fg"], 1)
                dve.wait_ge(s["r_fg"], half + 1)
                nc.vector.tensor_scalar(rk[half], forget, -1.0, 1.0, ALU.mult, ALU.add).then_inc(s["r_k"], 1)
                dve.wait_ge(s["r_k"], half + 1)
                dve.wait_ge(s["r_ln"], half + 1)
                for h in range(4):
                    for t in range(T):
                        cut = slice(h * SEQ + t * P, h * SEQ + (t + 1) * P)
                        i = nc.vector.tensor_tensor_scan(rG[half][:, cut], logf[:, cut], logf[:, cut], 0.0, ALU.add,
                                                         ALU.bypass)
                i.then_inc(s["r_G"], 1)

            def rec_scale(half, level):
                dve.wait_ge(s["r_E"], LEVELS * half + level)
                if level > 2:
                    dve.wait_ge(s["r_mm"], PRODUCTS * half + level)
                elif half:
                    dve.wait_ge(s["r_mm"], PRODUCTS * half - 2 + level)
                if level == 1:
                    dve.wait_ge(s["r_tev"], 2 * half + 2)
                h = gh(level)
                v = lambda y: y.rearrange("p (b two h) -> p b two h", two=2, h=h)
                E = v(rE[:, level % 2])
                Z = v(rZ[:, level % 2])
                nc.vector.tensor_tensor(Z[:, :, 0, :], v(rk[half])[:, :, 0, :], E[:, :, 0, :], ALU.mult)
                nc.vector.tensor_tensor(Z[:, :, 1, :], v(rq[half])[:, :, 1, :], E[:, :, 1, :], ALU.mult
                                        ).then_inc(s["r_q"], 1)

            def rec_take(half, o):
                dve.wait_ge(s["r_mm"], PRODUCTS * half + o + 1)
                if half and o == 0:
                    dve.wait_ge(s["r_o"], 2)
                if half or o:
                    dve.wait_ge(s["r_A"], (LEVELS + 1) * half + o)
                if o < 2:
                    dst = Am[:, 0:2].rearrange("p t (h b two) -> p (t h) b two", h=4, two=2)[:, :, :, o]
                    v = lambda y: y
                else:
                    n = gh(o - 1)
                    dst = Am[:, 0:2].rearrange("p t (g b two h) -> p (t g) b two h", g=4, two=2, h=n)[:, :, :, 1, :]
                    v = lambda y: y.rearrange("p g (b h) -> p g b h", h=n)
                m = masks[:, o, :].rearrange("p (o t) -> p o t", o=1).to_broadcast([P, 8, P // 2])
                nc.vector.copy_predicated(dst, v(m), v(bank[4 + o % 2][:].rearrange("p (g t) -> p g t", g=8))
                                          ).then_inc(s["r_A"], 1)

            def rec_squares(half, t):
                n = 2 * half + t
                dve.wait_ge(s["r_osq"], n + 1)
                c = 32 + 8 * half + 4 * t
                nc.vector.tensor_reduce(small[:, c:c + 4], sq[:, t].rearrange("p (h d) -> p h d", d=P), AX_X, ALU.add
                                        ).then_inc(s["r_ored"], 1)

            def rec_gate(half, t):
                dve.wait_ge(s["r_orstd"], half + 1)
                if t == 0:
                    c = 8 * half
                    refine(small[:, 48 + c:56 + c], small[:, 32 + c:40 + c], 8, 8, 1.0 / P)
                dve.wait_ge(s["r_oev"], 2 * half + t + 1)
                dve.wait_ge(s["r_nat"], 7 + half)
                for h in range(4):
                    cut = slice((4 * half + h) * P, (4 * half + h + 1) * P)
                    c = 48 + 8 * half + 4 * t + h
                    i = nc.vector.scalar_tensor_tensor(out=rV[:, t, cut], in0=rV[:, t, cut], scalar=small[:, c:c + 1],
                                                       in1=gates[:, t, cut], op0=ALU.mult, op1=ALU.mult)
                i.then_inc(s["r_on"], 1)

            def rec_out_rest(half, t):
                dve.wait_ge(s["r_ohi"], 2 * half + t + 1)
                cut = slice(t * P, (t + 1) * P)
                nc.vector.scalar_tensor_tensor(out=oT_lo[:, 4 * half:4 * half + 4, cut],
                                               in0=bank[6 + t][:].rearrange("p (h t) -> p h t", t=P),
                                               scalar=cols[:, GNORM0:GNORM0 + 1],
                                               in1=fp(oT_hi[:, 4 * half:4 * half + 4, cut]),
                                               op0=ALU.mult, op1=ALU.subtract).then_inc(s["r_olo"], 1)

            dve.wait_ge(s["masks_in"], 16)
            for step in range(16):
                scales = [(half, o - 1) for half, o in products_at(step) if o >= 2]
                takes = [(half, o) for half, o in products_at(step - 1) if o < PRODUCTS - 1]
                for n in range(2):
                    if n < len(takes):
                        rec_take(*takes[n])
                    if n < len(scales):
                        rec_scale(*scales[n])
                split_unit(M_IN + step + AHEAD)
                if step in (3, 9):
                    rec_gates(step // 9)
                for t in range(T):
                    if step == 13:
                        rec_squares(0, t)
                    if step == 14:
                        rec_gate(0, t)
                    if step == 15:
                        rec_out_rest(0, t)
            for half, o in products_at(15):
                if o < PRODUCTS - 1:
                    rec_take(half, o)
            split_unit(M_OUT1 + AHEAD)
            split_unit(M_OUT1 + 1 + AHEAD)
            for t in range(T):
                rec_squares(1, t)
            for t in range(T):
                rec_gate(1, t)
            for t in range(T):
                rec_out_rest(1, t)
            split_unit(M_OUT1 + 2 + AHEAD)
            split_unit(M_OUT1 + 3 + AHEAD)
            residual(2, M_OUT1 + 3)
            ffn(1, M_FFN1)


ROWS = [("c", 0, 8), ("norm_mix", 8, 16), ("norm_ffn", 24, 16), ("attn_q_gain", 40, 3), ("attn_k_gain", 43, 3),
        ("hgrn_lower_bounds", 46, 16), ("hgrn_gnorm", 62, 1)]
ROW_AP = {"c": "a (k d) -> (a k) d", "norm_mix": "a (k d) -> (a k) d", "norm_ffn": "a (k d) -> (a k) d",
          "attn_q_gain": "a g d -> (a g) d", "attn_k_gain": "a g d -> (a g) d",
          "hgrn_lower_bounds": "a (k d) -> (a k) d", "hgrn_gnorm": "a d -> a d"}
ROW_AP = {k: v for k, v in ROW_AP.items()}
NROWS = 63
NORM0, GAIN0, LB0, GNORM0 = 8, 40, 46, 62

TASKS = [(blk, kind, c0) for blk in range(2 * ADA_BLOCKS)
         for kind, c0 in ([("row", 0), ("row", 512)] if blk % ADA_BLOCKS in (2, 5) else [(KC, 0)])]


def tasks_until(block):
    return sum(1 for t in TASKS if t[0] <= block)


def tasks_at(m):
    late = {6: [8], 11: [9], 16: [10], 17: [11], 22: [12], 27: [13], 32: [14, 15]}
    return {9: [2], 10: [3], 18: [4], 26: [5], 33: [6], 34: [7]}.get(m, []) + late.get(m - M_FFN0, [])


TRANSPOSED = (2, 4, 8, 10)


def products_at(step):
    half, first = (0, 5) if step < 11 else (1, 11)
    return [(half, 2 * (step - first) + i) for i in range(2)] if first <= step < first + 5 else []


def base_of(n):
    f, j = divmod(n, NF)
    return (M_FFN0, M_FFN1)[f] + (3 * (j + 1) + 1 if j < NF - 1 else 3 * NF - 1)


_INS = ["x", "c", "rel_bias", "ada_w", "ada_b", "norm_mix", "norm_ffn", "attn_w_qkv", "attn_w_out", "attn_q_gain",
        "attn_k_gain", "hgrn_w_in", "hgrn_w_out", "hgrn_gnorm", "hgrn_lower_bounds", "ffn_w1", "ffn_w3", "ffn_w2"]


def kernel(**inputs):
    import numpy as _np
    import concourse.bacc as _bacc
    from concourse import mybir as _mybir
    from concourse.bass_utils import run_bass_kernel_spmd as _run

    nc = _bacc.Bacc("TRN2", target_bir_lowering=False, num_devices=1)
    data = {name: _np.ascontiguousarray(inputs[name]) for name in _INS}
    data |= {"distance_table": distance_table(), "mask_rows": mask_rows(), "pair_masks": pair_masks()}
    arrays, args = {}, {}
    for name, v in data.items():
        arrays[f"in_{name}_dram"] = v
        args[name] = nc.dram_tensor(f"in_{name}_dram", v.shape, _mybir.dt.from_np(v.dtype), kind="ExternalInput").ap()
    out = nc.dram_tensor("out_0_dram", (1, SEQ, D), F32, kind="ExternalOutput").ap()
    hybrid_trunk(nc, args, out)
    r = _run(nc, [arrays], core_ids=[0])
    return r.results[0]["out_0_dram"]
```

```python
from contextlib import ExitStack

import numpy as np
import concourse.bass as bass
from concourse import mybir

ALU = mybir.AluOpType
ACT = mybir.ActivationFunctionType
AX_X = mybir.AxisListType.X
F32 = mybir.dt.float32
F32R = mybir.dt.float32r
I32 = mybir.dt.int32

P = 128
SEQ = 256
D = 1024
KC = D // P
T = SEQ // P
HEADS = 8
GROUPS = ((128, 1), (512, 4), (2048, 16))
NG = len(GROUPS)
BUCKETS = 32
MAX_DISTANCE = 2048
F = ((8 * D // 3 + 255) // 256) * 256
FC = 256
NF = F // FC
EPS = 1e-6
MASKED = -1e30
UNIT = 2048
RAW = 3
SPL = 3
AHEAD = 2
PAIRS = HEADS // 2
QU = 9
ADA_COLS = D
FIRST = 8
ADA_RING = 2
ADA_BLOCKS = 6 * D // ADA_COLS
ADA_LATE = 2 * KC + PAIRS * QU + 4
LEVELS = 8
PRODUCTS = LEVELS + 2

M_OUT0 = PAIRS * QU
M_FFN0 = M_OUT0 + 4
M_IN = M_FFN0 + 3 * NF
M_OUT1 = M_IN + 16
M_FFN1 = M_OUT1 + 4
UNITS = M_FFN1 + 3 * NF


def distance_table():
    table = np.zeros((NG * BUCKETS + NG, 2 * P + P - 1), np.float32)
    exact = BUCKETS // 2
    for g, (window, dil) in enumerate(GROUPS):
        for i in range(table.shape[1]):
            dist = 2 * P - 1 - i
            if dist < 0 or dist > window or dist % dil:
                table[NG * BUCKETS + g, i] = 1.0
                continue
            large = exact + int(np.log(max(dist, 1) / exact) / np.log(MAX_DISTANCE / exact) * (BUCKETS - exact))
            table[g * BUCKETS + (dist if dist < exact else min(large, BUCKETS - 1)), i] = 1.0
    return table


def mask_rows():
    rows = np.zeros((NG, NG * HEADS), np.float32)
    for g in range(NG):
        rows[g, g * HEADS:(g + 1) * HEADS] = MASKED
    return rows


def pair_masks():
    masks = [np.eye(P, dtype=np.int32)]
    s = np.arange(P)[:, None]
    for level in range(1, LEVELS):
        h = gh(level)
        t = np.arange(P).reshape(-1, 2, h)[:, 1].reshape(1, -1)
        masks.append(((s // (2 * h) == t // (2 * h)) & (s % (2 * h) < h)).astype(np.int32))
    return np.concatenate(masks, axis=1)


def gh(level):
    return 1 << (level - 1)


def hybrid_trunk(nc, a, out):
    TABLE = 2 * P + P - 1
    GH = NG * HEADS
    with ExitStack() as ctx:
        def sb(name, shape, dt=F32):
            return ctx.enter_context(nc.sbuf_tensor(name, shape, dt))

        def sem(name):
            return ctx.enter_context(nc.semaphore(name))

        bank = [ctx.enter_context(nc.psum_tensor(f"bank{i}", [P, 512], F32)) for i in range(8)]

        raw = sb("raw", [P, RAW, UNIT])
        whi = sb("whi", [P, SPL, UNIT], F32R)
        wlo = sb("wlo", [P, SPL, UNIT], F32R)
        ada_w = sb("ada_w", [P, ADA_RING, ADA_COLS])
        acc = sb("acc", [P, 2, ADA_COLS])
        x = sb("x", [P, T, D])
        hT_hi = sb("hT_hi", [P, KC, SEQ], F32R)
        hT_lo = sb("hT_lo", [P, KC, SEQ], F32R)
        oT_hi = sb("oT_hi", [P, KC, SEQ], F32R)
        oT_lo = sb("oT_lo", [P, KC, SEQ], F32R)
        gate = sb("gate", [P, 2, D])
        ident = sb("ident", [P, P])
        ones = sb("ones", [P, P])
        rows = sb("rows", [64, P])
        cols = sb("cols", [P, 64])
        cact = sb("cact", [P, KC])
        mod_a = sb("mod_a", [P, 2, 2, KC])
        mod_b = sb("mod_b", [P, 2, 2, KC])
        lb = sb("lb", [P, 2, KC])
        lbd = sb("lbd", [P, KC])
        small = sb("small", [P, 64])
        eps = sb("eps", [P, 1])
        late_gate = sb("late_gate", [P, D])
        arena = sb("arena", [P, 14336])

        def part(at, shape):
            v = arena[:, at:at + int(np.prod(shape))]
            if len(shape) > 1:
                names = "abcd"[:len(shape)]
                v = v.rearrange(f"p ({' '.join(names)}) -> p {' '.join(names)}",
                                **{k: n for k, n in zip(names, shape)})
            return v

        hT = part(0, [KC, SEQ])
        xn = part(3072, [T, D])
        first_w = [part(at, [ADA_COLS]) for at in (0, 1024, 2048, 5120, 6144, 7168, 8192, 11264)]
        qT = part(0, [2, NG, 2 * SEQ])
        kT = part(3072, [2, NG, 2 * SEQ])
        vN = part(6144, [2, T, NG * 2 * P])
        qkn = part(9216, [2, T * 512])
        prob = part(11264, [768])
        probT = part(12032, [768])
        bias = part(12800, [2, NG, SEQ])
        rel3 = qkn[0:NG * BUCKETS + NG, 0, 0:GH]
        tabw = qkn[0:NG * BUCKETS + NG, 0, 64:64 + TABLE]
        tabT = qkn[0:GH, 0, 512:512 + TABLE]
        sil = part(6144, [T, FC])
        hid = part(6656, [T, FC])
        rq = [part(0, [1024]), ada_w[:, 0]]
        rk = [part(1024, [1024]), acc[:, 0]]
        rG = [part(2048, [1024]), acc[:, 1]]
        forget, logf = part(3072, [1024]), part(4096, [1024])
        gates = xn
        nat = part(5120, [T, 512])
        rE = part(6144, [2, 1024])
        rZ = part(8192, [2, 1024])
        rV = part(10240, [T, 1024])
        Am = part(12288, [3, 512])
        sq = sb("sq", [P, T, 512])
        masks = sb("masks", [P, (LEVELS + 1) * P // 2], I32)

        def hidT(v, n):
            return v[:, 2 * (n % 2):2 * (n % 2) + 2, :]

        scratch = nc.dram_tensor("bias_rows", (GH, TABLE), F32, kind="Internal").ap()

        raw_in = [sem(f"raw_in{i}") for i in range(RAW)]
        ada_in = [sem(f"ada_in{i}") for i in range(ADA_RING)]
        first_in = [sem(f"first_in{i}") for i in range(FIRST)]
        bias_in = [sem(f"bias_in{i}") for i in range(2)]
        names = """x_in rows_in masks_in rel_in tab_out out_done
            rounded split pe_unit
            pool_setup
            cols_t cols_s cact_s lbd_s lb_s
            ada_used ada_half ada_red ada_ev adab_in0 adab_in1 ada_zero
            tab_mm tab_cp
            xn_ssq xn_ln xn_rstd xn_s xn_tr xn_aff xn_aff_s xn_hi xn_lo res
            qk_sq qk_red qk_ln qk_rstd qk_norm qk_tr qk_tev v_ev
            att_s att_m att_nm att_p att_rs att_pn att_tr pt_ev att_pv ot_hi ot_ev
            f_sil f_hid f_tr f_hi f_lo
            yres_t y_first newton
            r_nat r_tr r_tev r_fg r_k r_ln r_G r_D r_E r_q r_mm r_A r_zero r_X r_o r_oev r_osq r_ored r_oln r_orstd
            r_on r_otr r_ohi r_olo""".split()
        s = {n: sem(n) for n in names}

        block = ctx.enter_context(nc.Block())

        def cols_of(w, c0, n, k0, nk):
            return w.rearrange("(k p) n -> p k n", p=P)[:, k0:k0 + nk, c0:c0 + n]

        def pieces(m):
            if m < M_OUT0:
                pr, j = divmod(m, QU)
                w = a["attn_w_qkv"][0]
                col = lambda g, which: (3 * g + which) * D + pr * 256
                if j == 8:
                    return [(cols_of(w, col(2, 2), 256, 0, 8), 8, 0, 256)]
                k0 = 4 * (j % 2)
                left, right = ((j // 2, 0), (j // 2, 1)) if j < 6 else ((0, 2), (1, 2))
                return [(cols_of(w, col(*left), 256, k0, 4), 4, 0, 256), (cols_of(w, col(*right), 256, k0, 4), 4, 256, 256)]
            if M_IN <= m < M_OUT1:
                c, j = divmod(m - M_IN, 2)
                first = [1024, 0, 2048, 1536, 512, 2560, 3072, 3584][c]
                return [(cols_of(a["hgrn_w_in"][0], first, 512, 4 * j, 4), 4, 0, 512)]
            for base, w in ((M_OUT0, a["attn_w_out"][0]), (M_OUT1, a["hgrn_w_out"][0])):
                if base <= m < base + 4:
                    return [(cols_of(w, 0, 1024, 2 * (m - base), 2), 2, 0, 1024)]
            layer, r = (0, m - M_FFN0) if m < M_IN else (1, m - M_FFN1)
            kind, j = ffn_step(r)
            if kind == 2:
                return [(cols_of(a["ffn_w2"][layer], 0, 1024, 2 * j, 2), 2, 0, 1024)]
            return [(cols_of(a["ffn_w1"][layer], j * FC, FC, 4 * kind, 4), 4, 0, FC),
                    (cols_of(a["ffn_w3"][layer], j * FC, FC, 4 * kind, 4), 4, FC, FC)]

        def ffn_step(r):
            if r < 2:
                return r, 0
            if r == 3 * NF - 1:
                return 2, NF - 1
            j, k = divmod(r + 1, 3)
            return (k, j) if k < 2 else (2, j - 1)

        def hidden_after(r):
            kind, j = ffn_step(r)
            return 0 if r == 2 else j + 1 if kind == 2 and j < NF - 1 else None

        need, came = [], [0] * RAW
        for m in range(UNITS):
            came[m % RAW] += 16 * len(pieces(m))
            need.append(came[m % RAW])

        def load_bias(sp, h):
            if h >= 2:
                sp.wait_ge(s["att_nm"], 2 * (h - 1))
            skewed = bass.AP(scratch.tensor, h * TABLE, [[1, P], [HEADS * TABLE, NG], [1, SEQ]])
            sp.dma_start(bias[:, h % 2], skewed).then_inc(bias_in[h % 2], 16)

        @block.sync
        def _(sp):
            sp.dma_start(x[:], a["x"][0].rearrange("(t p) d -> p t d", p=P)).then_inc(s["x_in"], 16)
            for n, (name, r0, nr) in enumerate(ROWS):
                src = a[name].rearrange(ROW_AP[name], d=P)
                sp.dma_start(rows[r0:r0 + nr, :], src).then_inc(s["rows_in"], 16)
            for g in range(NG):
                sp.wait_ge(s["pool_setup"], 4)
                sp.dma_start(rel3[g * BUCKETS:(g + 1) * BUCKETS, g * HEADS:(g + 1) * HEADS],
                             a["rel_bias"][:, g * HEADS:(g + 1) * HEADS]).then_inc(s["rel_in"], 16)
            sp.dma_start(rel3[NG * BUCKETS:, :], a["mask_rows"]).then_inc(s["rel_in"], 16)
            sp.dma_start(tabw, a["distance_table"]).then_inc(s["rel_in"], 16)
            for m in range(UNITS):
                if m == 0:
                    sp.wait_ge(s["ada_used"], KC)
                if m >= RAW:
                    sp.wait_ge(s["split"], m - RAW + 1)
                for src, nk, c0, n in pieces(m):
                    slot = raw[:, m % RAW, :].rearrange("p (k n) -> p k n", k=nk)
                    sp.dma_start(slot[:, :, c0:c0 + n], src).then_inc(raw_in[m % RAW], 16)
                if m == 2:
                    sp.dma_start(masks[:], a["pair_masks"]).then_inc(s["masks_in"], 16)
                    sp.wait_ge(s["tab_cp"], 1)
                    sp.dma_start(scratch, tabT).then_inc(s["tab_out"], 16)
                    sp.wait_ge(s["tab_out"], 16)
                    load_bias(sp, 0)
                    load_bias(sp, 1)
                for h in range(2, HEADS):
                    if m == QU * (h // 2 + 1) + 4 * (h % 2):
                        load_bias(sp, h)
            for t in range(T):
                sp.wait_ge(s["res"], 4 * 3 + 2 * (t + 1))
                sp.dma_start(out[0, t * P:(t + 1) * P, :], x[:, t]).then_inc(s["out_done"], 16)
            sp.wait_ge(s["out_done"], 16 * T)

        @block.gpsimd
        def _(pool):
            pool.memset(ident[:], 0.0).then_inc(s["pool_setup"], 1)
            pool.memset(ones[:], 1.0).then_inc(s["pool_setup"], 1)
            pool.memset(eps[:], EPS).then_inc(s["pool_setup"], 1)
            pool.memset(rel3, 0.0).then_inc(s["pool_setup"], 1)
            pool.wait_ge(s["pool_setup"], 1)
            pool.affine_select(out=ident[:], in_=ident[:], compare_op=ALU.not_equal, fill=1.0, base=0,
                               pattern=[[-1, P]], channel_multiplier=1).then_inc(s["pool_setup"], 1)
            for n in range(2 * ADA_BLOCKS * KC):
                layer, b, k = n // (ADA_BLOCKS * KC), n // KC % ADA_BLOCKS, n % KC
                if k == 0:
                    blk = ADA_BLOCKS * layer + b
                    if blk >= 2:
                        pool.wait_ge(s["ada_red"], tasks_until(blk - 2))
                        pool.memset(acc[:, blk % 2], 0.0).then_inc(s["ada_zero"], 1)
                    pool.wait_ge(s["ada_zero"], max(1, blk))
                    pool.dma_start(acc[0:1, blk % 2, :], a["ada_b"][layer:layer + 1, b * ADA_COLS:(b + 1) * ADA_COLS]
                                   ).then_inc(s[f"adab_in{blk % 2}"], 16)
                if n < 2 * KC:
                    if n >= FIRST:
                        pool.wait_ge(s["ada_used"], n - FIRST + 1)
                    pool.dma_start(first_w[n % FIRST], a["ada_w"][layer, k * P:(k + 1) * P, b * ADA_COLS:(b + 1) * ADA_COLS]
                                   ).then_inc(first_in[n % FIRST], 16)
                    continue
                if n >= 2 * KC + ADA_RING:
                    pool.wait_ge(s["ada_used"], n - ADA_RING + 1)
                pool.dma_start(ada_w[:, n % ADA_RING], a["ada_w"][layer, k * P:(k + 1) * P, b * ADA_COLS:(b + 1) * ADA_COLS]
                               ).then_inc(ada_in[n % ADA_RING], 16)

            def rec_diff(half, level):
                E, G = rE[:, level % 2], rG[half]
                pool.wait_ge(s["r_G"], half + 1)
                if LEVELS * half + level > 2:
                    pool.wait_ge(s["r_q"], LEVELS * half + level - 2)
                if level < LEVELS:
                    h = gh(level)
                    v = lambda y: y.rearrange("p (b two h) -> p b two h", two=2, h=h)
                    mid = v(G)[:, :, 0, h - 1:h].to_broadcast([P, 1024 // (2 * h), h])
                    pool.tensor_tensor(v(E)[:, :, 0, :], mid, v(G)[:, :, 0, :], ALU.subtract)
                    i = pool.tensor_tensor(v(E)[:, :, 1, :], v(G)[:, :, 1, :], mid, ALU.subtract)
                else:
                    v = lambda y: y.rearrange("p (h t n) -> p h t n", t=2, n=P)
                    end = v(G)[:, :, 0, P - 1:P].to_broadcast([P, 4, P])
                    pool.tensor_tensor(v(E)[:, :, 0, :], end, v(G)[:, :, 0, :], ALU.subtract)
                    i = pool.tensor_copy(v(E)[:, :, 1, :], v(G)[:, :, 1, :])
                i.then_inc(s["r_D"], 1)

            for half in range(2):
                for level in range(1, LEVELS + 1):
                    rec_diff(half, level)

        PURE = PAIRS * QU

        def chunk_end(n):
            pr, c = divmod(n, 5)
            return pr * QU + (2 * c + 2 if c < 4 else 9)

        def blocks_of(qt):
            return [(g, kt) for g in range(NG) for kt in range(qt + 1)]

        LATE = 4 * (PAIRS - 1)

        def second(J):
            return J > LATE and J % 2 == 1

        def before(J):
            return J - 1 if J > LATE else J

        def probs(J):
            return (part(9216, [384]), part(9600, [384])) if second(J) else (prob, probT)

        def stat(J, i):
            c = (48 if second(J) else 24) + i
            return small[:, c:c + 1]

        def score_bank(J):
            return bank[6] if second(J) else bank[4]

        def out_bank(J):
            return bank[6][:, 384:512] if second(J) else bank[7][:, 0:P]

        @block.tensor
        def _(pe):
            def unit(m, lhs_hi, lhs_lo, nk, k0, n, dst, first, last, tiles=range(T), tile_done=None):
                sl = m % SPL
                w = [v[:, sl, :].rearrange("p (k n) -> p k n", k=nk) for v in (whi, wlo)]
                pe.wait_ge(s["split"], m + 1)
                for t in tiles:
                    for k in range(nk):
                        hi = lhs_hi[:, k0 + k, t * P:(t + 1) * P]
                        lo = lhs_lo[:, k0 + k, t * P:(t + 1) * P]
                        for c, d in enumerate(dst[t]):
                            cut = slice(c * 512, c * 512 + n)
                            for q, (l, r) in enumerate(((hi, w[0]), (hi, w[1]), (lo, w[0]))):
                                mm = nc.tensor.matmul(d[:, 0:n], l, r[:, k, cut],
                                                      start=first and k == 0 and q == 0,
                                                      stop=last and k == nk - 1 and q == 2)
                    if t == 0 and tile_done is not None:
                        mm.then_inc(s[tile_done], 1)
                if t == T - 1:
                    mm.then_inc(s["pe_unit"], 1)

            def norm_t(q, t):
                pe.wait_ge(s["xn_s"], 2 * q + t + 1)
                if q and t:
                    pe.wait_ge(s["ada_ev"], pv[1])
                for g in range(2):
                    for k in range(4):
                        c = (4 * g + k) * P
                        mm = nc.tensor.transpose(bank[4 + 2 * t + g][:, k * P:(k + 1) * P], xn[:, t, c:c + P], ident[:])
                    mm.then_inc(s["xn_tr"], 1)

            def first_units(q, m, dst):
                for t in range(T):
                    for j in range(2):
                        if q and (t, j) == (0, 1):
                            norm_t(q, 1)
                        pe.wait_ge(s["xn_lo"], 4 * q + 2 * t + j + 1)
                        unit(m + j, hT_hi, hT_lo, 4, 4 * j, 512, dst, j == 0, j == 1, tiles=(t,))

            pv = [0, 0]

            def reduce_task(r, b=7):
                blk, kind, half = TASKS[r]
                pe.wait_ge(s["ada_half" if r == 1 else "ada_used"], KC * (blk + 1))
                if r:
                    pe.wait_ge(s["ada_ev"], 1 if r == 2 else r)
                if pv[0]:
                    pe.wait_ge(s["ot_ev"], pv[0])
                pv[1] = r + 1
                src = acc[:, blk % 2, :]
                if kind == "row":
                    mm = nc.tensor.matmul(bank[b][:], ones[:], src[:, half:half + 512], start=True, stop=True)
                else:
                    for j in range(kind):
                        mm = nc.tensor.matmul(bank[b][:, j:j + 1], src[:, half + j * P:half + (j + 1) * P],
                                              ones[:, 0:1], start=True, stop=True)
                mm.then_inc(s["ada_red"], 1)

            pe.wait_ge(s["rows_in"], 16 * len(ROWS))
            pe.wait_ge(s["pool_setup"], 5)
            nc.tensor.transpose(bank[0][:, 0:NROWS], rows[0:NROWS, :], ident[0:NROWS, 0:NROWS]).then_inc(s["cols_t"], 1)
            pe.wait_ge(s["rel_in"], 16 * 5)
            nc.tensor.matmul(bank[1][0:GH, 0:TABLE], rel3, tabw, start=True, stop=True).then_inc(s["tab_mm"], 1)
            for t in range(T):
                norm_t(0, t)
            for r in range(3):
                reduce_task(r, 3 if r < 2 else 2)
            pe.wait_ge(s["tab_cp"], 1)

            def qkv_unit(m):
                pr, j = divmod(m, QU)
                n = 5 * pr + min(j // 2, 4)
                if j % 2 == 0 and n >= 2:
                    c = (n - 2) % 5
                    if c < 3:
                        pe.wait_ge(s["qk_norm"], 3 * ((n - 2) // 5) + c + 1)
                    else:
                        pe.wait_ge(s["v_ev"], 2 * ((n - 2) // 5) + c - 2)
                b = 2 * (n % 2)
                nk, w = (8, 256) if j == 8 else (4, 512)
                unit(m, hT_hi, hT_lo, nk, 0 if j == 8 else 4 * (j % 2), w, [[bank[b]], [bank[b + 1]]],
                     j % 2 == 0, j % 2 == 1 or j == 8)

            def qk_transposes(n, which):
                pe.wait_ge(s["qk_norm"], n + 1)
                pe.wait_ge(s["qk_tev"], 2 * n + which)
                for h in range(2):
                    for t in range(T):
                        c = t * 512 + (2 * which + h) * P
                        mm = nc.tensor.transpose(bank[6][:, h * SEQ + t * P:h * SEQ + (t + 1) * P],
                                                 qkn[:, n % 2, c:c + P], ident[:])
                mm.then_inc(s["qk_tr"], 1)

            def att_scores(J):
                pr, hh, qt = J // 4, J // 2 % 2, 1 - J % 2
                pe.wait_ge(s["qk_tev"], 6 * (pr + 1))
                if J:
                    pe.wait_ge(s["pt_ev"], before(J))
                if second(J):
                    pe.wait_ge(s["ot_ev"], before(J))
                w = (qt + 1) * P
                for g in range(NG):
                    dst = score_bank(J)[:, g * w:(g + 1) * w] if (g + 1) * w <= 512 else bank[5][:, 0:w]
                    base = hh * SEQ
                    mm = nc.tensor.matmul(dst, qT[:, pr % 2, g, base + qt * P:base + (qt + 1) * P],
                                          kT[:, pr % 2, g, base:base + w], start=True, stop=True)
                mm.then_inc(s["att_s"], 1)

            def att_transposes(J):
                qt = 1 - J % 2
                pe.wait_ge(s["att_pn"], J + 1)
                for i in range(len(blocks_of(qt))):
                    dst = score_bank(J) if i < 4 else bank[5]
                    mm = nc.tensor.transpose(dst[:, i % 4 * P:(i % 4 + 1) * P], probs(J)[0][:, i * P:(i + 1) * P],
                                             ident[:])
                mm.then_inc(s["att_tr"], 1)

            def att_values(J):
                pr, hh, qt = J // 4, J // 2 % 2, 1 - J % 2
                pe.wait_ge(s["pt_ev"], J + 1)
                pe.wait_ge(s["v_ev"], 2 * (pr + 1))
                if J:
                    pe.wait_ge(s["ot_ev"], before(J))
                pe.wait_ge(s["ada_ev"], pv[1])
                pv[0] = J + 1
                todo = blocks_of(qt)
                for i, (g, kt) in enumerate(todo):
                    c = g * 256 + hh * P
                    mm = nc.tensor.matmul(out_bank(J), vN[:, pr % 2, kt, c:c + P], probs(J)[1][:, i * P:(i + 1) * P],
                                          start=i == 0, stop=i == len(todo) - 1)
                mm.then_inc(s["att_pv"], 1)

            def qkv_extra(m):
                pr, j = divmod(m, QU)
                if pr >= 1:
                    J = 4 * (pr - 1) + j // 2
                    if j % 2 == 0 and j < 8:
                        att_scores(J)
                    if j % 2 == 0 and j > 0:
                        att_values(J - 1)
                    if j % 2 == 1:
                        att_transposes(J)
                if pr < PAIRS and 3 <= j <= 8:
                    qk_transposes(3 * pr + (j - 3) // 2, (j - 3) % 2)

            first_units(0, 0, [[bank[0]], [bank[1]]])
            for m in range(PURE):
                if m >= 2:
                    qkv_unit(m)
                qkv_extra(m)
                for r in tasks_at(m):
                    reduce_task(r)
            Y = [[bank[0], bank[1]], [bank[2], bank[3]]]

            def out_tile(v, t):
                unit(M_OUT0 + v, oT_hi, oT_lo, 2, 2 * v, 512, Y, v == 0, False, tiles=(t,))

            pe.wait_ge(s["v_ev"], 2 * PAIRS)
            pe.wait_ge(s["qk_norm"], 3 * PAIRS)
            pe.wait_ge(s["ot_ev"], 4)
            out_tile(0, 0)
            att_scores(LATE)
            att_scores(LATE + 1)
            out_tile(0, 1)
            pe.wait_ge(s["ot_ev"], 8)
            out_tile(1, 0)
            att_transposes(LATE)
            att_transposes(LATE + 1)
            out_tile(1, 1)
            att_values(LATE)
            att_values(LATE + 1)
            att_scores(LATE + 2)
            att_scores(LATE + 3)
            pe.wait_ge(s["ot_ev"], 12)
            out_tile(2, 0)
            out_tile(2, 1)
            att_transposes(LATE + 2)
            att_transposes(LATE + 3)
            att_values(LATE + 2)
            att_values(LATE + 3)
            pe.wait_ge(s["ot_ev"], 16)
            unit(M_OUT0 + 3, oT_hi, oT_lo, 2, 6, 512, Y, False, True, tile_done="y_first")

            def ffn(f, base):
                q = 2 * f + 1
                if f == 0:
                    reduce_task(AT_NORM[q][0])
                norm_t(q, 0)
                if f == 0:
                    reduce_task(AT_NORM[q][1])
                first_units(q, base, [[bank[0]], [bank[1]]])
                for r in range(3 * NF):
                    kind, j = ffn_step(r)
                    n = NF * f + j
                    if kind < 2 and j == 0:
                        pass
                    elif kind < 2:
                        if kind == 0 and j > 1:
                            pe.wait_ge(s["f_hid"], n)
                        unit(base + r, hT_hi, hT_lo, 4, 4 * kind, 512, [[bank[4]], [bank[5]]], kind == 0, kind == 1)
                    else:
                        pe.wait_ge(s["f_lo"], n + 1)
                    for t in range(T if kind == 2 else 0):
                        if t:
                            hidden_transposes(f, hidden_after(r))
                        unit(base + r, hidT(oT_hi, n), hidT(oT_lo, n), 2, 0, 512, Y, j == 0, j == NF - 1, tiles=(t,),
                             tile_done="y_first" if j == NF - 1 else None)
                    if r == 2:
                        hidden_transposes(f, 0)
                    if f == 0:
                        for task in tasks_at(M_FFN0 + r):
                            reduce_task(task)

            def hidden_transposes(f, jt):
                if jt is None:
                    return
                n = NF * f + jt
                pe.wait_ge(s["f_hid"], n + 1)
                if n:
                    pe.wait_ge(s["f_lo"], n)
                for k in range(2):
                    for t in range(T):
                        mm = nc.tensor.transpose(bank[6][:, k * SEQ + t * P:k * SEQ + (t + 1) * P],
                                                 hid[:, t, k * P:(k + 1) * P], ident[:])
                mm.then_inc(s["f_tr"], 1)

            ffn(0, M_FFN0)

            reduce_task(AT_NORM[2][0])
            norm_t(2, 0)
            reduce_task(AT_NORM[2][1])

            def rec_transposes(n):
                pe.wait_ge(s["r_nat"], (1, 2, 4, 5)[n])
                if n:
                    pe.wait_ge(s["r_tev"], n)
                else:
                    pe.wait_ge(s["ada_ev"], pv[1])
                for h in range(4):
                    for t in range(T):
                        mm = nc.tensor.transpose(bank[6 + h // 2][:, h % 2 * SEQ + t * P:h % 2 * SEQ + (t + 1) * P],
                                                 nat[:, t, h * P:(h + 1) * P], ident[:])
                mm.then_inc(s["r_tr"], 1)

            def rec_product(half, o):
                level = o - 1
                dst = bank[4 + o % 2]
                if o < 2:
                    pe.wait_ge(s["r_tev"], 2 * half + 2)
                    pe.wait_ge(s["r_k"], half + 1)
                    q_, k_ = rq[half], rk[half]
                else:
                    pe.wait_ge(s["r_q"], LEVELS * half + level)
                    q_ = k_ = rZ[:, level % 2]
                if o == 1 and half:
                    pe.wait_ge(s["r_X"], half)
                elif o != 1 and (half or o):
                    pe.wait_ge(s["r_A"], (LEVELS + 1) * half + max(o - 1, 0))
                for h in range(4):
                    if o < 2:
                        tok = slice(h * SEQ + o * P, h * SEQ + (o + 1) * P)
                        mm = nc.tensor.matmul(dst[:, h * P:(h + 1) * P], k_[:, tok], q_[:, tok], start=True, stop=True)
                        continue
                    if level == LEVELS:
                        mm = nc.tensor.matmul(dst[:, h * P:(h + 1) * P], k_[:, h * SEQ:h * SEQ + P],
                                              q_[:, h * SEQ + P:(h + 1) * SEQ], start=True, stop=True)
                        continue
                    for t in range(T):
                        tok = slice(h * SEQ + t * P, h * SEQ + (t + 1) * P)
                        y = dst[:, (4 * t + h) * 64:(4 * t + h + 1) * 64]
                        n = gh(level)
                        cols_t = q_[:, tok].rearrange("p (b two h) -> p b two h", two=2, h=n)[:, :, 1, :]
                        y = y.rearrange("p (b h) -> p b h", h=n)
                        mm = nc.tensor.matmul(y, k_[:, tok], cols_t, start=True, stop=True)
                mm.then_inc(s["r_mm"], 1)

            def rec_values(half, t):
                pe.wait_ge(s["r_A"], (LEVELS + 1) * (half + 1))
                pe.wait_ge(s["r_X"], half + 1)
                pe.wait_ge(s["r_nat"], 6 if half else 3)
                if half:
                    pe.wait_ge(s["r_olo"], 2)
                else:
                    pe.wait_ge(s["r_tev"], 4)
                for h in range(4):
                    c = slice(h * P, (h + 1) * P)
                    v = slice(half * 512 + h * P, half * 512 + (h + 1) * P)
                    mm = nc.tensor.matmul(bank[6 + t][:, c], Am[:, t, c], rV[:, t, v], start=True, stop=t == 0)
                    if t:
                        mm = nc.tensor.matmul(bank[6 + t][:, c], Am[:, 2, c], rV[:, 0, v], start=False, stop=True)
                mm.then_inc(s["r_o"], 1)

            def rec_out_transposes(half, t):
                pe.wait_ge(s["r_on"], 2 * half + t + 1)
                for h in range(4):
                    mm = nc.tensor.transpose(bank[6 + t][:, h * P:(h + 1) * P],
                                             rV[:, t, (4 * half + h) * P:(4 * half + h + 1) * P], ident[:])
                mm.then_inc(s["r_otr"], 1)

            for step in range(16):
                c, j = divmod(step, 2)
                if j == 0 and c >= 2:
                    pe.wait_ge(s["r_nat"], c - 1)
                b = 2 * (c % 2)
                if c:
                    unit(M_IN + step, hT_hi, hT_lo, 4, 4 * j, 512, [[bank[b]], [bank[b + 1]]], j == 0, j == 1)
                elif j == 0:
                    first_units(2, M_IN, [[bank[0]], [bank[1]]])
                    reduce_task(len(TASKS) - 1)
                if step in TRANSPOSED:
                    rec_transposes(TRANSPOSED.index(step))
                if step == 11:
                    for t in range(T):
                        rec_values(0, t)
                for half, o in products_at(step):
                    rec_product(half, o)
                if step == 14:
                    for t in range(T):
                        rec_out_transposes(0, t)
            pe.wait_ge(s["r_nat"], 8)
            pe.wait_ge(s["r_olo"], 2)
            unit(M_OUT1, oT_hi, oT_lo, 2, 0, 512, Y, True, False)
            for t in range(T):
                rec_values(1, t)
            unit(M_OUT1 + 1, oT_hi, oT_lo, 2, 2, 512, Y, False, False)
            for t in range(T):
                rec_out_transposes(1, t)
            pe.wait_ge(s["r_olo"], 4)
            unit(M_OUT1 + 2, oT_hi, oT_lo, 2, 4, 512, Y, False, False)
            unit(M_OUT1 + 3, oT_hi, oT_lo, 2, 6, 512, Y, False, True, tile_done="y_first")
            ffn(1, M_FFN1)

        @block.scalar
        def _(act):
            count = {}

            def copy(dst, src):
                return nc.scalar.activation(dst, src, ACT.Copy)

            def round_unit(m):
                if m >= UNITS:
                    return
                act.wait_ge(raw_in[m % RAW], need[m])
                if m >= SPL:
                    act.wait_ge(s["pe_unit"], m - SPL + 1)
                copy(whi[:, m % SPL, :], raw[:, m % RAW, :]).then_inc(s["rounded"], 1)

            def ada_row(r):
                blk, _, half = TASKS[r]
                layer, what = divmod(blk, ADA_BLOCKS)
                act.wait_ge(s["ada_red"], r + 1)
                dst = late_gate if (layer, what) == (1, 5) else gate[:, what // 5, :]
                copy(dst[:, half:half + 512], bank[7][:]).then_inc(s["ada_ev"], 1)

            def rsqrt(dst, src, ln_sem, out_sem, n, scale):
                nc.scalar.activation(dst, src, ACT.Ln, bias=eps[:, 0:1], scale=scale).then_inc(s[ln_sem], 1)
                act.wait_ge(s[ln_sem], n + 1)
                nc.scalar.activation(dst, dst, ACT.Exp, scale=-0.5).then_inc(s[out_sem], 1)

            def norm_stats(q, t):
                if q:
                    act.wait_ge(s["res"], 4 * (q - 1) + 2 * (t + 1))
                else:
                    act.wait_ge(s["x_in"], 16)
                    act.wait_ge(s["pool_setup"], 3)
                if q or t:
                    act.wait_ge(s["xn_ssq"], 2 * q + t)
                junk = part(2048, [D]) if q else sq[:, :, :].rearrange("p a b -> p (a b)")
                nc.scalar.activation(junk, x[:, t], ACT.Square, accum_out=small[:, t:t + 1]
                                     ).then_inc(s["xn_ssq"], 1)
                act.wait_ge(s["xn_ssq"], 2 * q + t + 1)
                rsqrt(small[:, 2 + t:3 + t], small[:, t:t + 1], "xn_ln", "xn_rstd", 2 * q + t, 1.0 / D)

            def norm_round(q, t):
                layer, sub = q // 2, q % 2
                cut = slice(t * P, (t + 1) * P)
                act.wait_ge(s["xn_tr"], 4 * q + 2 * t + 2)
                if q == 0:
                    act.wait_ge(s["xn_aff"], t + 1)
                    copy(hT_hi[:, 0:4, cut], hT[:, 0:4, cut]).then_inc(s["xn_hi"], 1)
                    act.wait_ge(s["ada_ev"], 3)
                for kc in range(4, KC):
                    i = nc.scalar.activation(hT[:, kc, cut], bank[5 + 2 * t][:, (kc - 4) * P:(kc - 3) * P],
                                             ACT.Identity, bias=mod_b[:, layer, sub, kc:kc + 1],
                                             scale=mod_a[:, layer, sub, kc:kc + 1])
                i.then_inc(s["xn_aff_s"], 1)
                if q:
                    act.wait_ge(s["xn_aff"], 2 * q + t + 1)
                    copy(hT_hi[:, 0:4, cut], hT[:, 0:4, cut]).then_inc(s["xn_hi"], 1)
                act.wait_ge(s["xn_aff_s"], 2 * q + t + 1)
                copy(hT_hi[:, 4:8, cut], hT[:, 4:8, cut]).then_inc(s["xn_hi"], 1)

            act.wait_ge(s["cols_s"], 1)
            nc.scalar.activation(cact[:], cols[:, 0:KC], ACT.Silu).then_inc(s["cact_s"], 1)
            act.wait_ge(s["lbd_s"], 1)
            nc.scalar.activation(lb[:, 0, :], lbd[:], ACT.Sigmoid).then_inc(s["lb_s"], 1)
            nc.scalar.preload_act_table_set("natural_log_exp_and_others")
            for t in range(T):
                norm_stats(0, t)
            round_unit(0)
            norm_round(0, 0)
            round_unit(1)
            norm_round(0, 1)

            def qk_square(n):
                act.wait_ge(s["pe_unit"], chunk_end(5 * (n // 3) + n % 3))
                if n:
                    act.wait_ge(s["qk_red"], n)
                b = 2 * ((5 * (n // 3) + n % 3) % 2)
                for t in range(T):
                    i = nc.scalar.activation(sq[:, t], bank[b + t][:], ACT.Square)
                i.then_inc(s["qk_sq"], 1)

            def qk_rsqrt(n):
                act.wait_ge(s["qk_red"], n + 1)
                if n:
                    act.wait_ge(s["qk_norm"], n)
                rsqrt(small[:, 16:24], small[:, 8:16], "qk_ln", "qk_rstd", n, 1.0 / P)

            def qk_evac(n, which):
                pr, g = divmod(n, 3)
                act.wait_ge(s["qk_tr"], 2 * n + which + 1)
                if pr >= 2:
                    act.wait_ge(s["att_s"], 4 * (pr - 1))
                view = lambda y: y.rearrange("p (b t) -> p b t", t=P)
                dst, src = view((qT, kT)[which][:, pr % 2, g, :]), view(bank[6][:])
                if which == 0:
                    src = src[:, :, ::-1]
                nc.scalar.activation(dst, src, ACT.Copy, scale=gains[:, which * NG + g:which * NG + g + 1]
                                     ).then_inc(s["qk_tev"], 1)

            def v_evac(pr, c):
                n = 5 * pr + 3 + c
                act.wait_ge(s["pe_unit"], chunk_end(n))
                if pr >= 2:
                    act.wait_ge(s["att_pv"], 4 * (pr - 1))
                b = 2 * (n % 2)
                for t in range(T):
                    i = copy(vN[:, pr % 2, t, 512:768], bank[b + t][:, 0:256]) if c else \
                        copy(vN[:, pr % 2, t, 0:512], bank[b + t][:])
                i.then_inc(s["v_ev"], 1)

            def att_exp(J):
                w = 768 if J % 2 == 0 else 384
                act.wait_ge(s["att_nm"], J + 1)
                pr_ = probs(J)[0][:, 0:w]
                nc.scalar.activation(pr_, pr_, ACT.Exp, bias=stat(J, 2), accum_out=stat(J, 3)).then_inc(s["att_p"], 1)

            def att_evac(J):
                act.wait_ge(s["att_tr"], J + 1)
                if J:
                    act.wait_ge(s["att_pv"], before(J))
                if J % 2 == 0:
                    copy(probT[:, 0:512], bank[4][:])
                    i = copy(probT[:, 512:768], bank[5][:, 0:256])
                else:
                    i = copy(probs(J)[1][:, 0:384], score_bank(J)[:, 0:384])
                i.then_inc(s["pt_ev"], 1)

            def att_out(J):
                h, qt = J // 2, 1 - J % 2
                act.wait_ge(s["att_pv"], J + 1)
                copy(oT_hi[:, h, qt * P:(qt + 1) * P], out_bank(J)[:, ::-1]).then_inc(s["ot_hi"], 1)

            def qkv_extra(m):
                pr, j = divmod(m, QU)
                if pr < PAIRS and j in (1, 3, 5):
                    qk_square(3 * pr + j // 2)
                if pr < PAIRS and j in (2, 4, 6):
                    qk_rsqrt(3 * pr + j // 2 - 1)
                if pr >= 1:
                    J = 4 * (pr - 1) + j // 2
                    if j % 2 == 0 and j > 0:
                        att_out(J - 1)
                    if j % 2 == 0 and j < 8:
                        att_exp(J)
                    if j % 2 == 1:
                        att_evac(J)
                if pr < PAIRS:
                    if 3 <= j <= 8:
                        qk_evac(3 * pr + (j - 3) // 2, (j - 3) % 2)
                    if j >= 7:
                        v_evac(pr, j - 7)

            gains = cols[:, GAIN0:GAIN0 + 2 * NG]
            act.wait_ge(s["cols_s"], 2)
            for m in range(PURE):
                round_unit(m + AHEAD)
                qkv_extra(m)
            round_unit(M_OUT0 + AHEAD)
            att_exp(LATE)
            att_exp(LATE + 1)
            round_unit(M_OUT0 + 1 + AHEAD)
            att_evac(LATE)
            att_evac(LATE + 1)
            att_out(LATE)
            att_out(LATE + 1)
            round_unit(M_OUT0 + 2 + AHEAD)
            att_exp(LATE + 2)
            att_exp(LATE + 3)
            att_evac(LATE + 2)
            att_evac(LATE + 3)
            att_out(LATE + 2)
            att_out(LATE + 3)
            round_unit(M_OUT0 + 3 + AHEAD)

            def ffn(f, base):
                norm_stats(2 * f + 1, 0)
                if f == 0:
                    ada_row(AT_NORM[1][0])
                norm_round(2 * f + 1, 0)
                norm_stats(2 * f + 1, 1)
                if f == 0:
                    ada_row(AT_NORM[1][1])
                nc.scalar.preload_act_table(ACT.Silu)
                norm_round(2 * f + 1, 1)
                for r in range(3 * NF):
                    kind, j = ffn_step(r)
                    round_unit(base + r + AHEAD)
                    if kind == 1:
                        n = NF * f + j
                        act.wait_ge(s["pe_unit"], base + r + 1)
                        if n:
                            act.wait_ge(s["f_hid"], n)
                        for t in range(T):
                            i = nc.scalar.activation(sil[:, t], bank[(4 if j else 0) + t][:, 0:FC], ACT.Silu)
                        i.then_inc(s["f_sil"], 1)
                    jt = hidden_after(r)
                    if jt is not None:
                        n = NF * f + jt
                        act.wait_ge(s["f_tr"], n + 1)
                        if n >= 2:
                            act.wait_ge(s["pe_unit"], base_of(n - 2) + 1)
                        copy(hidT(oT_hi, n), bank[6][:].rearrange("p (k t) -> p k t", k=2)).then_inc(s["f_hi"], 1)

            ffn(0, M_FFN0)
            nc.scalar.preload_act_table_set("natural_log_exp_and_others")
            norm_stats(2, 0)
            norm_round(2, 0)
            norm_stats(2, 1)
            ada_row(AT_NORM[2][1])
            norm_round(2, 1)

            def rec_exp(half, level):
                n = LEVELS * half + level - 1
                act.wait_ge(s["r_D"], n + 1)
                nc.scalar.activation(rE[:, level % 2], rE[:, level % 2], ACT.Exp).then_inc(s["r_E"], 1)

            def rec_cross(half):
                act.wait_ge(s["r_mm"], PRODUCTS * (half + 1))
                if half:
                    act.wait_ge(s["r_o"], 2)
                copy(Am[:, 2], bank[5][:]).then_inc(s["r_X"], 1)

            def rec_out(half):
                for t in range(T):
                    act.wait_ge(s["r_o"], 2 * half + t + 1)
                    if half:
                        act.wait_ge(s["r_ored"], 2)
                    nc.scalar.activation(sq[:, t], bank[6 + t][:], ACT.Square).then_inc(s["r_osq"], 1)
                for t in range(T):
                    copy(rV[:, t, half * 512:(half + 1) * 512], bank[6 + t][:]).then_inc(s["r_oev"], 1)

            def rec_rsqrt(half):
                act.wait_ge(s["r_ored"], 2 * half + 2)
                c = 8 * half
                rsqrt(small[:, 48 + c:56 + c], small[:, 32 + c:40 + c], "r_oln", "r_orstd", half, 1.0 / P)

            def rec_out_round(half, t):
                act.wait_ge(s["r_otr"], 2 * half + t + 1)
                nc.scalar.activation(oT_hi[:, 4 * half:4 * half + 4, t * P:(t + 1) * P],
                                     bank[6 + t][:].rearrange("p (h t) -> p h t", t=P), ACT.Copy,
                                     scale=cols[:, GNORM0:GNORM0 + 1]).then_inc(s["r_ohi"], 1)

            def rec_transposed(n):
                half = n // 2
                act.wait_ge(s["r_tr"], n + 1)
                dst = rq[half] if n % 2 else rk[half]
                for g in range(2):
                    i = nc.scalar.activation(dst[:, g * 512:(g + 1) * 512], bank[6 + g][:],
                                             ACT.Silu if n % 2 else ACT.Sigmoid)
                i.then_inc(s["r_tev"], 1)
                nc.scalar.preload_act_table_set("natural_log_exp_and_others")

            def rec_log(half):
                act.wait_ge(s["r_fg"], half + 1)
                if half:
                    act.wait_ge(s["r_G"], half)
                nc.scalar.activation(logf, forget, ACT.Ln).then_inc(s["r_ln"], 1)

            def rec_chunk(c):
                act.wait_ge(s["pe_unit"], M_IN + 2 * c + 2)
                b = 2 * (c % 2)
                if c in (1, 3, 4):
                    act.wait_ge(s["r_tr"], {1: 1, 3: 2, 4: 3}[c])
                if c == 6:
                    act.wait_ge(s["r_G"], 2)
                for t in range(T):
                    src = bank[b + t][:]
                    if c in (2, 5):
                        h = c // 3
                        i = copy(rV[:, t, h * 512:(h + 1) * 512], src)
                    elif c < 6:
                        i = copy(nat[:, t], src)
                    else:
                        i = nc.scalar.activation(gates[:, t, (c - 6) * 512:(c - 5) * 512], src, ACT.Silu)
                i.then_inc(s["r_nat"], 1)
                if c >= 6:
                    nc.scalar.preload_act_table_set("natural_log_exp_and_others")

            for step in range(16):
                if step == 10:
                    rec_cross(0)
                if step - 1 in TRANSPOSED and step != 9:
                    rec_transposed(TRANSPOSED.index(step - 1))
                for half, o in products_at(step):
                    if o >= 2:
                        rec_exp(half, o - 1)
                round_unit(M_IN + step + AHEAD)
                if step == 9:
                    rec_transposed(2)
                if step in (3, 9):
                    rec_log(step // 9)
                if step == 12:
                    rec_out(0)
                if step == 13:
                    rec_rsqrt(0)
                if step == 15:
                    for t in range(T):
                        rec_out_round(0, t)
                if step % 2:
                    rec_chunk(step // 2)
            rec_cross(1)
            round_unit(M_OUT1 + AHEAD)
            round_unit(M_OUT1 + 1 + AHEAD)
            rec_out(1)
            rec_rsqrt(1)
            for t in range(T):
                rec_out_round(1, t)
            round_unit(M_OUT1 + 2 + AHEAD)
            round_unit(M_OUT1 + 3 + AHEAD)
            ffn(1, M_FFN1)

        @block.vector
        def _(dve):
            def fp(v):
                return v.bitcast(F32)

            def split_unit(m):
                if m >= UNITS:
                    return
                dve.wait_ge(s["rounded"], m + 1)
                nc.vector.tensor_tensor(wlo[:, m % SPL, :], raw[:, m % RAW, :], fp(whi[:, m % SPL, :]), ALU.subtract
                                        ).then_inc(s["split"], 1)

            def ada_op(n):
                blk, k = divmod(n, KC)
                if n < 2 * KC:
                    w = first_w[n % FIRST]
                    dve.wait_ge(first_in[n % FIRST], 16 * (n // FIRST + 1))
                else:
                    w = ada_w[:, n % ADA_RING]
                    dve.wait_ge(ada_in[n % ADA_RING], 16 * ((n - 2 * KC) // ADA_RING + 1))
                if k == 0:
                    dve.wait_ge(s[f"adab_in{blk % 2}"], 16 * (blk // 2 + 1))
                if n < 2 * KC:
                    for half, signal in enumerate(("ada_half", "ada_used")):
                        if n:
                            dve.wait_ge(s[signal], n)
                        cut = slice(half * 512, (half + 1) * 512)
                        nc.vector.scalar_tensor_tensor(out=acc[:, blk % 2, cut], in0=w[:, cut],
                                                       scalar=cact[:, k:k + 1], in1=acc[:, blk % 2, cut],
                                                       op0=ALU.mult, op1=ALU.add).then_inc(s[signal], 1)
                    return
                dve.wait_ge(s["ada_used"], n)
                nc.vector.scalar_tensor_tensor(out=acc[:, blk % 2], in0=w, scalar=cact[:, k:k + 1],
                                               in1=acc[:, blk % 2], op0=ALU.mult, op1=ALU.add
                                               ).then_inc(s["ada_used"], 1)

            def ada_evac(r, b=7):
                blk, kind, half = TASKS[r]
                layer = blk // ADA_BLOCKS
                dve.wait_ge(s["ada_red"], r + 1)
                src = bank[b][:, 0:KC]
                if blk == 1:
                    c = half // P
                    i = scale_gain(layer, 0, bank[b][:, 0:kind], c, kind)
                    i.then_inc(s["ada_ev"], 1)
                    return
                what = blk % ADA_BLOCKS
                if what in (2, 5):
                    dst = late_gate if (layer, what) == (1, 5) else gate[:, what // 5, :]
                    i = nc.vector.tensor_copy(dst[:, half:half + 512], bank[b][:])
                elif what in (0, 3):
                    i = nc.vector.tensor_copy(mod_b[:, layer, what // 3], src)
                else:
                    i = scale_gain(layer, what // 4, src)
                i.then_inc(s["ada_ev"], 1)

            def scale_gain(layer, sub, src, c=0, n=KC):
                first = NORM0 + (2 * sub + layer) * KC + c
                g = cols[:, first:first + n]
                return nc.vector.scalar_tensor_tensor(out=mod_a[:, layer, sub, c:c + n], in0=src, scalar=1.0, in1=g,
                                                      op0=ALU.add, op1=ALU.mult)

            done = [0]

            def refine(y, ss, n, c, inv):
                v, w = small[:, c:c + n], small[:, c + n:c + 2 * n]
                nc.vector.tensor_scalar(v, ss, -0.5 * inv, -0.5 * EPS, ALU.mult, ALU.add)
                nc.vector.tensor_tensor(w, y, y, ALU.mult).then_inc(s["newton"], 1)
                dve.wait_ge(s["newton"], done[0] + 1)
                nc.vector.tensor_tensor(w, w, v, ALU.mult).then_inc(s["newton"], 1)
                dve.wait_ge(s["newton"], done[0] + 2)
                nc.vector.scalar_tensor_tensor(out=y, in0=w, scalar=1.5, in1=y, op0=ALU.add, op1=ALU.mult
                                               ).then_inc(s["newton"], 1)
                dve.wait_ge(s["newton"], done[0] + 3)
                done[0] += 3

            def norm_scale(q, t):
                dve.wait_ge(s["xn_rstd"], 2 * q + t + 1)
                refine(small[:, 2 + t:3 + t], small[:, t:t + 1], 1, 4 + 2 * t, 1.0 / D)
                nc.vector.tensor_scalar(xn[:, t], x[:, t], small[:, 2 + t:3 + t], None, ALU.mult
                                        ).then_inc(s["xn_s"], 1)

            def norm_affine(q, t):
                layer, sub = q // 2, q % 2
                dve.wait_ge(s["xn_tr"], 4 * q + 2 * t + 1)
                for kc in range(4):
                    i = nc.vector.tensor_scalar(hT[:, kc, t * P:(t + 1) * P], bank[4 + 2 * t][:, kc * P:(kc + 1) * P],
                                                mod_a[:, layer, sub, kc:kc + 1], mod_b[:, layer, sub, kc:kc + 1],
                                                ALU.mult, ALU.add)
                i.then_inc(s["xn_aff"], 1)

            def norm_rest(q, t):
                for g in range(2):
                    dve.wait_ge(s["xn_hi"], 4 * q + 2 * t + g + 1)
                    v = lambda y: y[:, 4 * g:4 * g + 4, t * P:(t + 1) * P]
                    nc.vector.tensor_tensor(v(hT_lo), v(hT), fp(v(hT_hi)), ALU.subtract).then_inc(s["xn_lo"], 1)

            def boundary(q, last_unit):
                residual(q - 1, last_unit, range(3))
                if q == 2:
                    ada_evac(AT_NORM[2][0])
                norm_scale(q, 0)
                residual(q - 1, last_unit, range(3, 4))
                norm_affine(q, 0)
                norm_rest(q, 0)
                split_unit(last_unit + AHEAD)
                norm_scale(q, 1)
                norm_affine(q, 1)
                norm_rest(q, 1)

            def residual(q, last_unit, blocks):
                g = gate[:, 0, :] if q % 2 == 0 else (gate[:, 1, :] if q == 1 else late_gate)
                for b in blocks:
                    t, c = divmod(b, 2)
                    if b == 0:
                        dve.wait_ge(s["y_first"], q + 1)
                    if b == 2:
                        dve.wait_ge(s["pe_unit"], last_unit + 1)
                    cut = slice(c * 512, (c + 1) * 512)
                    n = 4 * q + b
                    if n >= 2:
                        dve.wait_ge(s["res"], n - 1)
                    nc.vector.tensor_tensor(sq[:, b % 2], bank[b][:], g[:, cut], ALU.mult).then_inc(s["yres_t"], 1)
                    dve.wait_ge(s["yres_t"], n + 1)
                    nc.vector.tensor_tensor(x[:, t, cut], x[:, t, cut], sq[:, b % 2], ALU.add).then_inc(s["res"], 1)

            nc.vector.memset(acc[:], 0.0).then_inc(s["ada_zero"], 1)
            dve.wait_ge(s["cols_t"], 1)
            nc.vector.tensor_copy(cols[:, 0:NROWS], bank[0][:, 0:NROWS]).then_inc(s["cols_s"], 1)
            dve.wait_ge(s["cols_s"], 1)
            nc.vector.tensor_scalar(cols[:, GAIN0:GAIN0 + NG], cols[:, GAIN0:GAIN0 + NG], float(P) ** -0.5, None,
                                    ALU.mult).then_inc(s["cols_s"], 1)
            nc.vector.tensor_tensor(lbd[:], cols[:, LB0 + KC:LB0 + 2 * KC], cols[:, LB0:LB0 + KC], ALU.subtract
                                    ).then_inc(s["lbd_s"], 1)
            dve.wait_ge(s["lb_s"], 1)
            nc.vector.tensor_scalar(lb[:, 1, :], lb[:, 0, :], -1.0, 1.0, ALU.mult, ALU.add).then_inc(s["lbd_s"], 1)
            dve.wait_ge(s["cact_s"], 1)
            dve.wait_ge(s["ada_zero"], 1)
            for n in range(2 * KC):
                ada_op(n)
                if n == 1:
                    dve.wait_ge(s["tab_mm"], 1)
                    nc.vector.tensor_copy(tabT, bank[1][0:GH, 0:TABLE]).then_inc(s["tab_cp"], 1)
                if n in (4, 5):
                    norm_scale(0, n - 4)
                if n == 12:
                    ada_evac(0, 3)
            split_unit(0)
            ada_evac(1, 3)
            dve.wait_ge(s["ada_ev"], 2)
            norm_affine(0, 0)
            ada_evac(2, 2)
            norm_rest(0, 0)
            norm_affine(0, 1)
            split_unit(1)
            norm_rest(0, 1)

            def qk_reduce(n):
                dve.wait_ge(s["qk_sq"], n + 1)
                if n:
                    dve.wait_ge(s["qk_rstd"], n)
                nc.vector.tensor_reduce(small[:, 8:16], sq[:, :, :].rearrange("p t (h d) -> p (t h) d", d=P), AX_X,
                                        ALU.add).then_inc(s["qk_red"], 1)

            def qk_normalise(n):
                dve.wait_ge(s["qk_rstd"], n + 1)
                if n >= 2:
                    dve.wait_ge(s["qk_tr"], 2 * (n - 1))
                if n == 0:
                    dve.wait_ge(s["tab_out"], 16)
                refine(small[:, 16:24], small[:, 8:16], 8, 32, 1.0 / P)
                b = 2 * ((5 * (n // 3) + n % 3) % 2)
                for t in range(T):
                    r = small[:, 16 + 4 * t:20 + 4 * t].rearrange("p (h o) -> p h o", o=1).to_broadcast([P, 4, P])
                    i = nc.vector.tensor_tensor(qkn[:, n % 2, t * 512:(t + 1) * 512].rearrange("p (h d) -> p h d", d=P),
                                                bank[b + t][:].rearrange("p (h d) -> p h d", d=P), r, ALU.mult)
                i.then_inc(s["qk_norm"], 1)

            def att_max(J):
                h, qt = J // 2, 1 - J % 2
                dve.wait_ge(s["att_s"], J + 1)
                if J:
                    dve.wait_ge(s["att_tr"], before(J))
                dve.wait_ge(bias_in[h % 2], 16 * (h // 2 + 1))
                if qt:
                    nc.vector.tensor_tensor_reduce(prob[:, 0:512].rearrange("p (g k) -> p g k", g=2),
                                                   bank[4][:].rearrange("p (g k) -> p g k", g=2),
                                                   bias[:, h % 2, 0:2, :], 1.0, -3e38, ALU.add, ALU.max,
                                                   stat(J, 0))
                    nc.vector.tensor_tensor_reduce(prob[:, 512:768], bank[5][:, 0:256], bias[:, h % 2, 2, :], 1.0,
                                                   -3e38, ALU.add, ALU.max, stat(J, 1)).then_inc(s["att_m"], 1)
                    dve.wait_ge(s["att_m"], J + 1)
                    nc.vector.tensor_scalar(stat(J, 2), stat(J, 0), stat(J, 1), -1.0, ALU.max, ALU.mult
                                            ).then_inc(s["att_nm"], 1)
                else:
                    nc.vector.tensor_tensor_reduce(probs(J)[0][:, 0:384].rearrange("p (g k) -> p g k", g=3),
                                                   score_bank(J)[:, 0:384].rearrange("p (g k) -> p g k", g=3),
                                                   bias[:, h % 2, :, P:2 * P], 1.0, -3e38, ALU.add, ALU.max,
                                                   stat(J, 0)).then_inc(s["att_m"], 1)
                    dve.wait_ge(s["att_m"], J + 1)
                    nc.vector.tensor_scalar(stat(J, 2), stat(J, 0), -1.0, None, ALU.mult
                                            ).then_inc(s["att_nm"], 1)

            def att_normalise(J):
                w = 768 if J % 2 == 0 else 384
                dve.wait_ge(s["att_p"], J + 1)
                nc.vector.reciprocal(stat(J, 4), stat(J, 3)).then_inc(s["att_rs"], 1)
                dve.wait_ge(s["att_rs"], J + 1)
                pr_ = probs(J)[0][:, 0:w]
                nc.vector.tensor_scalar(pr_, pr_, stat(J, 4), None, ALU.mult
                                        ).then_inc(s["att_pn"], 1)

            def att_out(J):
                h, qt = J // 2, 1 - J % 2
                dve.wait_ge(s["ot_hi"], J + 1)
                cut = slice(qt * P, (qt + 1) * P)
                nc.vector.tensor_tensor(oT_lo[:, h, cut], out_bank(J)[:, ::-1], fp(oT_hi[:, h, cut]), ALU.subtract
                                        ).then_inc(s["ot_ev"], 1)

            def qkv_extra(m):
                pr, j = divmod(m, QU)
                J = 4 * (pr - 1) + j // 2
                if pr >= 1 and j % 2 == 0 and j > 0:
                    att_out(J - 1)
                if pr >= 1 and j % 2 == 0 and j < 8:
                    att_max(J)
                ada_op(2 * KC + m)
                if pr >= 1 and j % 2 == 0 and j < 8:
                    att_normalise(J)
                if pr < PAIRS:
                    if j in (1, 3, 5):
                        qk_reduce(3 * pr + j // 2)
                    if j in (2, 4, 6):
                        qk_normalise(3 * pr + j // 2 - 1)

            for m in range(PURE):
                split_unit(m + AHEAD)
                qkv_extra(m)
                for r in tasks_at(m):
                    ada_evac(r)
            split_unit(M_OUT0 + AHEAD)
            for J in (LATE, LATE + 1):
                att_max(J)
            for J in (LATE, LATE + 1):
                att_normalise(J)
            split_unit(M_OUT0 + 1 + AHEAD)
            for n in range(2):
                ada_op(ADA_LATE - 4 + n)
            for J in (LATE, LATE + 1):
                att_out(J)
            for J in (LATE + 2, LATE + 3):
                att_max(J)
            for J in (LATE + 2, LATE + 3):
                att_normalise(J)
            split_unit(M_OUT0 + 2 + AHEAD)
            for n in range(2, 4):
                ada_op(ADA_LATE - 4 + n)
            for J in (LATE + 2, LATE + 3):
                att_out(J)

            def ffn(f, base):
                q = 2 * f + 1
                boundary(q, base - 1)
                for r in range(3 * NF):
                    kind, j = ffn_step(r)
                    if r < 3 * NF - 1:
                        split_unit(base + r + AHEAD)
                    if kind == 1:
                        n = NF * f + j
                        dve.wait_ge(s["f_sil"], n + 1)
                        if n:
                            dve.wait_ge(s["f_tr"], n)
                        for t in range(T):
                            h1 = bank[(4 if j else 0) + t]
                            i = nc.vector.tensor_tensor(hid[:, t], h1[:, FC:2 * FC], sil[:, t], ALU.mult)
                        i.then_inc(s["f_hid"], 1)
                    jt = hidden_after(r)
                    if jt is not None:
                        n = NF * f + jt
                        dve.wait_ge(s["f_hi"], n + 1)
                        nc.vector.tensor_tensor(hidT(oT_lo, n), bank[6][:].rearrange("p (k t) -> p k t", k=2),
                                                fp(hidT(oT_hi, n)), ALU.subtract).then_inc(s["f_lo"], 1)
                    if f == 0:
                        rest = 2 * ADA_BLOCKS * KC - ADA_LATE
                        for n in range(rest * max(r - 1, 0) // 31, min(rest * r // 31, rest)):
                            ada_op(ADA_LATE + n)
                        for task in tasks_at(M_FFN0 + r):
                            ada_evac(task)

            ffn(0, M_FFN0)
            boundary(2, M_IN - 1)
            nc.vector.memset(Am, 0.0).then_inc(s["r_zero"], 1)
            dve.wait_ge(s["r_zero"], 1)

            def rec_gates(half):
                dve.wait_ge(s["r_tev"], 2 * half + 1)
                dve.wait_ge(s["lbd_s"], 2)
                for h in range(4):
                    c = 4 * half + h
                    cut = slice(h * SEQ, (h + 1) * SEQ)
                    i = nc.vector.tensor_scalar(forget[:, cut], rk[half][:, cut], lb[:, 1, c:c + 1],
                                                lb[:, 0, c:c + 1], ALU.mult, ALU.add)
                i.then_inc(s["r_fg"], 1)
                dve.wait_ge(s["r_fg"], half + 1)
                nc.vector.tensor_scalar(rk[half], forget, -1.0, 1.0, ALU.mult, ALU.add).then_inc(s["r_k"], 1)
                dve.wait_ge(s["r_k"], half + 1)
                dve.wait_ge(s["r_ln"], half + 1)
                for h in range(4):
                    for t in range(T):
                        cut = slice(h * SEQ + t * P, h * SEQ + (t + 1) * P)
                        i = nc.vector.tensor_tensor_scan(rG[half][:, cut], logf[:, cut], logf[:, cut], 0.0, ALU.add,
                                                         ALU.bypass)
                i.then_inc(s["r_G"], 1)

            def rec_scale(half, level):
                dve.wait_ge(s["r_E"], LEVELS * half + level)
                if level > 2:
                    dve.wait_ge(s["r_mm"], PRODUCTS * half + level)
                elif half:
                    dve.wait_ge(s["r_mm"], PRODUCTS * half - 2 + level)
                if level == 1:
                    dve.wait_ge(s["r_tev"], 2 * half + 2)
                h = gh(level)
                v = lambda y: y.rearrange("p (b two h) -> p b two h", two=2, h=h)
                E = v(rE[:, level % 2])
                Z = v(rZ[:, level % 2])
                nc.vector.tensor_tensor(Z[:, :, 0, :], v(rk[half])[:, :, 0, :], E[:, :, 0, :], ALU.mult)
                nc.vector.tensor_tensor(Z[:, :, 1, :], v(rq[half])[:, :, 1, :], E[:, :, 1, :], ALU.mult
                                        ).then_inc(s["r_q"], 1)

            def rec_take(half, o):
                dve.wait_ge(s["r_mm"], PRODUCTS * half + o + 1)
                if half and o == 0:
                    dve.wait_ge(s["r_o"], 2)
                if half or o:
                    dve.wait_ge(s["r_A"], (LEVELS + 1) * half + o)
                if o < 2:
                    dst = Am[:, o].rearrange("p (h t) -> p h t", h=4)
                    v = lambda y: y
                else:
                    n = gh(o - 1)
                    dst = Am[:, 0:2].rearrange("p t (g b two h) -> p (t g) b two h", g=4, two=2, h=n)[:, :, :, 1, :]
                    v = lambda y: y.rearrange("p g (b h) -> p g b h", h=n)
                m, blocks = (masks[:, 0:P], 4) if o < 2 else (masks[:, o * 64:(o + 1) * 64], 8)
                m = m.rearrange("p (o t) -> p o t", o=1).to_broadcast([P, blocks, 512 // blocks])
                nc.vector.copy_predicated(dst, v(m), v(bank[4 + o % 2][:].rearrange("p (g t) -> p g t", g=blocks))
                                          ).then_inc(s["r_A"], 1)

            def rec_squares(half, t):
                n = 2 * half + t
                dve.wait_ge(s["r_osq"], n + 1)
                c = 32 + 8 * half + 4 * t
                nc.vector.tensor_reduce(small[:, c:c + 4], sq[:, t].rearrange("p (h d) -> p h d", d=P), AX_X, ALU.add
                                        ).then_inc(s["r_ored"], 1)

            def rec_gate(half, t):
                dve.wait_ge(s["r_orstd"], half + 1)
                if t == 0:
                    c = 8 * half
                    refine(small[:, 48 + c:56 + c], small[:, 32 + c:40 + c], 8, 8, 1.0 / P)
                dve.wait_ge(s["r_oev"], 2 * half + t + 1)
                dve.wait_ge(s["r_nat"], 7 + half)
                for h in range(4):
                    cut = slice((4 * half + h) * P, (4 * half + h + 1) * P)
                    c = 48 + 8 * half + 4 * t + h
                    i = nc.vector.scalar_tensor_tensor(out=rV[:, t, cut], in0=rV[:, t, cut], scalar=small[:, c:c + 1],
                                                       in1=gates[:, t, cut], op0=ALU.mult, op1=ALU.mult)
                i.then_inc(s["r_on"], 1)

            def rec_out_rest(half, t):
                dve.wait_ge(s["r_ohi"], 2 * half + t + 1)
                cut = slice(t * P, (t + 1) * P)
                nc.vector.scalar_tensor_tensor(out=oT_lo[:, 4 * half:4 * half + 4, cut],
                                               in0=bank[6 + t][:].rearrange("p (h t) -> p h t", t=P),
                                               scalar=cols[:, GNORM0:GNORM0 + 1],
                                               in1=fp(oT_hi[:, 4 * half:4 * half + 4, cut]),
                                               op0=ALU.mult, op1=ALU.subtract).then_inc(s["r_olo"], 1)

            dve.wait_ge(s["masks_in"], 16)
            for step in range(16):
                scales = [(half, o - 1) for half, o in products_at(step) if o >= 2]
                takes = [(half, o) for half, o in products_at(step - 1) if o < PRODUCTS - 1]
                for n in range(2):
                    if n < len(takes):
                        rec_take(*takes[n])
                    if n < len(scales):
                        rec_scale(*scales[n])
                split_unit(M_IN + step + AHEAD)
                if step == 1:
                    ada_evac(len(TASKS) - 1)
                if step in (3, 9):
                    rec_gates(step // 9)
                for t in range(T):
                    if step == 13:
                        rec_squares(0, t)
                    if step == 14:
                        rec_gate(0, t)
                    if step == 15:
                        rec_out_rest(0, t)
            for half, o in products_at(15):
                if o < PRODUCTS - 1:
                    rec_take(half, o)
            split_unit(M_OUT1 + AHEAD)
            split_unit(M_OUT1 + 1 + AHEAD)
            for t in range(T):
                rec_squares(1, t)
            for t in range(T):
                rec_gate(1, t)
            for t in range(T):
                rec_out_rest(1, t)
            split_unit(M_OUT1 + 2 + AHEAD)
            ffn(1, M_FFN1)
            residual(3, UNITS - 1, range(4))


ROWS = [("c", 0, 8), ("norm_mix", 8, 16), ("norm_ffn", 24, 16), ("attn_q_gain", 40, 3), ("attn_k_gain", 43, 3),
        ("hgrn_lower_bounds", 46, 16), ("hgrn_gnorm", 62, 1)]
ROW_AP = {"c": "a (k d) -> (a k) d", "norm_mix": "a (k d) -> (a k) d", "norm_ffn": "a (k d) -> (a k) d",
          "attn_q_gain": "a g d -> (a g) d", "attn_k_gain": "a g d -> (a g) d",
          "hgrn_lower_bounds": "a (k d) -> (a k) d", "hgrn_gnorm": "a d -> a d"}
NROWS = 63
NORM0, GAIN0, LB0, GNORM0 = 8, 40, 46, 62

TASKS = [(blk, kind, c0) for blk in range(2 * ADA_BLOCKS)
         for kind, c0 in ([("row", 0), ("row", 512)] if blk % ADA_BLOCKS in (2, 5) else
                          [(KC // 2, 0), (KC // 2, 512)] if blk == 1 else [(KC, 0)])]


def tasks_until(block):
    return sum(1 for t in TASKS if t[0] <= block)


def tasks_at(m):
    late = {3: [9], 8: [10], 14: [11], 15: [12], 20: [13]}
    return {9: [3], 10: [4], 18: [5], 26: [6]}.get(m, []) + late.get(m - M_FFN0, [])


AT_NORM = {1: (7, 8), 2: (14, 15)}


TRANSPOSED = (2, 4, 8, 10)


def products_at(step):
    half, first = (0, 5) if step < 11 else (1, 11)
    return [(half, 2 * (step - first) + i) for i in range(2)] if first <= step < first + 5 else []


def base_of(n):
    f, j = divmod(n, NF)
    return (M_FFN0, M_FFN1)[f] + (3 * (j + 1) + 1 if j < NF - 1 else 3 * NF - 1)


_INS = ["x", "c", "rel_bias", "ada_w", "ada_b", "norm_mix", "norm_ffn", "attn_w_qkv", "attn_w_out", "attn_q_gain",
        "attn_k_gain", "hgrn_w_in", "hgrn_w_out", "hgrn_gnorm", "hgrn_lower_bounds", "ffn_w1", "ffn_w3", "ffn_w2"]


def kernel(**inputs):
    import numpy as _np
    import concourse.bacc as _bacc
    from concourse import mybir as _mybir
    from concourse.bass_utils import run_bass_kernel_spmd as _run

    nc = _bacc.Bacc("TRN2", target_bir_lowering=False, num_devices=1)
    data = {name: _np.ascontiguousarray(inputs[name]) for name in _INS}
    data |= {"distance_table": distance_table(), "mask_rows": mask_rows(), "pair_masks": pair_masks()}
    arrays, args = {}, {}
    for name, v in data.items():
        arrays[f"in_{name}_dram"] = v
        args[name] = nc.dram_tensor(f"in_{name}_dram", v.shape, _mybir.dt.from_np(v.dtype), kind="ExternalInput").ap()
    out = nc.dram_tensor("out_0_dram", (1, SEQ, D), F32, kind="ExternalOutput").ap()
    hybrid_trunk(nc, args, out)
    r = _run(nc, [arrays], core_ids=[0])
    return r.results[0]["out_0_dram"]
```
